# Optimizing a Trainium2 kernel written in Bass

```python
import math
import jax, jax.numpy as jnp
from jax import lax
import numpy as np

D_MODEL = 1024
BATCH = 1
SEQ = 256
DEPTH = 1
DEC_BATCH = 8
DEC_SEQ = 8
PAST_LEN = 2048
PAGE_SIZE = 128

M_HEADS = 4
M_V = (2 * D_MODEL) // M_HEADS
M_QK = M_V // 2
M_QK_W = M_HEADS * M_QK
M_V_W = M_HEADS * M_V
S_INNER = 2 * D_MODEL
S_HEADDIM = 64
S_HEADS = S_INNER // S_HEADDIM
S_GROUPS = 4
S_HPG = S_HEADS // S_GROUPS
S_STATE = 128
S_CONV_CH = S_INNER + 2 * S_GROUPS * S_STATE
CONV_W = 4
D_FF = 2816
CHUNK = 128
EPS = 1e-6
N_MOD = 9
SPLITS = (M_QK_W, M_QK_W, M_V_W, M_V_W, M_HEADS, M_HEADS, S_INNER, S_CONV_CH, S_HEADS, D_MODEL, D_MODEL)
IN_W = 2 * M_QK_W + 2 * M_V_W + 2 * M_HEADS + S_INNER + S_CONV_CH + S_HEADS + 2 * D_MODEL

kernel_name = 'hybrid_mlstm_ssd_macaron_adaln_step'

def _rmsnorm(x, g):
    x32 = x.astype(jnp.float32)
    y = x32 * lax.rsqrt(jnp.mean(x32 * x32, axis=-1, keepdims=True) + EPS)
    return (y * g.astype(jnp.float32)).astype(x.dtype)

def _modulate(xn, shift, scale):
    return xn * (1.0 + scale[:, None, :]) + shift[:, None, :]

def _swiglu(u, w1, w3, w2):
    return (jax.nn.silu(u @ w1) * (u @ w3)) @ w2

def _split_cols(a):
    idx = np.cumsum(np.array(SPLITS))[:-1].tolist()
    return jnp.split(a, idx, axis=-1)

def _causal_conv(x, buf, w, b):
    T = x.shape[1]
    xp = jnp.concatenate([buf, x], axis=1)
    out = xp[:, 0:T] * w[0]
    for j in range(1, CONV_W):
        out = out + xp[:, j:j + T] * w[j]
    return out + b, xp[:, -(CONV_W - 1):]

def _to_chunks(a, L):
    B, T = a.shape[0], a.shape[1]
    return jnp.moveaxis(a.reshape((B, T // L, L) + a.shape[2:]), 1, 0)

def _from_chunks(a):
    a = jnp.moveaxis(a, 0, 1)
    return a.reshape((a.shape[0], a.shape[1] * a.shape[2]) + a.shape[3:])

def _mlstm(q, k, v, i_pre, f_pre, C0, n0, m0):
    T = q.shape[1]
    L = math.gcd(T, CHUNK)
    f32 = jnp.float32
    q = q.astype(f32)
    k = k.astype(f32) * (M_QK ** -0.5)
    v = v.astype(f32)
    ig = i_pre.astype(f32)
    lf = jax.nn.log_sigmoid(f_pre.astype(f32))
    mask = jnp.tril(jnp.ones((L, L), dtype=bool))[None, :, :, None]

    def step(carry, inp):
        C, n, m = carry
        qc, kc, vc, ic, lfc = inp
        b = jnp.cumsum(lfc, axis=1)
        dmat = jnp.where(mask, b[:, :, None, :] - b[:, None, :, :] + ic[:, None, :, :], -jnp.inf)
        inter = b + m[:, None, :]
        mt = jnp.maximum(inter, jnp.max(dmat, axis=2))
        w_tok = jnp.exp(dmat - mt[:, :, None, :])
        w_st = jnp.exp(inter - mt)
        s = jnp.einsum('bthd,bshd->btsh', qc, kc) * w_tok
        num = jnp.einsum('btsh,bshv->bthv', s, vc) + w_st[..., None] * jnp.einsum('bthd,bhdv->bthv', qc, C)
        den = jnp.sum(s, axis=2) + w_st * jnp.einsum('bthd,bhd->bth', qc, n)
        h = num / jnp.maximum(jnp.abs(den), jnp.exp(-mt))[..., None]
        m_new = mt[:, -1]
        b_last = b[:, -1]
        ws = jnp.exp(b_last[:, None, :] - b + ic - m_new[:, None, :])
        decay = jnp.exp(b_last + m - m_new)
        C_new = decay[..., None, None] * C + jnp.einsum('bsh,bshd,bshv->bhdv', ws, kc, vc)
        n_new = decay[..., None] * n + jnp.einsum('bsh,bshd->bhd', ws, kc)
        return (C_new, n_new, m_new), h

    xs = (_to_chunks(q, L), _to_chunks(k, L), _to_chunks(v, L), _to_chunks(ig, L), _to_chunks(lf, L))
    (C1, n1, m1), h = lax.scan(step, (C0.astype(f32), n0.astype(f32), m0.astype(f32)), xs)
    return _from_chunks(h), C1, n1, m1

def _ssd(x, dt, A, Bm, Cm, h0):
    T = x.shape[1]
    L = math.gcd(T, CHUNK)
    mask = jnp.tril(jnp.ones((L, L), dtype=bool))[None, :, :, None, None]

    def step(h, inp):
        xc, dtc, bc, cc = inp
        cum = jnp.cumsum(dtc * A, axis=1)
        lmat = jnp.exp(jnp.where(mask, cum[:, :, None] - cum[:, None, :], -jnp.inf))
        xdt = xc * dtc[..., None]
        cb = jnp.einsum('btgn,bsgn->btsg', cc, bc)
        y = (jnp.einsum('btsg,btsge,bsgep->btgep', cb, lmat, xdt)
             + jnp.exp(cum)[..., None] * jnp.einsum('btgn,bgepn->btgep', cc, h))
        decay = jnp.exp(cum[:, -1:] - cum)
        h_new = (jnp.exp(cum[:, -1])[..., None, None] * h
                 + jnp.einsum('bsgn,bsge,bsgep->bgepn', bc, decay, xdt))
        return h_new, y

    xs = (_to_chunks(x, L), _to_chunks(dt, L), _to_chunks(Bm, L), _to_chunks(Cm, L))
    h1, y = lax.scan(step, h0, xs)
    return _from_chunks(y), h1

def _layer(x, c, st, p):
    C0, n0, m0, mconv0, ssm0, sconv0 = st
    Bsz, T, _ = x.shape
    f32 = jnp.float32
    mod = jax.nn.silu(c) @ p['ada_w'] + p['ada_b']
    sh1, sc1, g1, sh2, sc2, g2, sh3, sc3, g3 = jnp.split(mod, N_MOD, axis=-1)
    u = _modulate(_rmsnorm(x, p['norm_ff1']), sh1, sc1)
    x = x + 0.5 * g1[:, None, :] * _swiglu(u, p['ff1_w1'], p['ff1_w3'], p['ff1_w2'])
    u = _modulate(_rmsnorm(x, p['norm_mix']), sh2, sc2)
    mq, mk, mv, mo, mi, mf, z, xbc, dtp, ga, gb = _split_cols(u @ p['w_in'])
    qk, mconv1 = _causal_conv(jnp.concatenate([mq, mk], axis=-1), mconv0, p['m_conv_w'], p['m_conv_b'])
    qk = jax.nn.silu(qk)
    q = qk[..., :M_QK_W].reshape(Bsz, T, M_HEADS, M_QK)
    k = qk[..., M_QK_W:].reshape(Bsz, T, M_HEADS, M_QK)
    v = mv.reshape(Bsz, T, M_HEADS, M_V)
    i_pre = mi + p['m_if_b'][:M_HEADS]
    f_pre = mf + p['m_if_b'][M_HEADS:]
    hm, C1, n1, m1 = _mlstm(q, k, v, i_pre, f_pre, C0, n0, m0)
    mu = jnp.mean(hm, axis=-1, keepdims=True)
    var = jnp.mean(jnp.square(hm - mu), axis=-1, keepdims=True)
    hm = (hm - mu) * lax.rsqrt(var + EPS) * p['m_head_g'].astype(f32).reshape(M_HEADS, M_V)
    hm = hm * jax.nn.sigmoid(mo.astype(f32)).reshape(Bsz, T, M_HEADS, M_V)
    ya = hm.reshape(Bsz, T, M_V_W).astype(x.dtype) @ p['w_pa']
    xbc, sconv1 = _causal_conv(xbc, sconv0, p['s_conv_w'], p['s_conv_b'])
    xbc = jax.nn.silu(xbc).astype(f32)
    xs = xbc[..., :S_INNER].reshape(Bsz, T, S_GROUPS, S_HPG, S_HEADDIM)
    Bm = xbc[..., S_INNER:S_INNER + S_GROUPS * S_STATE].reshape(Bsz, T, S_GROUPS, S_STATE)
    Cm = xbc[..., S_INNER + S_GROUPS * S_STATE:].reshape(Bsz, T, S_GROUPS, S_STATE)
    dt = jax.nn.softplus((dtp + p['s_dt_bias']).astype(f32)).reshape(Bsz, T, S_GROUPS, S_HPG)
    A = -jnp.exp(p['s_A_log'].astype(f32)).reshape(S_GROUPS, S_HPG)
    h0 = ssm0.astype(f32).reshape(Bsz, S_GROUPS, S_HPG, S_HEADDIM, S_STATE)
    ys, h1 = _ssd(xs, dt, A, Bm, Cm, h0)
    ys = ys + p['s_D'].astype(f32).reshape(S_GROUPS, S_HPG)[..., None] * xs
    gated = ys.reshape(Bsz, T, S_INNER) * jax.nn.silu(z.astype(f32))
    gg = gated.reshape(Bsz, T, S_GROUPS, S_INNER // S_GROUPS)
    gg = gg * lax.rsqrt(jnp.mean(gg * gg, axis=-1, keepdims=True) + EPS)
    gated = gg.reshape(Bsz, T, S_INNER) * p['s_norm_g'].astype(f32)
    yb = gated.astype(x.dtype) @ p['w_pb']
    ssm1 = h1.reshape(Bsz, S_HEADS, S_HEADDIM, S_STATE)
    merged = jax.nn.sigmoid(ga) * ya + jax.nn.sigmoid(gb) * yb
    x = x + g2[:, None, :] * (merged @ p['w_out'])
    u = _modulate(_rmsnorm(x, p['norm_ff2']), sh3, sc3)
    x = x + 0.5 * g3[:, None, :] * _swiglu(u, p['ff2_w1'], p['ff2_w3'], p['ff2_w2'])
    return x, (C1, n1, m1, mconv1, ssm1, sconv1)

def setup_inputs(seed: int = 0) -> dict:
    key = jax.random.key(seed)
    ks = iter(jax.random.split(key, 48))
    f32 = jnp.float32

    def nrm(shape, scale):
        return jax.random.normal(next(ks), shape, f32) * scale

    def gain(shape):
        return 1.0 + nrm(shape, 0.05)

    D = D_MODEL
    dt0 = jnp.exp(jax.random.uniform(next(ks), (DEPTH, S_HEADS), f32, math.log(1e-3), math.log(1e-1)))
    f_bias = jnp.linspace(3.0, 6.0, M_HEADS, dtype=f32)[None, :] + nrm((DEPTH, M_HEADS), 0.1)
    return {
        'x_prompt': nrm((BATCH, SEQ, D), 1.0),
        'x_sample': nrm((DEC_BATCH, DEC_SEQ, D), 1.0),
        'c_prompt': nrm((BATCH, D), 1.0),
        'c_sample': nrm((DEC_BATCH, D), 1.0),
        'state_mlstm_C': nrm((DEPTH, DEC_BATCH, M_HEADS, M_QK, M_V), M_QK ** -0.5),
        'state_mlstm_n': nrm((DEPTH, DEC_BATCH, M_HEADS, M_QK), M_QK ** -0.5),
        'state_mlstm_m': nrm((DEPTH, DEC_BATCH, M_HEADS), 0.5),
        'state_mlstm_conv': nrm((DEPTH, DEC_BATCH, CONV_W - 1, 2 * M_QK_W), 1.0),
        'state_ssm': nrm((DEPTH, DEC_BATCH, S_HEADS, S_HEADDIM, S_STATE), 0.1),
        'state_ssm_conv': nrm((DEPTH, DEC_BATCH, CONV_W - 1, S_CONV_CH), 1.0),
        'ada_w': nrm((DEPTH, D, N_MOD * D), 0.5 * D ** -0.5),
        'ada_b': nrm((DEPTH, N_MOD * D), 0.02),
        'norm_ff1': gain((DEPTH, D)),
        'ff1_w1': nrm((DEPTH, D, D_FF), D ** -0.5),
        'ff1_w3': nrm((DEPTH, D, D_FF), D ** -0.5),
        'ff1_w2': nrm((DEPTH, D_FF, D), D_FF ** -0.5),
        'norm_mix': gain((DEPTH, D)),
        'w_in': nrm((DEPTH, D, IN_W), D ** -0.5),
        'm_conv_w': nrm((DEPTH, CONV_W, 2 * M_QK_W), CONV_W ** -0.5),
        'm_conv_b': nrm((DEPTH, 2 * M_QK_W), 0.02),
        'm_if_b': jnp.concatenate([nrm((DEPTH, M_HEADS), 0.1), f_bias], axis=-1),
        'm_head_g': gain((DEPTH, M_V_W)),
        'w_pa': nrm((DEPTH, M_V_W, D), M_V_W ** -0.5),
        's_conv_w': nrm((DEPTH, CONV_W, S_CONV_CH), CONV_W ** -0.5),
        's_conv_b': nrm((DEPTH, S_CONV_CH), 0.02),
        's_dt_bias': dt0 + jnp.log(-jnp.expm1(-dt0)),
        's_A_log': jnp.log(jax.random.uniform(next(ks), (DEPTH, S_HEADS), f32, 1.0, 16.0)),
        's_D': 1.0 + nrm((DEPTH, S_HEADS), 0.1),
        's_norm_g': gain((DEPTH, S_INNER)),
        'w_pb': nrm((DEPTH, S_INNER, D), S_INNER ** -0.5),
        'w_out': nrm((DEPTH, D, D), D ** -0.5),
        'norm_ff2': gain((DEPTH, D)),
        'ff2_w1': nrm((DEPTH, D, D_FF), D ** -0.5),
        'ff2_w3': nrm((DEPTH, D, D_FF), D ** -0.5),
        'ff2_w2': nrm((DEPTH, D_FF, D), D_FF ** -0.5),
        'final_norm': gain((D,)),
    }

def reference(x_prompt, x_sample, c_prompt, c_sample, state_mlstm_C, state_mlstm_n, state_mlstm_m,
              state_mlstm_conv, state_ssm, state_ssm_conv, ada_w, ada_b, norm_ff1, ff1_w1, ff1_w3,
              ff1_w2, norm_mix, w_in, m_conv_w, m_conv_b, m_if_b, m_head_g, w_pa, s_conv_w, s_conv_b,
              s_dt_bias, s_A_log, s_D, s_norm_g, w_pb, w_out, norm_ff2, ff2_w1, ff2_w3, ff2_w2,
              final_norm):
    f32 = jnp.float32
    Bp = x_prompt.shape[0]
    hp, hs = x_prompt, x_sample
    new_p, new_s = [], []
    for l in range(DEPTH):
        p = {'ada_w': ada_w[l], 'ada_b': ada_b[l], 'norm_ff1': norm_ff1[l], 'ff1_w1': ff1_w1[l],
             'ff1_w3': ff1_w3[l], 'ff1_w2': ff1_w2[l], 'norm_mix': norm_mix[l], 'w_in': w_in[l],
             'm_conv_w': m_conv_w[l], 'm_conv_b': m_conv_b[l], 'm_if_b': m_if_b[l],
             'm_head_g': m_head_g[l], 'w_pa': w_pa[l], 's_conv_w': s_conv_w[l],
             's_conv_b': s_conv_b[l], 's_dt_bias': s_dt_bias[l], 's_A_log': s_A_log[l],
             's_D': s_D[l], 's_norm_g': s_norm_g[l], 'w_pb': w_pb[l], 'w_out': w_out[l],
             'norm_ff2': norm_ff2[l], 'ff2_w1': ff2_w1[l], 'ff2_w3': ff2_w3[l], 'ff2_w2': ff2_w2[l]}
        st_p = (jnp.zeros((Bp, M_HEADS, M_QK, M_V), f32),
                jnp.zeros((Bp, M_HEADS, M_QK), f32),
                jnp.zeros((Bp, M_HEADS), f32),
                jnp.zeros((Bp, CONV_W - 1, 2 * M_QK_W), x_prompt.dtype),
                jnp.zeros((Bp, S_HEADS, S_HEADDIM, S_STATE), f32),
                jnp.zeros((Bp, CONV_W - 1, S_CONV_CH), x_prompt.dtype))
        st_s = (state_mlstm_C[l], state_mlstm_n[l], state_mlstm_m[l], state_mlstm_conv[l],
                state_ssm[l], state_ssm_conv[l])
        hp, sp = _layer(hp, c_prompt, st_p, p)
        hs, ss = _layer(hs, c_sample, st_s, p)
        new_p.append(sp)
        new_s.append(ss)
    y_prompt = _rmsnorm(hp, final_norm)
    y_sample = _rmsnorm(hs, final_norm)
    pC, pn, pm, pmc, pssm, psc = [jnp.stack([s[i] for s in new_p]) for i in range(6)]
    sC, sn, sm, smc, sssm, ssc = [jnp.stack([s[i] for s in new_s]) for i in range(6)]
    return (y_prompt, y_sample, pC, pn, pm, pmc, pssm, psc, sC, sn, sm, smc, sssm, ssc)


_drawn_inputs = setup_inputs


def setup_inputs(seed=0):
    import zlib

    import numpy as np

    out = dict(_drawn_inputs(seed))
    spreads = {}
    factors = {'norm_ff1': 4.665, 'm_head_g': 28.814, 's_D': 6.337, 's_norm_g': 19.276, 'norm_ff2': 7.521}
    for name, (base, spread) in spreads.items():
        noise = np.random.default_rng([zlib.crc32(name.encode()), seed]).standard_normal(out[name].shape)
        drawn = base * np.exp(spread * noise) if base else spread * noise
        out[name] = __import__('jax').numpy.asarray(drawn.astype(out[name].dtype))
    for name, factor in factors.items():
        out[name] = (out[name] * factor).astype(out[name].dtype)
    return out
```

```python
import concourse.bass as bass
from concourse import mybir
from contextlib import ExitStack

FP32 = mybir.dt.float32
ACT = mybir.ActivationFunctionType
ALU = mybir.AluOpType
AX = mybir.AxisListType

D = 1024
TP, SB, ST = 256, 8, 8
TS = SB * ST
T = TP + TS
KD = D // 128
DFF = 2816
KF = DFF // 128
NSEQ = 1 + SB
NMOD = 9
MH, DV, DK = 4, 512, 256
SH, SG, SN = 32, 4, 128
XCH = 2048
SCH = 3072
EPS = 1e-6
NEG = -1e30
HIST = 3
PADW = HIST + TP + SB * (HIST + ST)
CONVW = PADW - HIST
SLOTS = 4
IN_OFF = {"q": 0, "k": 1024, "v": 2048, "mo": 4096, "if": 6144, "z": 6152, "xbc": 8200, "dt": 11272, "ga": 11304, "gb": 12328}


class Segment:

    def __init__(self, name, first_panel, first_tile, panels, tiles, kc):
        self.name, self.g0, self.t0, self.panels, self.tiles, self.kc = name, first_panel, first_tile, panels, tiles, kc

    def slot(self, k):
        return (self.g0 + k) % SLOTS

    def slot_use(self, i, k):
        return i + (self.g0 + k) // SLOTS + 1

    def bank(self, k, j=0):
        return (self.t0 + k * self.tiles + j) % 4

    def bank_use(self, i, k, j=0):
        return i * self.tiles + (self.t0 + k * self.tiles + j) // 4

    def tile_no(self, i, k, j=0):
        return i * (4 * self.tiles) + (self.t0 + k * self.tiles + j)

    def own(self, i, k, j=0):
        return i * (4 * self.tiles) + (k * self.tiles + j)


def walk(eng, seg, body, chain=None, per=0):
    base = chain.n if chain else 0

    def step(i, k):
        if chain:
            chain.n = base + (i * (4 * per) + k * per)
        body(i, k)
        if chain and isinstance(i, int):
            assert chain.n == base + (4 * i + k + 1) * per, (chain.n - base, per)

    full = seg.panels // 4
    for k in range(min(4, seg.panels)):
        step(0, k)
    if full > 1:
        with eng.Fori(1, full) as i:
            for k in range(4):
                step(i, k)
    if full:
        for k in range(seg.panels % 4):
            step(full, k)
    if chain:
        chain.n = base + seg.panels * per


class Chain:

    def __init__(self, eng, sem):
        self.eng, self.sem, self.n = eng, sem, 0

    def link(self, ins):
        self.inc(ins)
        self.settle()

    def inc(self, ins):
        ins.then_inc(self.sem, 1)
        self.n = self.n + 1

    def settle(self):
        self.eng.wait_ge(self.sem, self.n)


def build(nc, io, out):
    segs, g, t = {}, 0, 0
    for name, panels, tiles, kc in (
        ("ada", NMOD * D // 256, 1, KD), ("up1", 2 * DFF // 256, 2, KD), ("down1", KD, 1, KF),
        ("qk", 8, 2, KD), ("v", 8, 2, KD), ("mo", 8, 2, KD), ("pa", 8, 1, 16),
        ("xbc", 12, 2, KD), ("z", 8, 2, KD), ("ga", 4, 2, KD), ("gb", 4, 2, KD), ("pb", 8, 1, 16),
        ("out", 4, 2, KD), ("up2", 2 * DFF // 256, 2, KD), ("down2", KD, 1, KF),
    ):
        segs[name] = Segment(name, g, t, panels, tiles, kc)
        g, t = g + panels, t + panels * tiles
    total_tiles = t

    ctx = ExitStack()
    with ctx:
        def sb(name, shape):
            return ctx.enter_context(nc.sbuf_tensor(name, shape, FP32))

        def sem(name):
            return ctx.enter_context(nc.semaphore(name))

        ident = sb("ident", [128, 128])
        ones = sb("ones", [128, 128])
        tri = sb("tri", [128, 384])
        tri_s = sb("tri_s", [64, 128])
        neg_p = sb("neg_p", [128, 128])
        neg_s = sb("neg_s", [64, 64])
        seg_m = sb("seg_m", [64, SB])
        seg_b = sb("seg_b", [128, SB, TS])
        seg_t = sb("seg_t", [SB, TS])
        row_last = sb("row_last", [128, 128])
        last_s = sb("last_s", [64, 64])
        last_b = sb("last_b", [64, SB])
        mod_sum = sb("mod_sum", [128, NSEQ])
        tile_of_head = sb("tile_of_head", [SH, 16])
        parity = sb("parity", [SH, 2, 64])
        parity2 = sb("parity2", [SH, 2])
        par = sb("par", [128, 336])
        mod = sb("mod", [128, NMOD * KD, NSEQ])
        gain = sb("gain", [128, KD, NSEQ])
        half_g = sb("half_g", [128, KD, NSEQ])
        a_neg = sb("a_neg", [128, SH])
        m0_b = sb("m0_b", [128, SB * MH])
        m0_r = sb("m0_r", [SB, MH])
        gate_w = sb("gate_w", [128, KD, 40])
        gate_sb = sb("gate_sb", [40, 4])
        eps_col = sb("eps_col", [128, 1])
        soft_a, soft_e, soft_l, soft_r = (sb(n, [128, 108]) for n in ("soft_a", "soft_e", "soft_l", "soft_r"))
        sp2 = sb("sp2", [128, 3, SH])
        d_col = sb("d_col", [SH, 1])
        x_t = sb("x_t", [128, KD, T])
        u_t = sb("u_t", [128, KD, T])
        rs = sb("rs", [128, T])
        ring = [sb(f"ring{s}", [128, DFF]) for s in range(SLOTS)]
        mod_row = [sb(f"mod_row{s}", [128, 256]) for s in range(2)]
        res_tmp = sb("res_tmp", [128, 4, TS])
        hist = sb("hist", [128, 40, SB * HIST])
        tails = sb("tails", [128, 40, HIST * (1 + SB)])
        g3 = sb("g3", [128, 3, 40])
        sp = sb("sp", [128, 3, 36])
        al = sb("al", [128, 3, 36])
        cum = sb("cum", [128, 3, 36])
        sm = sb("sm", [128, 12, 36])
        al2 = sb("al2", [64, SB * 2 * MH])
        lb = sb("lb", [128, SB, 2 * MH])
        dec = sb("dec", [128, SB * MH])
        stats = sb("stats", [128, 3, 6])
        mean_var = sb("mean_var", [128, 3, 2])
        coef = sb("coef", [128, 3, 2])
        hd_in = sb("hd_in", [SH, 16 * (SB + 1)])
        h_dec = sb("h_dec", [128, 16 * (SB + 1)])
        n_t = sb("n_t", [128, 8, SB])

        arena = sb("arena", [128, 28256])
        used = [0]

        def part(off, *shape):
            n = 1
            for s in shape:
                n *= s
            used[0] = max(used[0], off + n)
            assert off + n <= 28256, off + n
            v = arena[:, off:off + n]
            if len(shape) == 2:
                v = v.rearrange("p (a b) -> p a b", b=shape[1])
            if len(shape) == 3:
                v = v.rearrange("p (a b c) -> p a b c", b=shape[1], c=shape[2])
            return v

        pk = part(0, 3, 128)
        x_rows = part(384, 3, D)
        mh_rows = part(3456, 2048)
        sh_rows = part(5504, 3072)
        c_rows = part(8576, D)
        n_rows = part(9600, D)
        c_t = part(10624, KD, 32)
        sq = part(20320, KD, T)
        ff_h = part(12000, KF, T)
        ff_a = part(19040, 4, T)
        qk_t = part(0, 16, T)
        v_tok = part(5120, 3, 2048)
        hm = part(11264, 16, T)
        kw = part(16384, 3, 1024)
        pad = part(19456, 4, PADW)
        acc = part(20844, 4, PADW)
        dm = part(22220, MH, 448)
        v_tmp = part(22220, 4, T)
        cb = part(24012, MH, 2 * DV)
        st_s = part(19456, MH, 448)
        kwm = part(12952, MH, DK)
        num = part(0, 3, DV)
        num2 = part(1536, 3, DV)
        t1 = part(3072, DV)
        t2 = part(3584, DV)
        qm = part(11264, MH, 2, TS)
        xg = part(13976, T)
        ya = part(25696, KD, T)
        xbc_t = part(0, 24, T)
        pad2 = part(7680, 4, PADW)
        acc2 = part(9068, 4, PADW)
        xd = part(10444, 3, XCH)
        bt = part(16588, 3, 512)
        cbm = part(7680, SG, 448)
        w_int = part(18124, 2, 4 * 448)
        hb = part(18124, 2, 2048)
        h_t = part(22220, 2048)
        y_int = part(24268, 2, 512)
        btm = part(24268, 2, 512)
        cm = part(9472, 2, SG * TS)
        gate_tmp = part(22220, 4, T)
        g_root = part(24400, SG, T)
        gsq = part(18124, 2, 4 * T)
        acc_q = part(22220, 8, TS)
        n_rows2 = part(11800, 1152)
        y_rows = part(0, 3, D)
        merged_g = part(7680, KD, T)
        tail_out = part(19916, 2, 512)

        banks = [ctx.enter_context(nc.psum_tensor(f"bank{b}", [128, 512], FP32)) for b in range(4)]
        aux4 = ctx.enter_context(nc.psum_tensor("aux4", [128, 4, 512], FP32))
        aux = [aux4[:, b, :] for b in range(4)]

        slot_in = [sem(f"slot_in{s}") for s in range(SLOTS)]
        tile_done = sem("tile_done")
        bank_free = [sem(f"bank_free{b}") for b in range(4)]
        names = """params_in consts_made rows_clean packs_turned packs_read c_silu c_turned c_read x_turned x_read
            hist_turned hist_read mod_turned mod_read sq_ready sumsq_done root_ready u_ready res_done
            hist_put tails_saved conv_done conv_silu v_turned v_copied gate_used
            gate_mm gate_lin gate_tr sp_abs sp_exp al_ready cum_mm g_ready gb_mm mt_ready wtok_ready qk_mm s_ready
            st_mm st_copied bmx_ready last_mm ws_arg ws_exp ws_ready kt_mm kt_read qn_prod n_mm n_new n_tr n_row n_out
            masks_ready state_mm c_updated pc_mm pc_copied num_mm num_copied t1_ready num_whole var_ready std_ready
            norm_coef hn_ready hn_turned hn_read tail_tr tail_cp xt_mm xt_read bt_mm bt_read cb_mm cb_read
            lastx_mm lastx_read decx_ready hd_mm hd_rhs hd_mm2 hd_read cb_bc t_ready w_exp w_ready y_mm y_read xw_ready
            ph_mm ph_copied hmask_ready ht_mm ht_read up_mm up_done yi_mm yi_read yi_tr yi_add gsq_ready gss_done
            grs_ready gnorm_done fin_ready fin_tr fin_cp pad_zero merged act_chain dve_chain pool_chain""".split()
        S = {n: sem(n) for n in names}
        state_in = [sem(f"state_in{h}") for h in range(MH)]
        state_out = [sem(f"state_out{h}") for h in range(MH)]
        small_out = sem("small_out")
        tail_sent = [sem(f"tail_sent{h}") for h in range(2)]
        row_sent = sem("row_sent")

        def sequences(ap):
            return ap.rearrange("p (b t) -> p b t", t=ST)

        def convolved_samples(a):
            return a[:, TP + HIST:].rearrange("p (b w) -> p b w", w=HIST + ST)[:, :, 0:ST]

        def panel_source(name, p):
            if name == "ada":
                return io["ada_w"][0].rearrange("(k p) n -> p k n", p=128)[:, :, bass.ds(p * 256, 256)]
            if name in ("down1", "down2"):
                return io["ff1_w2" if name == "down1" else "ff2_w2"][0].rearrange("(k p) n -> p k n", p=128)[:, :, bass.ds(p * 128, 128)]
            if name in ("pa", "pb"):
                return io["w_" + name][0].rearrange("(k p) n -> p k n", p=128)[:, :, bass.ds(p * 128, 128)]
            if name == "out":
                return io["w_out"][0].rearrange("(k p) n -> p k n", p=128)[:, :, bass.ds(p * 256, 256)]
            off = IN_OFF["q" if name == "qk" else name]
            return io["w_in"][0].rearrange("(k p) n -> p k n", p=128)[:, :, bass.ds(p * 256 + off, 256)]

        block = ctx.enter_context(nc.Block())

        @block.sync
        def _(sp_):
            rows = [
                (pk[0:72, 0, :], io["ada_b"][0].rearrange("(r p) -> r p", p=128)),
                (pk[72:80, 0, :], io["norm_ff1"][0].rearrange("(r p) -> r p", p=128)),
                (pk[80:88, 0, :], io["norm_mix"][0].rearrange("(r p) -> r p", p=128)),
                (pk[88:96, 0, :], io["norm_ff2"][0].rearrange("(r p) -> r p", p=128)),
                (pk[96:104, 0, :], io["final_norm"].rearrange("(r p) -> r p", p=128)),
                (pk[0:16, 1, :], io["m_conv_b"][0].rearrange("(r p) -> r p", p=128)),
                (pk[16:80, 1, :], io["m_conv_w"][0].rearrange("w (r p) -> (w r) p", p=128)),
                (pk[80:96, 1, :], io["m_head_g"][0].rearrange("(r p) -> r p", p=128)),
                (pk[96:112, 1, :], io["s_norm_g"][0].rearrange("(r p) -> r p", p=128)),
                (pk[0:24, 2, :], io["s_conv_b"][0].rearrange("(r p) -> r p", p=128)),
                (pk[24:120, 2, :], io["s_conv_w"][0].rearrange("w (r p) -> (w r) p", p=128)),
                (x_rows[:, 0:2, :], io["x_prompt"][0].rearrange("(c p) d -> p c d", p=128)),
                (x_rows[0:64, 2, :], io["x_sample"].rearrange("b t d -> (b t) d")),
                (mh_rows[0:24, :], io["state_mlstm_conv"][0].rearrange("b j c -> (b j) c")),
                (sh_rows[0:24, :], io["state_ssm_conv"][0].rearrange("b j c -> (b j) c")),
                (n_rows[0:8, :], io["state_mlstm_n"][0].rearrange("b h d -> b (h d)")),
                (m0_r[:, :], io["state_mlstm_m"][0]),
                (m0_b[:, :], io["state_mlstm_m"][0].rearrange("b h -> (b h)").partition_broadcast(128)),
                (a_neg[:, :], io["s_A_log"][0].partition_broadcast(128)),
                (gate_sb[0:8, 0:1], io["m_if_b"][0].rearrange("(h o) -> h o", o=1)),
                (gate_sb[8:40, 0:1], io["s_dt_bias"][0].rearrange("(h o) -> h o", o=1)),
                (d_col[:, :], io["s_D"][0].rearrange("(h o) -> h o", o=1)),
                (gate_w[:, :, 0:8], io["w_in"][0].rearrange("(k p) n -> p k n", p=128)[:, :, IN_OFF["if"]:IN_OFF["if"] + 8]),
                (gate_w[:, :, 8:40], io["w_in"][0].rearrange("(k p) n -> p k n", p=128)[:, :, IN_OFF["dt"]:IN_OFF["dt"] + 32]),
            ]
            sp_.wait_ge(S["rows_clean"], 1)
            rows += [(c_rows[0:1, :], io["c_prompt"]), (c_rows[1:9, :], io["c_sample"])]
            with nc.allow_non_contiguous_dma(reason="a few parameter columns"):
                for dst, src in rows:
                    sp_.dma_start(dst, src).then_inc(S["params_in"], 16)

            done = 0
            last_of = []
            for name, seg in segs.items():
                for p in range(seg.panels):
                    done += seg.tiles
                    last_of.append(done)

            def load(seg, i, k):
                s = seg.slot(k)
                if isinstance(i, int):
                    if seg.g0 + 4 * i + k >= SLOTS:
                        sp_.wait_ge(tile_done, last_of[seg.g0 + 4 * i + k - SLOTS])
                else:
                    sp_.wait_ge(tile_done, i * (4 * seg.tiles) + (seg.t0 + (k - SLOTS + 1) * seg.tiles))
                if seg.name in ("up1", "up2"):
                    which = ("ff1_" if seg.name == "up1" else "ff2_") + ("w1" if k % 2 == 0 else "w3")
                    src = io[which][0].rearrange("(k p) n -> p k n", p=128)[:, :, bass.ds(i * 512 + (k // 2) * 256, 256)]
                else:
                    src = panel_source(seg.name, i * 4 + k)
                width = 256 if seg.kc == KD else 128
                dst = ring[s][:, 0:seg.kc * width].rearrange("p (k n) -> p k n", n=width)
                sp_.dma_start(dst, src).then_inc(slot_in[s], 16)

            for name, seg in segs.items():
                walk(sp_, seg, lambda i, k: load(seg, i, k))

        @block.gpsimd
        def _(pool):
            ch = Chain(pool, S["pool_chain"])
            nc.gpsimd.memset(c_rows[0:32, :], 0.0).then_inc(S["rows_clean"], 1)
            for m, v in ((ident, 0.0), (ones, 1.0), (tri, 1.0), (tri_s, 1.0), (neg_p, 0.0), (neg_s, 0.0), (seg_m, 1.0),
                         (seg_b, 0.0), (seg_t, 0.0), (row_last, 0.0), (last_s, 0.0), (last_b, 0.0), (mod_sum, 0.0),
                         (tile_of_head, 1.0), (g3, 0.0), (cum, 0.0), (sm, 0.0), (mean_var, 0.0)):
                ch.inc(nc.gpsimd.memset(m[:], v))
            ch.settle()

            def keep(ap, pattern, op, fill, base=0, per_partition=0):
                ch.link(nc.gpsimd.affine_select(out=ap, in_=ap, compare_op=op, fill=fill, base=base, pattern=pattern,
                                                channel_multiplier=per_partition))

            keep(ident[:, :], [[-1, 128]], ALU.not_equal, 1.0, 0, 1)
            keep(tri[:, 0:128], [[1, 128]], ALU.is_ge, 0.0, 0, -1)
            keep(tri[:, 256:384], [[1, 128]], ALU.is_ge, 0.0, 0, -1)
            ts4 = tri_s[:, :].rearrange("p (r b t) -> p r b t", r=2, t=ST)
            keep(ts4, [[0, 2], [-8, 8], [0, 8]], ALU.is_ge, 0.0, 0, 1)
            keep(ts4, [[0, 2], [8, 8], [1, 8]], ALU.is_ge, 0.0, 0, -1)
            keep(neg_p[:, :], [[-1, 128]], ALU.is_ge, NEG, 0, 1)
            ns3 = neg_s[:, :].rearrange("p (b t) -> p b t", t=ST)
            keep(ns3, [[-8, 8], [-1, 8]], ALU.is_ge, NEG, 0, 1)
            keep(ns3, [[8, 8], [0, 8]], ALU.is_ge, NEG, 7, -1)
            keep(seg_m[:, :], [[-8, 8]], ALU.is_ge, 0.0, 0, 1)
            keep(seg_m[:, :], [[8, 8]], ALU.is_ge, 0.0, 7, -1)
            keep(seg_b[:, :, :].rearrange("p c (b t) -> p c b t", t=ST), [[1, 8], [-1, 8], [0, 8]], ALU.not_equal, 1.0)
            keep(seg_t[:, :].rearrange("p (b t) -> p b t", t=ST), [[-1, 8], [0, 8]], ALU.not_equal, 1.0, 0, 1)
            keep(row_last[:, :], [[0, 128]], ALU.not_equal, 1.0, -127, 1)
            keep(last_s[:, :].rearrange("p (b t) -> p b t", t=ST), [[-8, 8], [0, 8]], ALU.not_equal, 1.0, -7, 1)
            keep(last_b[:, :], [[-8, 8]], ALU.not_equal, 1.0, -7, 1)
            for j in range(4):
                keep(mod_sum[:, :], [[-1, NSEQ]], ALU.not_equal, 1.0, -32 * j, 1)
            keep(tile_of_head[:, :], [[-2, 16]], ALU.is_ge, 0.0, 0, 1)
            keep(tile_of_head[:, :], [[2, 16]], ALU.is_ge, 0.0, 1, -1)
            nc.gpsimd.memset(sp[:], 0.0).then_inc(S["consts_made"], 1)

            def conv_side(seg, first, padded):
                def step(i, k):
                    for j in range(seg.tiles):
                        r = (k * seg.tiles + j) % 4
                        c = seg.own(i, k, j) + first
                        own = seg.own(i, k, j)
                        r2 = padded[:, r, TP + HIST:].rearrange("p (b w) -> p b w", w=HIST + ST)
                        if not isinstance(i, int) or 4 * i * seg.tiles + k * seg.tiles + j >= 4:
                            pool.wait_ge(S["conv_done"], c - 3)
                        nc.gpsimd.tensor_copy(r2[:, :, 0:HIST], hist[:, bass.ds(c, 1), :].rearrange("p o (b w) -> p (o b) w", w=HIST))\
                            .then_inc(S["hist_put"], 1)
                        pool.wait_ge(bank_free[seg.bank(k, j)], seg.bank_use(i, k, j) + 1)
                        ch.inc(nc.gpsimd.tensor_copy(tails[:, bass.ds(c, 1), 0:HIST], padded[:, r:r + 1, TP:TP + HIST]))
                        nc.gpsimd.tensor_copy(tails[:, bass.ds(c, 1), HIST:].rearrange("p o (b w) -> p (o b) w", w=HIST),
                                              r2[:, :, ST:]).then_inc(S["tails_saved"], 1)
                        pool.wait_ge(S["tails_saved"], c + 1)
                walk(pool, seg, step, ch, seg.tiles)

            pool.wait_ge(S["hist_read"], 3)
            pool.wait_ge(S["sumsq_done"], 2)
            nc.gpsimd.memset(pad[:, :, 0:HIST], 0.0).then_inc(S["pad_zero"], 1)
            conv_side(segs["qk"], 0, pad)

            def send_tails(first, tiles, prompt, sample, count0):
                for r in range(tiles // 4):
                    n = count0 + r
                    pool.wait_ge(S["tail_cp"], n + 1)
                    cols = slice(r * 512, (r + 1) * 512)
                    pool.dma_start(prompt[0, 0][:, cols], tail_out[0:HIST, n % 2, :]).then_inc(tail_sent[n % 2], 16)
                    pool.dma_start(sample[0].rearrange("b j c -> (b j) c")[:, cols], tail_out[HIST:27, n % 2, :])\
                        .then_inc(tail_sent[n % 2], 16)
            send_tails(0, 16, out["p_mconv"], out["s_mconv"], 0)

            def c_of(ap, b, h):
                return ap[0, bass.ds(b, 1), h].rearrange("o (d p) v -> p (o d) v", p=128)

            def cbuf(h):
                return cb[:, h, :].rearrange("p (d v) -> p d v", v=DV)

            for h in range(MH):
                pool.dma_start(cbuf(h), c_of(io["state_mlstm_C"], 0, h)).then_inc(state_in[h], 16)
            with pool.Fori(0, SB - 1) as b:
                for h in range(MH):
                    pool.wait_ge(S["c_updated"], b * MH + (h + 1))
                    pool.dma_start(c_of(out["s_C"], b, h), cbuf(h)).then_inc(state_out[h], 16)
                    pool.wait_ge(state_out[h], b * 16 + 16)
                    pool.dma_start(cbuf(h), c_of(io["state_mlstm_C"], b + 1, h)).then_inc(state_in[h], 16)
            for h in range(MH):
                pool.wait_ge(S["c_updated"], (SB - 1) * MH + h + 1)
                pool.dma_start(c_of(out["s_C"], SB - 1, h), cbuf(h)).then_inc(state_out[h], 16)
            for h in range(MH):
                pool.wait_ge(S["pc_copied"], 2 * (h + 1))
                pool.dma_start(c_of(out["p_C"], 0, h), cbuf(h)).then_inc(state_out[h], 16)
            pool.wait_ge(S["ws_ready"], 1)
            pool.dma_start(out["p_m"][0], sm[0:1, 6, 4:8]).then_inc(small_out, 16)
            pool.dma_start(out["s_m"].rearrange("o b h -> o (b h)"), sm[0:1, 11, 0:32]).then_inc(small_out, 16)
            pool.wait_ge(S["n_row"], 2)
            pool.dma_start(out["p_n"][0, 0].rearrange("h (d p) -> (h d) p", p=128), n_rows2[0:8, 1024:1152]).then_inc(small_out, 16)
            pool.dma_start(out["s_n"][0].rearrange("b h d -> b (h d)"), n_rows2[0:8, 0:1024]).then_inc(small_out, 16)

            pool.wait_ge(S["hn_read"], 16)
            nc.gpsimd.memset(pad2[:, :, 0:HIST], 0.0).then_inc(S["pad_zero"], 1)
            conv_side(segs["xbc"], 16, pad2)
            send_tails(16, 24, out["p_sconv"], out["s_sconv"], 4)

            def h_of(ap, b):
                return ap[0, bass.ds(b, 1)].rearrange("o (t e) q n -> (e q) (o t) n", e=2)

            def hbuf(r):
                return hb[:, r, :].rearrange("p (t n) -> p t n", n=SN)

            pool.wait_ge(S["ph_copied"], 4)
            pool.dma_start(h_of(out["p_ssm"], 0), h_t.rearrange("p (t n) -> p t n", n=SN)).then_inc(row_sent, 16)
            pool.wait_ge(S["y_mm"], 8)
            for r in range(2):
                pool.dma_start(hbuf(r), h_of(io["state_ssm"], r)).then_inc(state_in[r], 16)
            with pool.Fori(0, SB // 2 - 1) as i:
                for r in range(2):
                    pool.wait_ge(S["up_done"], i * 8 + 4 * (r + 1))
                    pool.dma_start(h_of(out["s_ssm"], i * 2 + r), hbuf(r)).then_inc(state_out[r], 16)
                    pool.wait_ge(state_out[r], i * 16 + (16 * (SB + 1) + 16))
                    pool.dma_start(hbuf(r), h_of(io["state_ssm"], i * 2 + (r + 2))).then_inc(state_in[r], 16)
            for r in range(2):
                pool.wait_ge(S["up_done"], (SB // 2 - 1) * 8 + 4 * (r + 1))
                pool.dma_start(h_of(out["s_ssm"], SB - 2 + r), hbuf(r)).then_inc(state_out[r], 16)

            for c in range(3):
                pool.wait_ge(S["fin_cp"], 2 * (c + 1))
                if c < 2:
                    pool.dma_start(out["y_p"][0, c * 128:(c + 1) * 128, :], y_rows[:, c, :]).then_inc(small_out, 16)
                else:
                    pool.dma_start(out["y_s"].rearrange("b t d -> (b t) d"), y_rows[0:64, 2, :]).then_inc(small_out, 16)
            pool.wait_ge(small_out, 7 * 16)
            pool.wait_ge(row_sent, 16)
            for r in range(2):
                pool.wait_ge(tail_sent[r], 5 * 32)
            for h in range(MH):
                pool.wait_ge(state_out[h], 16 * (SB + 1) + (16 * (SB // 2) if h < 2 else 0))

        @block.tensor
        def _(pe):
            def turn(dst, src, rows):
                return nc.tensor.transpose(dst, src, ident[0:rows, 0:rows])

            def mm(dst, lhs, rhs, first=True, last=True):
                return nc.tensor.matmul(dst, lhs, rhs, start=first, stop=last)

            def dense(seg, src, after=None):
                width = 256 if seg.kc == KD else 128

                def step(i, k):
                    s = seg.slot(k)
                    w = ring[s][:, 0:seg.kc * width].rearrange("p (k n) -> p k n", n=width)
                    pe.wait_ge(slot_in[s], seg.slot_use(i, k) * 16)
                    for j in range(seg.tiles):
                        b = seg.bank(k, j)
                        pe.wait_ge(bank_free[b], seg.bank_use(i, k, j))
                        for kc in range(seg.kc):
                            ins = mm(banks[b][:, 0:T], w[:, kc, j * 128:(j + 1) * 128], src[:, kc, :], kc == 0, kc == seg.kc - 1)
                        ins.then_inc(tile_done, 1)
                        if after:
                            after(i, k, j)
                walk(pe, seg, step)

            def settle_banks(seg):
                total = seg.t0 + seg.panels * seg.tiles
                for b in range(4):
                    pe.wait_ge(bank_free[b], total // 4)

            pe.wait_ge(S["params_in"], 26 * 16)
            pe.wait_ge(S["consts_made"], 1)
            turn(aux[0][:, 0:104], pk[0:104, 0, :], 104)
            turn(aux[0][:, 104:216], pk[0:112, 1, :], 112)
            turn(aux[0][:, 216:336], pk[0:120, 2, :], 120)
            for kc in range(8):
                ins = turn(aux[0][:, 336 + 8 * kc:344 + 8 * kc], n_rows[0:8, kc * 128:(kc + 1) * 128], 8)
            ins.then_inc(S["packs_turned"], 1)
            pe.wait_ge(S["c_silu"], 1)
            for kc in range(KD):
                ins = turn(aux[1][:, 32 * kc:32 * kc + 32], c_rows[0:32, kc * 128:(kc + 1) * 128], 32)
            ins.then_inc(S["c_turned"], 1)
            for c in range(16):
                ins = turn(aux[2][:, 24 * c:24 * c + 24], mh_rows[0:24, c * 128:(c + 1) * 128], 24)
            for c in range(20):
                ins = turn(aux[3][:, 24 * c:24 * c + 24], sh_rows[0:24, c * 128:(c + 1) * 128], 24)
            for c in range(4):
                ins = turn(aux[2][:, 384 + 24 * c:408 + 24 * c], sh_rows[0:24, (20 + c) * 128:(21 + c) * 128], 24)
            ins.then_inc(S["hist_turned"], 1)
            for kc in range(KD):
                b = kc % 4
                if kc == 0:
                    pe.wait_ge(S["packs_read"], 1)
                elif kc == 1:
                    pe.wait_ge(S["c_read"], 1)
                elif kc == 2:
                    pe.wait_ge(S["hist_read"], 3)
                elif kc >= 4:
                    pe.wait_ge(S["x_read"], kc - 3)
                turn(aux[b][:, 0:128], x_rows[:, 0, kc * 128:(kc + 1) * 128], 128)
                turn(aux[b][:, 128:256], x_rows[:, 1, kc * 128:(kc + 1) * 128], 128)
                turn(aux[b][:, 256:320], x_rows[0:64, 2, kc * 128:(kc + 1) * 128], 64).then_inc(S["x_turned"], 1)
            pe.wait_ge(S["x_read"], KD)

            ada = segs["ada"]

            def mod_columns(i, k):
                p = ada.own(i, k)
                r = k % 2
                pe.wait_ge(bank_free[ada.bank(k)], ada.bank_use(i, k) + 1)
                if not isinstance(i, int) or 4 * i + k >= 2:
                    pe.wait_ge(S["mod_read"], p - 1)
                for j in range(2):
                    ins = mm(aux[r][:, NSEQ * j:NSEQ * (j + 1)], mod_row[r][:, j * 128:(j + 1) * 128], mod_sum[:, :])
                ins.then_inc(S["mod_turned"], 1)

            def ada_step(i, k):
                s, b = ada.slot(k), ada.bank(k)
                w = ring[s][:, 0:KD * 256].rearrange("p (k n) -> p k n", n=256)
                pe.wait_ge(slot_in[s], ada.slot_use(i, k) * 16)
                if not isinstance(i, int) or i > 0:
                    pe.wait_ge(bank_free[b], ada.bank_use(i, k))
                for kc in range(KD):
                    q = kc % 4
                    ins = mm(banks[b][32 * q:32 * q + 32, 0:256], c_t[:, kc, :], w[:, kc, :], kc < 4, kc >= 4)
                ins.then_inc(tile_done, 1)
                if k > 0:
                    mod_columns(i, k - 1)
                elif not isinstance(i, int) or i > 0:
                    mod_columns(i - 1, 3)
            walk(pe, ada, ada_step)
            mod_columns(ada.panels // 4 - 1, 3)

            def sum_squares(n):
                pe.wait_ge(S["sq_ready"], n + 1)
                for kc in range(KD):
                    ins = mm(aux[0][:, 0:T], ones[:, :], sq[:, kc, :], kc == 0, kc == KD - 1)
                ins.then_inc(S["sumsq_done"], 1)

            pe.wait_ge(S["mod_read"], ada.panels)
            sum_squares(0)
            pe.wait_ge(S["u_ready"], 1)
            dense(segs["up1"], u_t)
            settle_banks(segs["up1"])
            dense(segs["down1"], ff_h)
            sum_squares(1)

            pe.wait_ge(S["u_ready"], 2)
            for kc in range(KD):
                ins = mm(aux[1][0:40, 0:T], gate_w[:, kc, :], u_t[:, kc, :], kc == 0, kc == KD - 1)
            ins.then_inc(S["gate_mm"], 1)
            dense(segs["qk"], u_t)
            pe.wait_ge(S["gate_lin"], 1)
            turn(aux[2][:, 0:40], xg[0:40, 0:128], 40)
            turn(aux[2][:, 40:80], xg[0:40, 128:256], 40)
            turn(aux[2][0:64, 80:120], xg[0:40, 256:320], 40).then_inc(S["gate_tr"], 1)

            vs = segs["v"]

            def turn_v(i, k, j):
                own = vs.own(i, k, j)
                r = (k * 2 + j) % 4
                x = aux[r % 2]
                pe.wait_ge(bank_free[vs.bank(k, j)], vs.bank_use(i, k, j) + 1)
                if not isinstance(i, int) or 8 * i + 2 * k + j >= 2:
                    pe.wait_ge(S["v_copied"], own - 1)
                turn(x[:, 0:128], v_tmp[:, r, 0:128], 128)
                turn(x[:, 128:256], v_tmp[:, r, 128:256], 128)
                turn(x[0:64, 256:384], v_tmp[:, r, 256:320], 128).then_inc(S["v_turned"], 1)

            def after_v(i, k, j):
                if j > 0:
                    turn_v(i, k, 0)
                elif k > 0:
                    turn_v(i, k - 1, 1)
                elif not isinstance(i, int) or i > 0:
                    turn_v(i - 1, 3, 1)
            dense(vs, u_t, after_v)
            turn_v(1, 3, 1)

            def turn_tails(first, tiles, count0):
                for r in range(tiles // 4):
                    n = count0 + r
                    x = aux[3 if count0 == 0 else n % 2]
                    if n > 0 and count0 == 0:
                        pe.wait_ge(S["tail_cp"], n)
                    if count0 and r >= 2:
                        pe.wait_ge(S["tail_cp"], n - 1)
                    for j in range(4):
                        ins = turn(x[0:27, j * 128:(j + 1) * 128], tails[:, first + 4 * r + j, :], 128)
                    ins.then_inc(S["tail_tr"], 1)
            pe.wait_ge(S["tails_saved"], 16)
            turn_tails(0, 16, 0)

            pe.wait_ge(S["al_ready"], 1)
            mm(aux[2][:, 0:36], tri[:, 0:128], al[:, 0, :])
            mm(aux[2][:, 36:72], ones[:, :], al[:, 0, :], True, False)
            mm(aux[2][:, 36:72], tri[:, 0:128], al[:, 1, :], False, True)
            mm(aux[2][:, 72:108], tri_s[:, :], al[0:64, 2, :])
            mm(aux[2][0:64, 108:112], seg_t[:, :], m0_r[:, :]).then_inc(S["cum_mm"], 1)
            pe.wait_ge(S["g_ready"], 1)
            pe.wait_ge(S["v_copied"], 16)
            pe.wait_ge(S["tail_cp"], 4)
            for h in range(MH):
                mm(aux[h][:, 0:128], sm[:, 0, h:h + 1].to_broadcast([128, 128]), ident[:, :])
                mm(aux[h][:, 128:256], sm[:, 1, h:h + 1].to_broadcast([128, 128]), ident[:, :])
                mm(aux[h][0:64, 256:320], sm[0:64, 2, h:h + 1].to_broadcast([64, 64]), ident[0:64, 0:64]).then_inc(S["gb_mm"], 1)
            pe.wait_ge(S["mt_ready"], 1)
            for h in range(MH):
                for d in range(2):
                    mm(aux[h][:, 0:128], qk_t[:, 2 * h + d, 0:128], qk_t[:, 8 + 2 * h + d, 0:128], d == 0, d == 1)
                for d in range(2):
                    mm(aux[h][:, 128:384], qk_t[:, 2 * h + d, 128:256], qk_t[:, 8 + 2 * h + d, 0:256], d == 0, d == 1)
                for d in range(2):
                    ins = mm(aux[h][0:64, 384:448], qk_t[:, 2 * h + d, 256:320], qk_t[:, 8 + 2 * h + d, 256:320], d == 0, d == 1)
                ins.then_inc(S["qk_mm"], 1)
            settle_banks(segs["v"])
            pe.wait_ge(S["bmx_ready"], 1)
            mm(banks[0][:, 0:8], row_last[:, :], sm[:, 4, 8:16])
            mm(banks[0][0:64, 8:16], last_s[:, :], sm[0:64, 4, 16:24])
            mm(banks[0][:, 16:80], ones[0:64, :], al2[0:64, :]).then_inc(S["last_mm"], 1)
            for h in range(MH):
                pe.wait_ge(S["s_ready"], h + 1)
                turn(aux[h][:, 0:128], dm[:, h, 0:128], 128)
                turn(aux[h][:, 128:256], dm[:, h, 128:256], 128)
                turn(aux[h][:, 256:384], dm[:, h, 256:384], 128)
                turn(aux[h][0:64, 384:448], dm[0:64, h, 384:448], 64).then_inc(S["st_mm"], 1)
            pe.wait_ge(S["ws_ready"], 1)
            for c in range(8):
                b = banks[c % 4]
                if c >= 4:
                    pe.wait_ge(S["kt_read"], c - 3)
                turn(b[:, 0:128], qk_t[:, 8 + c, 0:128], 128)
                turn(b[:, 128:256], qk_t[:, 8 + c, 128:256], 128)
                turn(b[0:64, 256:384], qk_t[:, 8 + c, 256:320], 128).then_inc(S["kt_mm"], 1)
            pe.wait_ge(S["kt_read"], 8)
            pe.wait_ge(S["qn_prod"], 1)
            for h in range(MH):
                for d in range(2):
                    mm(banks[0][0:64, h:h + 1], acc_q[:, 2 * h + d, :], ones[:, 0:1], d == 0, d == 1)
            for c in range(8):
                mm(banks[0][:, 8 + 8 * c:16 + 8 * c], kw[0:64, 2, c * 128:(c + 1) * 128], seg_m[:, :])
            for c in range(8):
                mm(banks[0][:, 80 + c:81 + c], kw[:, 0, c * 128:(c + 1) * 128], ones[:, 0:1], True, False)
                ins = mm(banks[0][:, 80 + c:81 + c], kw[:, 1, c * 128:(c + 1) * 128], ones[:, 0:1], False, True)
            ins.then_inc(S["n_mm"], 1)
            pe.wait_ge(S["n_new"], 1)
            for c in range(8):
                bk = banks[1 + c // 4]
                turn(bk[0:8, (c % 4) * 128:(c % 4 + 1) * 128], n_t[:, c, :], 128)
            turn(banks[3][0:8, 0:128], sm[:, 7, 0:8], 128).then_inc(S["n_tr"], 1)

            pe.wait_ge(S["st_copied"], MH)
            pe.wait_ge(S["n_row"], 2)

            def memory(b, h, first, last=False):
                n = b * MH + h
                c_h = cb[:, h, :].rearrange("p (d v) -> p d v", v=DV)
                pe.wait_ge(state_in[h], b * 16 + 16)
                pe.wait_ge(S["masks_ready"], n + 1)
                for d in range(2):
                    mm(aux[h][64 * d:64 * d + 64, :], qm[:, h, d, :], c_h[:, d, :], first, last)
                if not first or h >= 2:
                    pe.wait_ge(S["c_updated"], n - 1)
                for d in range(2):
                    ins = mm(banks[2 * (h % 2) + d][:, :], kwm[0:64, h, d * 128:(d + 1) * 128], v_tok[0:64, 2, h * DV:(h + 1) * DV])
                ins.then_inc(S["state_mm"], 1)
            for h in range(MH):
                memory(0, h, True)
            with pe.Fori(1, SB - 1) as b:
                for h in range(MH):
                    memory(b, h, False)
            for h in range(MH):
                memory(SB - 1, h, False, True)
            for h in range(MH):
                for d in range(2):
                    n = 2 * h + d
                    bk = banks[n % 4]
                    pe.wait_ge(S["c_updated"], SB * MH)
                    if n >= 4:
                        pe.wait_ge(S["pc_copied"], n - 3)
                    c = h * 2 + d
                    mm(bk[:, :], kw[:, 0, c * 128:(c + 1) * 128], v_tok[:, 0, h * DV:(h + 1) * DV], True, False)
                    mm(bk[:, :], kw[:, 1, c * 128:(c + 1) * 128], v_tok[:, 1, h * DV:(h + 1) * DV], False, True).then_inc(S["pc_mm"], 1)
            pe.wait_ge(S["pc_copied"], 8)

            def turn_head(h):
                pe.wait_ge(S["hn_ready"], h + 1)
                nm = (num, num2)[h % 2]
                for j in range(4):
                    c = 4 * h + j
                    pe.wait_ge(S["num_whole"], h + 1)
                    x = aux[h]
                    if j > 0:
                        pe.wait_ge(S["hn_read"], c)
                    turn(x[:, 0:128], nm[:, 0, j * 128:(j + 1) * 128], 128)
                    turn(x[:, 128:256], nm[:, 1, j * 128:(j + 1) * 128], 128)
                    turn(x[:, 256:320], nm[0:64, 2, j * 128:(j + 1) * 128], 64).then_inc(S["hn_turned"], 1)
            for h in range(MH):
                if h > 0:
                    pe.wait_ge(S["num_whole"], h)
                v_h = slice(h * DV, (h + 1) * DV)
                mm(banks[0][:, :], st_s[:, h, 0:128], v_tok[:, 0, v_h])
                mm(banks[1][:, :], st_s[:, h, 128:256], v_tok[:, 0, v_h], True, False)
                mm(banks[1][:, :], st_s[:, h, 256:384], v_tok[:, 1, v_h], False, True)
                mm(banks[2][0:64, :], st_s[0:64, h, 384:448], v_tok[0:64, 2, v_h]).then_inc(S["num_mm"], 1)
                if h > 0:
                    turn_head(h - 1)
            turn_head(MH - 1)

            pe.wait_ge(S["num_whole"], MH)
            dense(segs["mo"], u_t)
            pe.wait_ge(S["gate_used"], 16)
            dense(segs["pa"], hm)
            dense(segs["xbc"], u_t)

            settle_banks(segs["xbc"])
            pe.wait_ge(S["tails_saved"], 40)
            turn_tails(16, 24, 4)
            pe.wait_ge(S["conv_silu"], 40)
            for n in range(12):
                gr, c = divmod(n, 3)
                b = banks[n % 4]
                if n >= 4:
                    pe.wait_ge(S["xt_read"], n - 3)
                for j in range(4):
                    src = xbc_t[:, 4 * gr + j, c * 128:min(T, (c + 1) * 128)]
                    dst = b[:, j * 128:(j + 1) * 128] if c < 2 else b[0:64, j * 128:(j + 1) * 128]
                    ins = turn(dst, src, 128)
                ins.then_inc(S["xt_mm"], 1)
            for c in range(3):
                if c == 0:
                    pe.wait_ge(S["tail_cp"], 10)
                x = aux[c]
                for j in range(4):
                    src = xbc_t[:, 16 + j, c * 128:min(T, (c + 1) * 128)]
                    dst = x[:, j * 128:(j + 1) * 128] if c < 2 else x[0:64, j * 128:(j + 1) * 128]
                    ins = turn(dst, src, 128)
                ins.then_inc(S["bt_mm"], 1)
            for gr in range(SG):
                b = banks[gr]
                pe.wait_ge(S["xt_read"], 12)
                mm(b[:, 0:256], xbc_t[:, 16 + gr, 0:128], xbc_t[:, 20 + gr, 0:256])
                mm(b[:, 256:384], xbc_t[:, 16 + gr, 128:256], xbc_t[:, 20 + gr, 128:256])
                mm(b[0:64, 384:448], xbc_t[:, 16 + gr, 256:320], xbc_t[:, 20 + gr, 256:320]).then_inc(S["cb_mm"], 1)
            mm(aux[3][:, 0:32], row_last[:, :], cum[:, 1, 4:36])
            mm(aux[3][0:64, 32:64], last_s[:, :], cum[0:64, 2, 4:36]).then_inc(S["lastx_mm"], 1)
            pe.wait_ge(S["decx_ready"], 1)
            mm(aux[3][0:32, 64:72], sm[0:64, 8, 0:32], last_b[:, :]).then_inc(S["hd_mm"], 1)
            pe.wait_ge(S["hd_rhs"], 1)
            mm(aux[3][:, 128:272], parity[:, :, :].rearrange("p a b -> p (a b)"), hd_in[0:32, :]).then_inc(S["hd_mm2"], 1)

            def decay_rows(q):
                for j in range(4):
                    h = 4 * q + j
                    if q == 0:
                        if j < 3:
                            pe.wait_ge(S["bt_read"], j + 1)
                        else:
                            pe.wait_ge(S["hd_read"], 1)
                    else:
                        pe.wait_ge(S["t_ready"], 4 * (q - 1) + j + 1)
                    mm(aux[j][:, 0:128], al[:, 0, 4 + h:5 + h].to_broadcast([128, 128]), tri[:, 0:128])
                    mm(aux[j][:, 128:256], al[:, 0, 4 + h:5 + h].to_broadcast([128, 128]), ones[:, :], True, False)
                    mm(aux[j][:, 128:256], al[:, 1, 4 + h:5 + h].to_broadcast([128, 128]), tri[:, 0:128], False, True)
                    mm(aux[j][0:64, 256:320], al[0:64, 2, 4 + h:5 + h].to_broadcast([64, 64]), tri_s[:, 0:64]).then_inc(S["cb_bc"], 1)

            def head_outputs(q):
                pe.wait_ge(S["w_ready"], q + 1)
                w = w_int[:, q % 2, :].rearrange("p (j s) -> p j s", s=448)
                for pr in range(2):
                    n = 2 * q + pr
                    b = banks[n % 4]
                    if n < 4:
                        pe.wait_ge(S["cb_read"], n + 1)
                    else:
                        pe.wait_ge(S["y_read"], n - 3)
                    for e in range(2):
                        h = 4 * q + 2 * pr + e
                        o = slice(64 * e, 64 * e + 64)
                        col = slice(h * 64, (h + 1) * 64)
                        mm(b[o, 0:128], xd[:, 0, col], w[:, 2 * pr + e, 0:128])
                        mm(b[o, 128:256], xd[:, 0, col], w[:, 2 * pr + e, 128:256], True, False)
                        mm(b[o, 128:256], xd[:, 1, col], w[:, 2 * pr + e, 256:384], False, True)
                        ins = mm(b[o, 256:320], xd[0:64, 2, col], w[0:64, 2 * pr + e, 384:448])
                    ins.then_inc(S["y_mm"], 1)
            decay_rows(0)
            for q in range(8):
                if q < 7:
                    decay_rows(q + 1)
                head_outputs(q)
            pe.wait_ge(S["xw_ready"], 1)
            for gr in range(SG):
                pe.wait_ge(S["y_read"], 16)
                for j in range(4):
                    c = slice((4 * gr + j) * 128, (4 * gr + j + 1) * 128)
                    mm(banks[gr][:, j * 128:(j + 1) * 128], xd[:, 0, c], bt[:, 0, gr * 128:(gr + 1) * 128], True, False)
                    ins = mm(banks[gr][:, j * 128:(j + 1) * 128], xd[:, 1, c], bt[:, 1, gr * 128:(gr + 1) * 128], False, True)
                ins.then_inc(S["ph_mm"], 1)

            def ssm_step(i, r, first, last=False):
                b = i * 2 + r
                h3 = hb[:, r, :].rearrange("p (t n) -> p t n", n=SN)
                up_banks = (aux[2], aux[3], banks[2], banks[3])
                pe.wait_ge(state_in[r], i * 16 + (16 * SB + 16))
                pe.wait_ge(S["hmask_ready"], b + 1)
                for gr in range(SG):
                    if not first or gr >= 2:
                        pe.wait_ge(S["ht_read"], b * 4 + (gr - 1))
                    for j in range(4):
                        ins = turn(aux[gr % 2][:, j * 128:(j + 1) * 128], h3[:, 4 * gr + j, :], 128)
                    ins.then_inc(S["ht_mm"], 1)
                    if not first:
                        pe.wait_ge(S["up_done"], b * 4 + (gr - 3))
                    for j in range(4):
                        c = 4 * gr + j
                        ins = mm(up_banks[gr][:, j * 128:(j + 1) * 128], xd[0:64, 2, c * 128:(c + 1) * 128],
                                 btm[0:64, r, gr * 128:(gr + 1) * 128])
                    ins.then_inc(S["up_mm"], 1)
                for gr in range(SG):
                    pe.wait_ge(S["ht_read"], b * 4 + (gr + 1))
                    o = slice(64 * (gr % 2), 64 * (gr % 2) + 64)
                    ins = mm(banks[gr // 2][o, :], cm[:, r, gr * TS:(gr + 1) * TS], h_t[:, gr * 512:(gr + 1) * 512], first, last)
                ins.then_inc(S["yi_mm"], 1)
            pe.wait_ge(S["ph_copied"], 4)
            pe.wait_ge(row_sent, 16)
            ssm_step(0, 0, True)
            ssm_step(0, 1, False)
            with pe.Fori(1, SB // 2 - 1) as i:
                ssm_step(i, 0, False)
                ssm_step(i, 1, False)
            ssm_step(SB // 2 - 1, 0, False)
            ssm_step(SB // 2 - 1, 1, False, True)
            pe.wait_ge(S["yi_read"], 2)
            pe.wait_ge(S["ht_read"], 4 * SB)
            for gr in range(SG):
                o = slice(64 * (gr % 2), 64 * (gr % 2) + 64)
                for j in range(4):
                    c = 4 * gr + j
                    ins = nc.tensor.transpose(aux[gr][:, j * 64:(j + 1) * 64], y_int[o, gr // 2, j * 128:(j + 1) * 128], ident[o, o])
                ins.then_inc(S["yi_tr"], 1)
            pe.wait_ge(S["up_done"], 4 * SB)
            pe.wait_ge(S["yi_add"], SG)
            dense(segs["z"], u_t)
            for gr in range(SG):
                pe.wait_ge(S["gsq_ready"], gr + 1)
                for j in range(4):
                    ins = mm(aux[gr][:, 0:T], ones[:, :], gsq[:, gr % 2, j * T:(j + 1) * T], j == 0, j == 3)
                ins.then_inc(S["gss_done"], 1)
            dense(segs["ga"], u_t)
            dense(segs["gb"], u_t)
            pe.wait_ge(S["gnorm_done"], 16)
            dense(segs["pb"], xbc_t)
            settle_banks(segs["pb"])
            pe.wait_ge(S["merged"], KD)
            dense(segs["out"], ya)
            sum_squares(2)
            pe.wait_ge(S["u_ready"], 3)
            dense(segs["up2"], u_t)
            settle_banks(segs["up2"])
            dense(segs["down2"], ff_h)
            sum_squares(3)
            pe.wait_ge(S["fin_ready"], 1)
            for c in range(3):
                rows = 128 if c < 2 else 64
                for half in range(2):
                    n = 2 * c + half
                    x = aux[1 + n % 2]
                    if n >= 2:
                        pe.wait_ge(S["fin_cp"], n - 1)
                    for j in range(4):
                        ins = turn(x[0:rows, j * 128:(j + 1) * 128], u_t[:, 4 * half + j, c * 128:c * 128 + rows], 128)
                    ins.then_inc(S["fin_tr"], 1)

        @block.scalar
        def _(act):
            ch = Chain(act, S["act_chain"])

            def copy(dst, src, scale=1.0):
                return nc.scalar.activation(dst, src, ACT.Copy, scale=scale)

            act.wait_ge(S["params_in"], 26 * 16)
            nc.scalar.activation(c_rows[0:32, :], c_rows[0:32, :], ACT.Silu).then_inc(S["c_silu"], 1)
            act.wait_ge(S["packs_turned"], 1)
            ch.inc(copy(par[:, :], aux[0][:, 0:336]))
            copy(n_t[:, :, :], aux[0][:, 336:400].rearrange("p (a b) -> p a b", b=SB)).then_inc(S["packs_read"], 1)
            act.wait_ge(S["c_turned"], 1)
            copy(c_t[:, :, :], aux[1][:, 0:256].rearrange("p (a b) -> p a b", b=32)).then_inc(S["c_read"], 1)
            act.wait_ge(S["hist_turned"], 1)
            copy(hist[:, 0:16, :], aux[2][:, 0:384].rearrange("p (a b) -> p a b", b=24)).then_inc(S["hist_read"], 1)
            copy(hist[:, 16:36, :], aux[3][:, 0:480].rearrange("p (a b) -> p a b", b=24)).then_inc(S["hist_read"], 1)
            copy(hist[:, 36:40, :], aux[2][:, 384:480].rearrange("p (a b) -> p a b", b=24)).then_inc(S["hist_read"], 1)
            for kc in range(KD):
                act.wait_ge(S["x_turned"], kc + 1)
                copy(x_t[:, kc, :], aux[kc % 4][:, 0:T]).then_inc(S["x_read"], 1)
            nc.scalar.activation(a_neg[:, :], a_neg[:, :], ACT.Exp).then_inc(S["act_chain"], 1)
            ch.n += 1

            def square(n):
                nc.scalar.activation(sq[:, :, :], x_t[:, :, :], ACT.Square).then_inc(S["sq_ready"], 1)

            def root(n):
                act.wait_ge(S["sumsq_done"], n + 1)
                nc.scalar.activation(rs[:, :], aux[0][:, 0:T], ACT.Sqrt, bias=eps_col[:, 0:1], scale=1.0 / D).then_inc(S["root_ready"], 1)

            act.wait_ge(S["x_read"], KD)
            square(0)

            ada = segs["ada"]

            def ada_row(i, k):
                p, b = ada.own(i, k), ada.bank(k)
                act.wait_ge(tile_done, ada.tile_no(i, k) + 1)
                if not isinstance(i, int) or 4 * i + k >= 2:
                    act.wait_ge(S["mod_turned"], p - 1)
                copy(mod_row[k % 2][:, :], banks[b][:, 0:256]).then_inc(bank_free[b], 1)
            walk(act, ada, ada_row)
            root(0)

            def up(seg):
                def step(i, k):
                    if k % 2:
                        return
                    for j in range(2):
                        b = seg.bank(k, j)
                        act.wait_ge(tile_done, seg.tile_no(i, k, j) + 1)
                        if not isinstance(i, int) or i > 0:
                            act.wait_ge(bank_free[seg.bank(k + 1, j)], seg.bank_use(i, k + 1, j) - 1)
                        nc.scalar.activation(ff_a[:, k + j, :], banks[b][:, 0:T], ACT.Silu).then_inc(bank_free[b], 1)
                walk(act, seg, step)
            up(segs["up1"])
            act.wait_ge(S["res_done"], KD)
            square(1)
            root(1)
            act.wait_ge(S["gate_mm"], 1)
            act.wait_ge(S["u_ready"], 1)
            nc.scalar.activation(xg[0:40, :], aux[1][0:40, 0:T], ACT.Identity, bias=gate_sb[:, 2:3], scale=gate_sb[:, 1:2])\
                .then_inc(S["gate_lin"], 1)

            def conv(seg, first, padded, accs, dst):
                def silu(i, k, j):
                    r = (k * seg.tiles + j) % 4
                    c = seg.own(i, k, j)
                    act.wait_ge(S["conv_done"], c + (first + 1))
                    a = accs[:, r, :]
                    nc.scalar.activation(dst[:, bass.ds(c, 1), 0:TP], accs[:, r:r + 1, 0:TP], ACT.Silu)
                    nc.scalar.activation(dst[:, bass.ds(c, 1), TP:].rearrange("p o (b t) -> p (o b) t", t=ST),
                                         convolved_samples(a),
                                         ACT.Silu).then_inc(S["conv_silu"], 1)

                def step(i, k):
                    for j in range(seg.tiles):
                        b = seg.bank(k, j)
                        r = (k * seg.tiles + j) % 4
                        c = seg.own(i, k, j)
                        act.wait_ge(tile_done, seg.tile_no(i, k, j) + 1)
                        if not isinstance(i, int) or 8 * i + 2 * k + j >= 4:
                            act.wait_ge(S["conv_done"], c + (first - 3))
                            act.wait_ge(S["tails_saved"], c + (first - 3))
                        elif k + j == 0:
                            act.wait_ge(S["pad_zero"], 1 if first == 0 else 2)
                        copy(padded[:, r, HIST:HIST + TP], banks[b][:, 0:TP])
                        copy(padded[:, r, HIST + TP:].rearrange("p (b w) -> p b w", w=HIST + ST)[:, :, HIST:],
                             sequences(banks[b][:, TP:T])).then_inc(bank_free[b], 1)
                        if j > 0:
                            silu(i, k, 0)
                        elif k > 0:
                            silu(i, k - 1, 1)
                        elif not isinstance(i, int) or i > 0:
                            silu(i - 1, 3, 1)
                walk(act, seg, step)
                silu(seg.panels // 4 - 1, 3, 1)

            conv(segs["qk"], 0, pad, acc, qk_t)

            act.wait_ge(S["sp_abs"], 1)
            ch.link(nc.scalar.activation(soft_e[:, :], soft_a[:, :], ACT.Exp, scale=-1.0))
            nc.scalar.activation(soft_l[:, :], soft_e[:, :], ACT.Ln, bias=1.0).then_inc(S["sp_exp"], 1)

            vs = segs["v"]

            def v_row(i, k):
                for j in range(2):
                    b = vs.bank(k, j)
                    r = (2 * k + j) % 4
                    act.wait_ge(tile_done, vs.tile_no(i, k, j) + 1)
                    if not isinstance(i, int) or 8 * i + 2 * k + j >= 4:
                        act.wait_ge(S["v_turned"], vs.own(i, k, j) - 3)
                    copy(v_tmp[:, r, :], banks[b][:, 0:T]).then_inc(bank_free[b], 1)
            act.wait_ge(S["conv_silu"], 16)
            walk(act, vs, v_row)

            def copy_tails(first_round, rounds):
                for n in range(first_round, first_round + rounds):
                    x = aux[3 if n < 4 else n % 2]
                    act.wait_ge(S["tail_tr"], n + 1)
                    if n >= 2:
                        act.wait_ge(tail_sent[n % 2], 32 * (n // 2))
                    copy(tail_out[0:27, n % 2, :], x[0:27, :]).then_inc(S["tail_cp"], 1)
            copy_tails(0, 4)

            act.wait_ge(S["mt_ready"], 1)
            for h in range(MH):
                for c, (lo, hi, n) in enumerate(((0, 128, 128), (128, 384, 128), (384, 448, 64))):
                    ch.inc(nc.scalar.activation(dm[0:n, h, lo:hi], dm[0:n, h, lo:hi], ACT.Exp, bias=sm[0:n, 5, 12 + 4 * c + h:13 + 4 * c + h]))
            ch.inc(nc.scalar.activation(sm[:, 5, 24:36], sm[:, 5, 0:12], ACT.Exp))
            nc.scalar.activation(sm[:, 6, 16:28], sm[:, 5, 12:24], ACT.Exp).then_inc(S["wtok_ready"], 1)
            act.wait_ge(S["ws_arg"], 1)
            ch.inc(nc.scalar.activation(sm[:, 10, 0:12], sm[:, 10, 0:12], ACT.Exp))
            nc.scalar.activation(dec[:, :], dec[:, :], ACT.Exp).then_inc(S["ws_exp"], 1)
            for r in range(2):
                act.wait_ge(tail_sent[r], 64)
            for h in range(MH):
                act.wait_ge(S["st_mm"], h + 1)
                ch.inc(copy(st_s[:, h, 0:384], aux[h][:, 0:384]))
                copy(st_s[0:64, h, 384:448], aux[h][0:64, 384:448]).then_inc(S["st_copied"], 1)
            act.wait_ge(S["n_tr"], 1)
            ch.inc(copy(n_rows2[0:8, 0:512], banks[1][0:8, :]))
            ch.inc(copy(n_rows2[0:8, 512:1024], banks[2][0:8, :]))
            copy(n_rows2[0:8, 1024:1152], banks[3][0:8, 0:128]).then_inc(S["n_row"], 2)
            for h in range(MH):
                for d in range(2):
                    n = 2 * h + d
                    act.wait_ge(S["pc_mm"], n + 1)
                    act.wait_ge(state_out[h], 16 * SB)
                    copy(cb[:, h, d * DV:(d + 1) * DV], banks[n % 4][:, :]).then_inc(S["pc_copied"], 1)
            for h in range(MH):
                nm = (num, num2)[h % 2]
                act.wait_ge(S["num_mm"], h + 1)
                if h >= 2:
                    act.wait_ge(S["hn_turned"], 4 * (h - 1))
                if h >= 1:
                    act.wait_ge(S["num_whole"], h)
                ch.inc(copy(nm[:, 0, :], banks[0][:, :]))
                ch.inc(copy(nm[:, 1, :], banks[1][:, :]))
                copy(t1[0:64, :], aux[h][64:128, :], scale=sm[0:64, 5, 32 + h:33 + h]).then_inc(S["t1_ready"], 1)
                act.wait_ge(S["var_ready"], h + 1)
                nc.scalar.activation(coef[:, :, 0], coef[:, :, 0], ACT.Sqrt).then_inc(S["std_ready"], 1)
                act.wait_ge(S["norm_coef"], h + 1)
                for c, n in enumerate((128, 128, 64)):
                    ins = nc.scalar.activation(nm[0:n, c, :], nm[0:n, c, :], ACT.Identity, bias=coef[0:n, c, 1:2], scale=coef[0:n, c, 0:1])
                    if c < 2:
                        ch.inc(ins)
                ins.then_inc(S["hn_ready"], 1)

            def gate(seg, func, count0, dst=None):
                def step(i, k):
                    for j in range(seg.tiles):
                        b = seg.bank(k, j)
                        r = (k * seg.tiles + j) % 4
                        act.wait_ge(tile_done, seg.tile_no(i, k, j) + 1)
                        if dst is None:
                            if not isinstance(i, int) or 8 * i + 2 * k + j >= 4 or count0:
                                act.wait_ge(S["gate_used"], seg.own(i, k, j) + (count0 - 3))
                            o = gate_tmp[:, r:r + 1, :]
                        else:
                            o = dst[:, bass.ds(seg.own(i, k, j), 1), :]
                        nc.scalar.activation(o, banks[b][:, None, 0:T], func).then_inc(bank_free[b], 1)
                walk(act, seg, step)
            gate(segs["mo"], ACT.Sigmoid, 0)

            def pa_row(i, k):
                b = segs["pa"].bank(k)
                act.wait_ge(tile_done, segs["pa"].tile_no(i, k) + 1)
                copy(ya[:, bass.ds(segs["pa"].own(i, k), 1), :], banks[b][:, None, 0:T]).then_inc(bank_free[b], 1)
            for h in range(MH):
                act.wait_ge(state_out[h], 16 * (SB + 1))
            walk(act, segs["pa"], pa_row)
            conv(segs["xbc"], 16, pad2, acc2, xbc_t)
            copy_tails(4, 6)

            for c in range(3):
                n = 128 if c < 2 else 64
                act.wait_ge(S["bt_mm"], c + 1)
                copy(bt[0:n, c, :], aux[c][0:n, :]).then_inc(S["bt_read"], 1)
            act.wait_ge(S["lastx_read"], 1)
            ch.inc(nc.scalar.activation(sp2[:, :, :], sp2[:, :, :], ACT.Exp))
            nc.scalar.activation(sm[:, 8, 0:32], cum[:, 2, 4:36], ACT.Exp).then_inc(S["decx_ready"], 1)
            for q in range(8):
                act.wait_ge(S["t_ready"], 4 * (q + 1))
                w = w_int[:, q % 2, :].rearrange("p (j s) -> p j s", s=448)
                ch.inc(nc.scalar.activation(w[:, :, 0:384], w[:, :, 0:384], ACT.Exp))
                nc.scalar.activation(w[0:64, :, 384:448], w[0:64, :, 384:448], ACT.Exp).then_inc(S["w_exp"], 1)
            for gr in range(SG):
                act.wait_ge(S["ph_mm"], gr + 1)
                copy(h_t[:, gr * 512:(gr + 1) * 512], banks[gr][:, :]).then_inc(S["ph_copied"], 1)
            act.wait_ge(row_sent, 16)

            def turned_state(i, r, first):
                b = i * 2 + r
                for gr in range(SG):
                    act.wait_ge(S["ht_mm"], b * 4 + (gr + 1))
                    if gr == 0 and not first:
                        act.wait_ge(S["yi_mm"], b)
                    copy(h_t[:, gr * 512:(gr + 1) * 512], aux[gr % 2][:, :]).then_inc(S["ht_read"], 1)
            turned_state(0, 0, True)
            turned_state(0, 1, False)
            with act.Fori(1, SB // 2) as i:
                turned_state(i, 0, False)
                turned_state(i, 1, False)
            gate(segs["z"], ACT.Silu, 16)
            for gr in range(SG):
                act.wait_ge(S["gate_used"], 32)
                if gr == 0:
                    for r in range(2):
                        act.wait_ge(state_out[r], 16 * (SB + 1) + 16 * (SB // 2))
                if gr >= 2:
                    act.wait_ge(S["gss_done"], gr - 1)
                nc.scalar.activation(gsq[:, gr % 2, :], xbc_t[:, 4 * gr:4 * gr + 4, :].rearrange("p a b -> p (a b)"), ACT.Square)\
                    .then_inc(S["gsq_ready"], 1)
            for gr in range(SG):
                act.wait_ge(S["gss_done"], gr + 1)
                nc.scalar.activation(g_root[:, gr, :], aux[gr][:, 0:T], ACT.Sqrt, bias=eps_col[:, 0:1], scale=1.0 / 512).then_inc(S["grs_ready"], 1)
            gate(segs["ga"], ACT.Sigmoid, 32)
            gate(segs["gb"], ACT.Sigmoid, 40, merged_g)
            act.wait_ge(S["res_done"], 2 * KD)
            square(2)
            root(2)
            up(segs["up2"])
            act.wait_ge(S["res_done"], 3 * KD)
            square(3)
            root(3)
            for n in range(6):
                c, half = divmod(n, 2)
                rows = 128 if c < 2 else 64
                act.wait_ge(S["fin_tr"], n + 1)
                copy(y_rows[0:rows, c, half * 512:(half + 1) * 512], aux[1 + n % 2][0:rows, :]).then_inc(S["fin_cp"], 1)

        @block.vector
        def _(dve):
            ch = Chain(dve, S["dve_chain"])
            V = nc.vector
            ch.inc(V.memset(eps_col[:, :], EPS))
            dve.wait_ge(S["params_in"], 26 * 16)
            ch.inc(V.memset(gate_sb[:, 1:2], 1.0))
            ch.settle()
            ch.link(V.memset(gate_sb[0:8, 1:2], -1.0))
            ch.link(V.tensor_tensor(gate_sb[:, 2:3], gate_sb[:, 0:1], gate_sb[:, 1:2], ALU.mult))
            dve.wait_ge(S["packs_read"], 1)

            ada = segs["ada"]

            def mod_read(i, k):
                p, r = ada.own(i, k), k % 2
                dve.wait_ge(S["mod_turned"], p + 1)
                V.tensor_tensor(mod[:, bass.ds(p * 2, 2), :], aux[r][:, 0:2 * NSEQ].rearrange("p (j s) -> p j s", s=NSEQ),
                                bias_of(p), ALU.add).then_inc(S["mod_read"], 1)

            def bias_of(p):
                return par[:, None, bass.ds(p * 2, 2)].rearrange("p o c -> p c o").to_broadcast([128, 2, NSEQ])
            walk(dve, ada, mod_read)
            dve.wait_ge(S["mod_read"], ada.panels)

            def mod_of(q):
                return mod[:, q * KD:(q + 1) * KD, :]

            def per_token(ap):
                return ap[:, :, 1:NSEQ].unsqueeze(3).to_broadcast([128, KD, SB, ST])

            def samples(ap):
                return ap[:, :, TP:T].rearrange("p k (b t) -> p k b t", t=ST)

            def modulated(n, shift, scale, norm_col):
                g = par[:, norm_col:norm_col + KD].unsqueeze(2).to_broadcast([128, KD, NSEQ])
                ch.link(V.scalar_tensor_tensor(out=gain[:, :, :], in0=mod_of(scale), scalar=1.0, in1=g, op0=ALU.add, op1=ALU.mult))
                dve.wait_ge(S["root_ready"], n + 1)
                ch.link(V.reciprocal(rs[:, :], rs[:, :]))
                ch.link(V.tensor_tensor(u_t[:, :, :], x_t[:, :, :], rs[:, None, :].to_broadcast([128, KD, T]), ALU.mult))
                for kc in range(KD):
                    ch.inc(V.tensor_scalar(u_t[:, kc, 0:TP], u_t[:, kc, 0:TP], gain[:, kc, 0:1], mod_of(shift)[:, kc, 0:1], ALU.mult, ALU.add))
                ch.link(V.tensor_tensor(samples(u_t), samples(u_t), per_token(gain), ALU.mult))
                V.tensor_tensor(samples(u_t), samples(u_t), per_token(mod_of(shift)), ALU.add).then_inc(S["u_ready"], 1)
                dve.wait_ge(S["u_ready"], n + 1)

            def up(seg):
                def step(i, k):
                    if k % 2 == 0:
                        return
                    for j in range(2):
                        b = seg.bank(k, j)
                        dve.wait_ge(bank_free[seg.bank(k - 1, j)], seg.bank_use(i, k - 1, j) + 1)
                        dve.wait_ge(tile_done, seg.tile_no(i, k, j) + 1)
                        V.tensor_tensor(ff_h[:, bass.ds(i * 4 + (k - 1 + j), 1), :], banks[b][:, None, 0:T], ff_a[:, k - 1 + j:k + j, :], ALU.mult)\
                            .then_inc(bank_free[b], 1)
                walk(dve, seg, step)

            def residual(seg, gate_mod, factor, count0):
                ch.link(V.tensor_scalar(half_g[:, :, :], mod_of(gate_mod), factor, None, ALU.mult))

                def step(i, k):
                    for j in range(seg.tiles):
                        b = seg.bank(k, j)
                        r = (k * seg.tiles + j) % 4
                        kc = seg.own(i, k, j)
                        dve.wait_ge(tile_done, seg.tile_no(i, k, j) + 1)
                        x1 = x_t[:, bass.ds(kc, 1), 0:TP]
                        ch.inc(V.scalar_tensor_tensor(out=x1, in0=banks[b][:, None, 0:TP], scalar=half_g[:, bass.ds(kc, 1), 0:1].rearrange("p a b -> p (a b)"),
                                                      in1=x1, op0=ALU.mult, op1=ALU.add))
                        V.tensor_tensor(sequences(res_tmp[:, r, :]), sequences(banks[b][:, TP:T]),
                                        half_g[:, bass.ds(kc, 1), 1:NSEQ].rearrange("p o b -> p (o b)").unsqueeze(2).to_broadcast([128, SB, ST]),
                                        ALU.mult).then_inc(bank_free[b], 1)
                        dve.wait_ge(bank_free[b], seg.bank_use(i, k, j) + 1)
                        x2 = x_t[:, bass.ds(kc, 1), TP:T]
                        V.tensor_tensor(x2, x2, res_tmp[:, r:r + 1, :], ALU.add).then_inc(S["res_done"], 1)
                        dve.wait_ge(S["res_done"], kc + (count0 + 1))
                walk(dve, seg, step, ch, seg.tiles)

            modulated(0, 0, 1, 72)
            up(segs["up1"])
            residual(segs["down1"], 2, 0.5, 0)
            modulated(1, 3, 4, 80)

            def conv(seg, first, padded, accs, b_col, w_col, tiles):
                def step(i, k):
                    for j in range(seg.tiles):
                        r = (k * seg.tiles + j) % 4
                        c = seg.own(i, k, j)
                        dve.wait_ge(bank_free[seg.bank(k, j)], seg.bank_use(i, k, j) + 1)
                        dve.wait_ge(S["hist_put"], c + (first + 1))
                        if not isinstance(i, int) or 8 * i + 2 * k + j >= 4:
                            dve.wait_ge(S["conv_silu"], c + (first - 3))
                        a, p = accs[:, r, 0:CONVW], padded[:, r, :]
                        ch.link(V.tensor_scalar(a, p[:, 0:CONVW], par[:, bass.ds(c + w_col, 1)], par[:, bass.ds(c + b_col, 1)], ALU.mult, ALU.add))
                        for tap in (1, 2):
                            ch.link(V.scalar_tensor_tensor(out=a, in0=p[:, tap:tap + CONVW], scalar=par[:, bass.ds(c + (w_col + tap * tiles), 1)],
                                                           in1=a, op0=ALU.mult, op1=ALU.add))
                        V.scalar_tensor_tensor(out=a, in0=p[:, 3:3 + CONVW], scalar=par[:, bass.ds(c + (w_col + 3 * tiles), 1)],
                                               in1=a, op0=ALU.mult, op1=ALU.add).then_inc(S["conv_done"], 1)
                walk(dve, seg, step, ch, 3 * seg.tiles)
            conv(segs["qk"], 0, pad, acc, 104, 120, 16)

            dve.wait_ge(S["gate_tr"], 1)
            ch.inc(V.tensor_copy(g3[:, 0:2, :], aux[2][:, 0:80].rearrange("p (c g) -> p c g", g=40)))
            ch.link(V.tensor_copy(g3[0:64, 2, :], aux[2][0:64, 80:120]))
            gx = g3[:, :, 4:40]

            def f3(t):
                return t[:, :].rearrange("p (c g) -> p c g", g=36)
            ch.inc(V.tensor_scalar(sp[:, :, :], gx, 0.0, None, ALU.max))
            V.scalar_tensor_tensor(out=f3(soft_a), in0=gx, scalar=-1.0, in1=gx, op0=ALU.mult, op1=ALU.max).then_inc(S["sp_abs"], 1)

            vs = segs["v"]

            def v_read(i, k):
                for j in range(2):
                    r = (2 * k + j) % 4
                    x = aux[r % 2]
                    c = vs.own(i, k, j)
                    dve.wait_ge(S["v_turned"], c + 1)
                    ch.inc(V.tensor_copy(v_tok[:, 0:2, bass.ds(c * 128, 128)], x[:, 0:256].rearrange("p (c n) -> p c n", n=128)))
                    V.tensor_copy(v_tok[0:64, 2:3, bass.ds(c * 128, 128)], x[0:64, None, 256:384]).then_inc(S["v_copied"], 1)
            walk(dve, vs, v_read, ch, 2)

            dve.wait_ge(S["sp_exp"], 1)
            ch.link(V.tensor_scalar(soft_a[:, :], soft_e[:, :], 1.0, None, ALU.add))
            ch.inc(V.reciprocal(soft_r[:, :], soft_a[:, :]))
            ch.link(V.scalar_tensor_tensor(out=soft_e[:, :], in0=soft_a[:, :], scalar=-1.0, in1=soft_e[:, :], op0=ALU.add, op1=ALU.subtract))
            ch.link(V.scalar_tensor_tensor(out=soft_e[:, :], in0=soft_e[:, :], scalar=-1.0, in1=soft_r[:, :], op0=ALU.mult, op1=ALU.mult))
            ch.link(V.tensor_tensor(soft_l[:, :], soft_l[:, :], soft_e[:, :], ALU.add))
            ch.link(V.tensor_tensor(sp[:, :, :], sp[:, :, :], f3(soft_l), ALU.add))
            ch.inc(V.tensor_scalar(al[:, :, 0:4], sp[:, :, 0:4], -1.0, None, ALU.mult))
            V.scalar_tensor_tensor(out=al[:, :, 4:36], in0=sp[:, :, 4:36], scalar=-1.0, in1=a_neg[:, None, :].to_broadcast([128, 3, SH]),
                                   op0=ALU.mult, op1=ALU.mult).then_inc(S["al_ready"], 1)
            dve.wait_ge(S["cum_mm"], 1)
            inter = sm[:, 3, 0:12].rearrange("p (c h) -> p c h", h=MH)
            mx = sm[:, 3, 12:24].rearrange("p (c h) -> p c h", h=MH)
            mt = sm[:, 3, 24:36].rearrange("p (c h) -> p c h", h=MH)
            ch.inc(V.tensor_copy(cum[:, :, :], aux[2][:, 0:108].rearrange("p (c g) -> p c g", g=36)))
            ch.link(V.tensor_copy(sm[0:64, 9, 24:28], aux[2][0:64, 108:112]))
            ch.inc(V.tensor_copy(inter[:, 0:2, :], cum[:, 0:2, 0:4]))
            ch.inc(V.tensor_tensor(inter[:, 2, :], cum[:, 2, 0:4], sm[:, 9, 24:28], ALU.add))
            V.scalar_tensor_tensor(out=sm[:, 0:3, 0:4], in0=g3[:, :, 0:4], scalar=-1.0, in1=cum[:, :, 0:4], op0=ALU.mult, op1=ALU.subtract)\
                .then_inc(S["g_ready"], 1)
            for h in range(MH):
                dve.wait_ge(S["gb_mm"], h + 1)
                x = aux[h]
                ch.inc(V.scalar_tensor_tensor(out=dm[:, h, 0:128], in0=x[:, 0:128], scalar=cum[:, 0, h:h + 1], in1=neg_p[:, :], op0=ALU.add, op1=ALU.add))
                ch.inc(V.tensor_scalar(dm[:, h, 128:256], x[:, 0:128], cum[:, 1, h:h + 1], None, ALU.add))
                ch.inc(V.scalar_tensor_tensor(out=dm[:, h, 256:384], in0=x[:, 128:256], scalar=cum[:, 1, h:h + 1], in1=neg_p[:, :], op0=ALU.add, op1=ALU.add))
                ch.inc(V.scalar_tensor_tensor(out=dm[0:64, h, 384:448], in0=x[0:64, 256:320], scalar=cum[0:64, 2, h:h + 1], in1=neg_s[:, :], op0=ALU.add, op1=ALU.add))
            ch.settle()
            ch.inc(V.tensor_reduce(mx[:, 0, :], dm[:, :, 0:128], AX.X, ALU.max))
            ch.inc(V.tensor_reduce(mx[:, 1, :], dm[:, :, 128:384], AX.X, ALU.max))
            ch.link(V.tensor_reduce(mx[0:64, 2, :], dm[0:64, :, 384:448], AX.X, ALU.max))
            ch.link(V.tensor_tensor(mt, inter, mx, ALU.max))
            ch.inc(V.tensor_tensor(sm[:, 5, 0:12], sm[:, 3, 0:12], sm[:, 3, 24:36], ALU.subtract))
            V.tensor_scalar(sm[:, 5, 12:24], sm[:, 3, 24:36], -1.0, None, ALU.mult).then_inc(S["mt_ready"], 1)
            bm = sm[:, 4, 0:24].rearrange("p (c g) -> p c g", g=8)
            ch.inc(V.tensor_copy(bm[:, :, 0:4], cum[:, :, 0:4]))
            ch.link(V.tensor_copy(bm[:, :, 4:8], mt))
            V.tensor_tensor(al2[:, :].rearrange("p (b g) -> p b g", g=8), sm[0:64, 4, 16:24].unsqueeze(1).to_broadcast([64, SB, 8]),
                            last_b[:, :].unsqueeze(2).to_broadcast([64, SB, 8]), ALU.mult).then_inc(S["bmx_ready"], 1)
            dve.wait_ge(S["last_mm"], 1)
            ch.inc(V.tensor_copy(sm[:, 6, 0:8], banks[0][:, 0:8]))
            ch.inc(V.tensor_copy(sm[0:64, 6, 8:16], banks[0][0:64, 8:16]))
            ch.link(V.tensor_copy(lb[:, :, :], banks[0][:, 16:80].rearrange("p (b g) -> p b g", g=8)))
            ch.inc(V.tensor_tensor(sm[:, 9, 28:32], sm[:, 6, 0:4], sm[:, 6, 4:8], ALU.subtract))
            ch.inc(V.tensor_tensor(sm[:, 9, 32:36], sm[:, 6, 8:12], sm[:, 6, 12:16], ALU.subtract))
            ch.inc(V.tensor_copy(sm[:, 11, 0:32].rearrange("p (b h) -> p b h", h=MH), lb[:, :, 4:8]))
            ch.link(V.tensor_tensor(dec[:, :].rearrange("p (b h) -> p b h", h=MH), lb[:, :, 0:4], lb[:, :, 4:8], ALU.subtract))
            ch.inc(V.tensor_tensor(dec[:, :], dec[:, :], m0_b[:, :], ALU.add))
            w3 = sm[:, 10, 0:12].rearrange("p (c h) -> p c h", h=MH)
            ch.inc(V.tensor_tensor(w3[:, 0:2, :], sm[:, 0:2, 0:4], sm[:, 9, 28:32].unsqueeze(1).to_broadcast([128, 2, MH]), ALU.add))
            V.tensor_tensor(w3[:, 2, :], sm[:, 2, 0:4], sm[:, 9, 32:36], ALU.add).then_inc(S["ws_arg"], 1)
            dve.wait_ge(S["wtok_ready"], 1)
            for h in range(MH):
                dve.wait_ge(S["qk_mm"], h + 1)
                for c, (lo, hi, n) in enumerate(((0, 128, 128), (128, 384, 128), (384, 448, 64))):
                    ins = V.scalar_tensor_tensor(out=dm[0:n, h, lo:hi], in0=aux[h][0:n, lo:hi], scalar=DK ** -0.5, in1=dm[0:n, h, lo:hi],
                                                 op0=ALU.mult, op1=ALU.mult, accum_out=sm[0:n, 7, 8 + 4 * c + h:9 + 4 * c + h])
                    if c < 2:
                        ch.inc(ins)
                ins.then_inc(S["s_ready"], 1)
            dve.wait_ge(S["ws_exp"], 1)
            V.tensor_scalar(sm[:, 10, 0:12], sm[:, 10, 0:12], DK ** -0.5, None, ALU.mult).then_inc(S["ws_ready"], 1)
            dve.wait_ge(S["ws_ready"], 1)
            for c in range(8):
                h, b = c // 2, banks[c % 4]
                dve.wait_ge(S["kt_mm"], c + 1)
                for blk, n in ((0, 128), (1, 128), (2, 64)):
                    ins = V.tensor_scalar(kw[0:n, blk, c * 128:(c + 1) * 128], b[0:n, blk * 128:(blk + 1) * 128],
                                          sm[0:n, 10, 4 * blk + h:4 * blk + h + 1], None, ALU.mult)
                    if blk < 2:
                        ch.inc(ins)
                ins.then_inc(S["kt_read"], 1)
            dve.wait_ge(S["st_mm"], MH)
            V.tensor_tensor(acc_q[:, :, :].rearrange("p k (b t) -> p k b t", t=ST),
                            qk_t[:, 0:8, TP:T].rearrange("p k (b t) -> p k b t", t=ST),
                            n_t[:, :, :].unsqueeze(3).to_broadcast([128, 8, SB, ST]), ALU.mult).then_inc(S["qn_prod"], 1)
            dve.wait_ge(S["n_mm"], 1)
            ch.inc(V.tensor_copy(sm[0:64, 7, 20:24], banks[0][0:64, 0:4]))
            ch.inc(V.tensor_copy(sm[:, 7, 0:8], banks[0][:, 80:88]))
            nt4 = n_t[:, :, :].rearrange("p (h d) b -> p h d b", d=2)
            dve.wait_ge(S["qn_prod"], 1)
            ch.link(V.tensor_tensor(nt4, nt4, dec[:, :].rearrange("p (b h) -> p h b", h=MH).unsqueeze(2).to_broadcast([128, MH, 2, SB]), ALU.mult))
            V.tensor_tensor(n_t[:, :, :], n_t[:, :, :], banks[0][:, 8:72].rearrange("p (c b) -> p c b", b=SB), ALU.add).then_inc(S["n_new"], 1)
            ch.link(V.tensor_tensor(sm[0:64, 7, 24:28], sm[0:64, 7, 20:24], sm[0:64, 5, 32:36], ALU.mult))
            ch.link(V.tensor_tensor(sm[0:64, 7, 16:20], sm[0:64, 7, 16:20], sm[0:64, 7, 24:28], ALU.add))
            ch.link(V.scalar_tensor_tensor(out=sm[:, 9, 0:12], in0=sm[:, 7, 8:20], scalar=-1.0, in1=sm[:, 7, 8:20], op0=ALU.mult, op1=ALU.max))
            ch.link(V.tensor_tensor(sm[:, 9, 0:12], sm[:, 9, 0:12], sm[:, 6, 16:28], ALU.max))
            ch.link(V.reciprocal(sm[:, 9, 0:12], sm[:, 9, 0:12]))
            ch.link(V.tensor_tensor(sm[:, 9, 12:24], sm[:, 9, 0:12], sm[:, 9, 0:12], ALU.mult))

            def masks(b, h, first):
                n = b * MH + h
                if not first:
                    dve.wait_ge(S["state_mm"], n - (MH - 1))
                ch.inc(V.tensor_scalar(kwm[0:64, h, :], kw[0:64, 2, h * DK:(h + 1) * DK], seg_m[:, bass.ds(b, 1)], None, ALU.mult))
                V.tensor_tensor(qm[:, h, :, :], qk_t[:, 2 * h:2 * h + 2, TP:T], seg_b[:, bass.ds(b, 1), :].to_broadcast([128, 2, TS]), ALU.mult)\
                    .then_inc(S["masks_ready"], 1)

            def update(b, h):
                n = b * MH + h
                dve.wait_ge(S["state_mm"], n + 1)
                for d in range(2):
                    c_h = cb[:, h, d * DV:(d + 1) * DV]
                    ins = V.scalar_tensor_tensor(out=c_h, in0=c_h, scalar=dec[:, bass.ds(n, 1)], in1=banks[2 * (h % 2) + d][:, :], op0=ALU.mult, op1=ALU.add)
                    if d == 0:
                        ch.inc(ins)
                ins.then_inc(S["c_updated"], 1)
            for h in range(MH):
                masks(0, h, True)
            base = ch.n
            with dve.Fori(0, SB - 1) as b:
                ch.n = base + b * (2 * MH)
                for h in range(MH):
                    update(b, h)
                    masks(b + 1, h, False)
            ch.n = base + (SB - 1) * 2 * MH
            for h in range(MH):
                update(SB - 1, h)

            for h in range(MH):
                nm = (num, num2)[h % 2]
                dve.wait_ge(S["t1_ready"], h + 1)
                ch.link(V.scalar_tensor_tensor(out=t2[0:64, :], in0=aux[h][0:64, :], scalar=sm[0:64, 5, 32 + h:33 + h], in1=t1[0:64, :], op0=ALU.mult, op1=ALU.add))
                V.tensor_tensor(nm[0:64, 2, :], banks[2][0:64, :], t2[0:64, :], ALU.add).then_inc(S["num_whole"], 1)
                dve.wait_ge(S["num_whole"], h + 1)
                for c, n in enumerate((128, 128, 64)):
                    ch.inc(V.bn_stats(stats[0:n, c, :], nm[0:n, c, :]))
                ch.settle()
                for c, n in enumerate((128, 128, 64)):
                    ch.inc(V.bn_aggr(mean_var[0:n, c, :], stats[0:n, c, :]))
                ch.settle()
                rd = sm[:, 9, 0:12].rearrange("p (c h) -> p c h", h=MH)[:, :, h]
                rd2 = sm[:, 9, 12:24].rearrange("p (c h) -> p c h", h=MH)[:, :, h]
                ch.link(V.tensor_tensor(coef[:, :, 0], mean_var[:, :, 1], rd2, ALU.mult))
                V.tensor_scalar(coef[:, :, 0], coef[:, :, 0], EPS, None, ALU.add).then_inc(S["var_ready"], 1)
                dve.wait_ge(S["std_ready"], h + 1)
                ch.link(V.reciprocal(coef[:, :, 0], coef[:, :, 0]))
                ch.link(V.tensor_tensor(coef[:, :, 0], coef[:, :, 0], rd, ALU.mult))
                V.scalar_tensor_tensor(out=coef[:, :, 1], in0=mean_var[:, :, 0], scalar=-1.0, in1=coef[:, :, 0], op0=ALU.mult, op1=ALU.mult)\
                    .then_inc(S["norm_coef"], 1)
                if h == 0:
                    dve.wait_ge(small_out, 64)
                for j in range(4):
                    c = 4 * h + j
                    dve.wait_ge(S["hn_turned"], c + 1)
                    V.tensor_scalar(hm[:, c, :], aux[h][:, 0:T], par[:, 184 + c:185 + c], None, ALU.mult).then_inc(S["hn_read"], 1)

            def gated(seg, dst, count0):
                def step(i, k):
                    for j in range(seg.tiles):
                        b = seg.bank(k, j)
                        r = (k * seg.tiles + j) % 4
                        dve.wait_ge(bank_free[b], seg.bank_use(i, k, j) + 1)
                        c = dst[:, bass.ds(seg.own(i, k, j), 1), :]
                        V.tensor_tensor(c, c, gate_tmp[:, r:r + 1, :], ALU.mult).then_inc(S["gate_used"], 1)
                walk(dve, seg, step)
            dve.wait_ge(S["hn_read"], 16)
            gated(segs["mo"], hm, 0)
            conv(segs["xbc"], 16, pad2, acc2, 216, 240, 24)

            for n in range(12):
                gr, c = divmod(n, 3)
                rows = 128 if c < 2 else 64
                dve.wait_ge(S["xt_mm"], n + 1)
                V.tensor_tensor(xd[0:rows, c, gr * 512:(gr + 1) * 512].rearrange("p (e q) -> p e q", q=64),
                                banks[n % 4][0:rows, :].rearrange("p (e q) -> p e q", q=64),
                                sp[0:rows, c, 4 + 8 * gr:12 + 8 * gr].unsqueeze(2).to_broadcast([rows, 8, 64]), ALU.mult).then_inc(S["xt_read"], 1)
            for gr in range(SG):
                dve.wait_ge(S["cb_mm"], gr + 1)
                ch.inc(V.tensor_tensor(cbm[:, gr, 0:384], banks[gr][:, 0:384], tri[:, :], ALU.mult))
                V.tensor_tensor(cbm[0:64, gr, 384:448], banks[gr][0:64, 384:448], tri_s[:, 0:64], ALU.mult).then_inc(S["cb_read"], 1)
            dve.wait_ge(S["lastx_mm"], 1)
            ch.inc(V.tensor_tensor(sp2[:, 0:2, :], aux[3][:, 0:32].unsqueeze(1).to_broadcast([128, 2, SH]), cum[:, 0:2, 4:36], ALU.subtract))
            ch.inc(V.memset(sp2[64:128, 2, :], 0.0))
            V.tensor_tensor(sp2[0:64, 2, :], aux[3][0:64, 32:64], cum[0:64, 2, 4:36], ALU.subtract).then_inc(S["lastx_read"], 1)
            dve.wait_ge(S["hd_mm"], 1)
            ch.inc(V.tensor_tensor(hd_in[:, 0:128].rearrange("p (t b) -> p t b", b=SB), aux[3][0:32, 64:72].unsqueeze(1).to_broadcast([SH, 16, SB]),
                                   tile_of_head[:, :].unsqueeze(2).to_broadcast([SH, 16, SB]), ALU.mult))
            ch.inc(V.tensor_reduce(parity2[:, :], ident[0:32, 0:32].rearrange("p (t e) -> p e t", e=2), AX.X, ALU.add))
            ch.link(V.tensor_scalar(hd_in[:, 128:144], tile_of_head[:, :], d_col[:, 0:1], None, ALU.mult))
            V.tensor_copy(parity[:, :, :], parity2[:, :].unsqueeze(2).to_broadcast([SH, 2, 64])).then_inc(S["hd_rhs"], 1)
            dve.wait_ge(S["hd_mm2"], 1)
            V.tensor_copy(h_dec[:, :], aux[3][:, 128:272]).then_inc(S["hd_read"], 1)
            dve.wait_ge(S["hd_read"], 1)
            for r in range(2):
                dve.wait_ge(tail_sent[r], 5 * 32)

            def exponents(q):
                w = w_int[:, q % 2, :].rearrange("p (j s) -> p j s", s=448)
                if q >= 2:
                    dve.wait_ge(S["y_mm"], 2 * (q - 1))
                for j in range(4):
                    h = 4 * q + j
                    dve.wait_ge(S["cb_bc"], h + 1)
                    ch.inc(V.tensor_scalar(w[:, j, 0:256], aux[j][:, 0:256], cum[:, 0, 4 + h:5 + h], 0.0, ALU.subtract, ALU.min))
                    ch.inc(V.tensor_scalar(w[:, j, 256:384], aux[j][:, 128:256], cum[:, 1, 4 + h:5 + h], 0.0, ALU.subtract, ALU.min))
                    V.tensor_scalar(w[0:64, j, 384:448], aux[j][0:64, 256:320], cum[0:64, 2, 4 + h:5 + h], 0.0, ALU.subtract, ALU.min).then_inc(S["t_ready"], 1)

            def weights(q):
                w = w_int[:, q % 2, :].rearrange("p (j s) -> p j s", s=448)
                dve.wait_ge(S["w_exp"], q + 1)
                gr = q // 2
                ch.inc(V.tensor_tensor(w[:, :, 0:384], w[:, :, 0:384], cbm[:, gr:gr + 1, 0:384].to_broadcast([128, 4, 384]), ALU.mult))
                V.tensor_tensor(w[0:64, :, 384:448], w[0:64, :, 384:448], cbm[0:64, gr:gr + 1, 384:448].to_broadcast([64, 4, 64]), ALU.mult).then_inc(S["w_ready"], 1)

            def outputs(q):
                for pr in range(2):
                    c = 2 * q + pr
                    dve.wait_ge(S["y_mm"], c + 1)
                    V.scalar_tensor_tensor(out=xbc_t[:, c, :], in0=xbc_t[:, c, :], scalar=h_dec[:, 128 + c:129 + c], in1=banks[c % 4][:, 0:T],
                                           op0=ALU.mult, op1=ALU.add).then_inc(S["y_read"], 1)
            exponents(0)
            for q in range(8):
                if q < 7:
                    exponents(q + 1)
                weights(q)
                outputs(q)
            dve.wait_ge(S["decx_ready"], 1)
            for blk, rows in ((0, 128), (1, 128), (2, 64)):
                v4 = xd[0:rows, blk, :].rearrange("p (e q) -> p e q", q=64)
                ins = V.tensor_tensor(v4, v4, sp2[0:rows, blk, :].unsqueeze(2).to_broadcast([rows, SH, 64]), ALU.mult)
                if blk < 2:
                    ch.inc(ins)
            ins.then_inc(S["xw_ready"], 1)
            dve.wait_ge(S["bt_read"], 3)

            def ssm_masks(i, r, first):
                b = i * 2 + r
                if not first:
                    dve.wait_ge(S["yi_mm"], b - 1)
                ch.inc(V.tensor_scalar(btm[0:64, r, :], bt[0:64, 2, :], seg_m[:, bass.ds(b, 1)], None, ALU.mult))
                V.tensor_tensor(cm[:, r, :].rearrange("p (g t) -> p g t", t=TS), xbc_t[:, 20:24, TP:T], seg_b[:, bass.ds(b, 1), :].to_broadcast([128, SG, TS]), ALU.mult)\
                    .then_inc(S["hmask_ready"], 1)

            def ssm_update(i, r):
                b = i * 2 + r
                up_banks = (aux[2], aux[3], banks[2], banks[3])
                hd3 = h_dec[:, 0:128].rearrange("p (t b) -> p t b", b=SB)
                for gr in range(SG):
                    dve.wait_ge(S["up_mm"], b * 4 + (gr + 1))
                    for j in range(4):
                        c = 4 * gr + j
                        hh = hb[:, r, c * SN:(c + 1) * SN]
                        ins = V.scalar_tensor_tensor(out=hh, in0=hh, scalar=hd3[:, c, bass.ds(b, 1)], in1=up_banks[gr][:, j * 128:(j + 1) * 128], op0=ALU.mult, op1=ALU.add)
                        if j < 3:
                            ch.inc(ins)
                    ins.then_inc(S["up_done"], 1)
            ssm_masks(0, 0, True)
            ssm_masks(0, 1, True)
            base = ch.n
            with dve.Fori(0, SB // 2 - 1) as i:
                ch.n = base + i * 26
                for r in range(2):
                    ssm_update(i, r)
                    ssm_masks(i + 1, r, False)
            ch.n = base + (SB // 2 - 1) * 26
            for r in range(2):
                ssm_update(SB // 2 - 1, r)
            dve.wait_ge(S["yi_mm"], SB)
            for q in range(2):
                for half in range(2):
                    gr = 2 * q + half
                    o = slice(64 * half, 64 * half + 64)
                    ins = V.tensor_tensor(y_int[o, q, :].rearrange("p (e q) -> p e q", q=64), banks[q][o, :].rearrange("p (e q) -> p e q", q=64),
                                          sm[o, 8, 8 * gr:8 * gr + 8].unsqueeze(2).to_broadcast([64, 8, 64]), ALU.mult)
                    if half == 0:
                        ch.inc(ins)
                ins.then_inc(S["yi_read"], 1)
            for gr in range(SG):
                dve.wait_ge(S["yi_tr"], gr + 1)
                y4 = xbc_t[:, 4 * gr:4 * gr + 4, TP:T]
                V.tensor_tensor(y4, y4, aux[gr][:, 0:4 * TS].rearrange("p (c t) -> p c t", t=TS), ALU.add).then_inc(S["yi_add"], 1)
            dve.wait_ge(S["yi_add"], SG)
            gated(segs["z"], xbc_t, 16)
            for gr in range(SG):
                dve.wait_ge(S["grs_ready"], gr + 1)
                ch.link(V.reciprocal(g_root[:, gr, :], g_root[:, gr, :]))
                for j in range(4):
                    c = 4 * gr + j
                    V.scalar_tensor_tensor(out=xbc_t[:, c, :], in0=xbc_t[:, c, :], scalar=par[:, 200 + c:201 + c], in1=g_root[:, gr, :], op0=ALU.mult, op1=ALU.mult)\
                        .then_inc(S["gnorm_done"], 1)
            gated(segs["ga"], ya, 32)

            def merge(i, k):
                seg = segs["pb"]
                b, r = seg.bank(k), k % 4
                c = seg.own(i, k)
                dve.wait_ge(tile_done, seg.tile_no(i, k) + 1)
                g1 = merged_g[:, bass.ds(c, 1), :]
                V.tensor_tensor(g1, g1, banks[b][:, None, 0:T], ALU.mult).then_inc(bank_free[b], 1)
                dve.wait_ge(bank_free[b], seg.bank_use(i, k) + 1)
                y1 = ya[:, bass.ds(c, 1), :]
                V.tensor_tensor(y1, y1, g1, ALU.add).then_inc(S["merged"], 1)
            gb = segs["gb"]
            for b in range(4):
                dve.wait_ge(bank_free[b], (gb.t0 + gb.panels * gb.tiles) // 4)
            dve.wait_ge(S["gate_used"], 40)
            walk(dve, segs["pb"], merge)
            residual(segs["out"], 5, 1.0, KD)
            modulated(2, 6, 7, 88)
            up(segs["up2"])
            residual(segs["down2"], 8, 0.5, 2 * KD)
            dve.wait_ge(S["root_ready"], 4)
            ch.link(V.reciprocal(rs[:, :], rs[:, :]))
            for kc in range(KD):
                ins = V.scalar_tensor_tensor(out=u_t[:, kc, :], in0=x_t[:, kc, :], scalar=par[:, 96 + kc:97 + kc], in1=rs[:, :], op0=ALU.mult, op1=ALU.mult)
                if kc < KD - 1:
                    ch.inc(ins)
            ins.then_inc(S["fin_ready"], 1)


_OUTS = {
    "y_p": (1, TP, D), "y_s": (SB, ST, D),
    "p_C": (1, 1, MH, DK, DV), "p_n": (1, 1, MH, DK), "p_m": (1, 1, MH), "p_mconv": (1, 1, 3, XCH), "p_ssm": (1, 1, SH, 64, SN), "p_sconv": (1, 1, 3, SCH),
    "s_C": (1, SB, MH, DK, DV), "s_n": (1, SB, MH, DK), "s_m": (1, SB, MH), "s_mconv": (1, SB, 3, XCH), "s_ssm": (1, SB, SH, 64, SN), "s_sconv": (1, SB, 3, SCH),
}


def kernel(**inputs):
    import numpy as np
    import concourse.bacc as bacc
    from concourse.bass_utils import run_bass_kernel_spmd

    nc = bacc.Bacc("TRN2", target_bir_lowering=False, num_devices=1)
    arrays, io, out = {}, {}, {}
    for name, a in inputs.items():
        a = np.ascontiguousarray(a)
        arrays[f"in_{name}"] = a
        io[name] = nc.dram_tensor(f"in_{name}", a.shape, mybir.dt.from_np(a.dtype), kind="ExternalInput").ap()
    for name, shape in _OUTS.items():
        out[name] = nc.dram_tensor(f"out_{name}", shape, FP32, kind="ExternalOutput").ap()
    build(nc, io, out)
    r = run_bass_kernel_spmd(nc, [arrays], core_ids=[0])
    return tuple(r.results[0][f"out_{name}"] for name in _OUTS)
```

```python
import concourse.bass as bass
from concourse import mybir
from contextlib import ExitStack

FP32 = mybir.dt.float32
F32R = mybir.dt.float32r
ACT = mybir.ActivationFunctionType
ALU = mybir.AluOpType
AX = mybir.AxisListType

D = 1024
TP, SB, ST = 256, 8, 8
TS = SB * ST
T = TP + TS
KD = D // 128
DFF = 2816
KF = DFF // 128
NSEQ = 1 + SB
NMOD = 9
MH, DV, DK = 4, 512, 256
SH, SG, SN = 32, 4, 128
XCH = 2048
SCH = 3072
EPS = 1e-6
NEG = -1e30
HIST = 3
PADW = HIST + TP + SB * (HIST + ST)
CONVW = PADW - HIST
SLOTS = 4
LAG = 2
ARENA = 24096
IN_OFF = {"q": 0, "k": 1024, "v": 2048, "mo": 4096, "if": 6144, "z": 6152, "xbc": 8200, "dt": 11272, "ga": 11304, "gb": 12328}


class Segment:

    def __init__(self, name, tiles, parts, kc, per_panel, gu, split, panel, unit, split_unit, tile):
        self.name, self.parts, self.kc, self.per_panel, self.gu, self.split = name, parts, kc, per_panel, gu, split
        self.g0, self.u0, self.s0, self.t0 = panel, unit, split_unit, tile
        self.tiles, self.units = tiles, tiles * parts
        self.panels, self.gp, self.gt = self.units // per_panel, gu // per_panel, gu // parts
        self.width, self.chunks = (256, kc) if parts == 1 else (128, kc * per_panel)

    def at(self, n):
        return divmod(n, self.gu)

    def slot(self, q):
        return (self.g0 + q // self.per_panel) % SLOTS

    def arrivals(self, i, q):
        return i * (16 * self.gp // SLOTS) + 16 * ((self.g0 + q // self.per_panel) // SLOTS + 1)

    def unit(self, i, q):
        return i * self.gu + (self.u0 + q)

    def split_no(self, i, q):
        return i * self.gu + (self.s0 + q)

    def bank(self, q):
        return (self.t0 + q // self.parts) % 4

    def bank_use(self, i, q):
        return i * (self.gt // 4) + (self.t0 + q // self.parts) // 4

    def own(self, i, q):
        return i * self.gt + q // self.parts


def walk(eng, seg, late, now=None, chain=None, per=0, lag=0):
    base = chain.n if chain else 0

    def step(i, q):
        if now:
            now(i, q)
        if isinstance(i, int) and i * seg.gu + q < lag:
            return
        if chain:
            chain.n = base + (i * (seg.gu * per) + (q - lag) * per)
        late(i + (q - lag) // seg.gu, (q - lag) % seg.gu)

    def group(i, units):
        for q in range(units):
            step(i, q)

    groups, rest = divmod(seg.units, seg.gu)
    if rest == 0:
        groups, rest = groups - 1, seg.gu
    if groups > 0:
        group(0, seg.gu)
    if groups > 1:
        with eng.Fori(1, groups) as i:
            group(i, seg.gu)
    group(groups, rest)
    for n in range(seg.units - lag, seg.units):
        if chain:
            chain.n = base + n * per
        late(*seg.at(n))
    if chain:
        chain.n = base + seg.units * per


class Chain:

    def __init__(self, eng, sem):
        self.eng, self.sem, self.n = eng, sem, 0

    def link(self, ins):
        self.inc(ins)
        self.settle()

    def inc(self, ins):
        ins.then_inc(self.sem, 1)
        self.n = self.n + 1

    def settle(self):
        self.eng.wait_ge(self.sem, self.n)


def build(nc, io, out):
    segs, panel, unit, split_unit, tile = {}, 0, 0, 0, 0
    panel_free, split_units = [], []
    for name, *shape in (
        ("ada", NMOD * D // 256, 1, KD, 1, 4, False), ("up1", 2 * KF, 1, KD, 2, 8, True), ("down1", KD, 2, KF // 2, 1, 8, True),
        ("qk", 16, 1, KD, 2, 8, True), ("v", 16, 1, KD, 2, 8, True), ("mo", 16, 1, KD, 2, 8, True), ("pa", KD, 2, 8, 2, 8, True),
        ("xbc", 24, 1, KD, 2, 8, True), ("z", 16, 1, KD, 2, 8, True), ("ga", KD, 1, KD, 2, 8, True), ("gb", KD, 1, KD, 2, 8, True),
        ("pb", KD, 2, 8, 2, 8, True), ("out", KD, 1, KD, 2, 8, True), ("up2", 2 * KF, 1, KD, 2, 8, True),
        ("down2", KD, 2, KF // 2, 1, 8, True),
    ):
        seg = segs[name] = Segment(name, *shape, panel, unit, split_unit, tile)
        for p in range(seg.panels):
            n = (p + 1) * seg.per_panel
            panel_free.append((seg.split, (split_unit if seg.split else unit) + n))
        if seg.split:
            split_units += range(unit, unit + seg.units)
        panel, unit, tile = panel + seg.panels, unit + seg.units, tile + seg.tiles
        split_unit += seg.units if seg.split else 0

    ctx = ExitStack()
    with ctx:
        def sb(name, shape, dtype=FP32):
            return ctx.enter_context(nc.sbuf_tensor(name, shape, dtype))

        def sem(name):
            return ctx.enter_context(nc.semaphore(name))

        ident = sb("ident", [128, 128])
        ones = sb("ones", [128, 128])
        tri = sb("tri", [128, 384])
        tri_s = sb("tri_s", [64, 128])
        neg_p = sb("neg_p", [128, 128])
        neg_s = sb("neg_s", [64, 64])
        seg_m = sb("seg_m", [64, SB])
        seg_b = sb("seg_b", [128, SB, TS])
        seg_t = sb("seg_t", [SB, TS])
        row_last = sb("row_last", [128, 128])
        last_s = sb("last_s", [64, 64])
        last_b = sb("last_b", [64, SB])
        mod_sum = sb("mod_sum", [128, NSEQ])
        tile_of_head = sb("tile_of_head", [SH, 16])
        parity = sb("parity", [SH, 2, 64])
        parity2 = sb("parity2", [SH, 2])
        par = sb("par", [128, 336])
        mod = sb("mod", [128, NMOD * KD, NSEQ])
        gain = sb("gain", [128, KD, NSEQ])
        half_g = sb("half_g", [128, KD, NSEQ])
        a_neg = sb("a_neg", [128, SH])
        m0_b = sb("m0_b", [128, SB * MH])
        m0_r = sb("m0_r", [SB, MH])
        gate_w = sb("gate_w", [128, KD, 40])
        gate_sb = sb("gate_sb", [40, 4])
        eps_col = sb("eps_col", [128, 1])
        sp2 = sb("sp2", [128, 3, SH])
        d_col = sb("d_col", [SH, 1])
        x_t = sb("x_t", [128, KD, T])
        u_hi, u_lo = (sb(n, [128, KD, T], F32R) for n in ("u_hi", "u_lo"))
        w_hi = [sb(f"w_hi{r}", [128, KF // 2, 128], F32R) for r in range(2)]
        w_lo = [sb(f"w_lo{r}", [128, KF // 2, 128], F32R) for r in range(2)]
        rs = sb("rs", [128, T])
        ring = [sb(f"ring{s}", [128, 2048]) for s in range(SLOTS)]
        res_tmp = sb("res_tmp", [128, 4, TS])
        hist = sb("hist", [128, 40, SB * HIST])
        tails = sb("tails", [128, 40, HIST * (1 + SB)])
        g3 = sb("g3", [128, 3, 40])
        sp = sb("sp", [128, 3, 36])
        al = sb("al", [128, 3, 36])
        cum = sb("cum", [128, 3, 36])
        sm = sb("sm", [128, 12, 36])
        al2 = sb("al2", [64, SB * 2 * MH])
        lb = sb("lb", [128, SB, 2 * MH])
        dec = sb("dec", [128, SB * MH])
        stats = sb("stats", [128, 3, 6])
        mean_var = sb("mean_var", [128, 3, 2])
        coef = sb("coef", [128, 3, 2])
        hd_in = sb("hd_in", [SH, 16 * (SB + 1)])
        h_dec = sb("h_dec", [128, 16 * (SB + 1)])
        n_t = sb("n_t", [128, 8, SB])

        with nc.sbuf_tensor("arena", [128, ARENA], FP32) as arena:
            pass

        def over(name, off, tiles):
            with nc.sbuf_tensor(name + "_below", [128, max(off, 1)], FP32), nc.sbuf_tensor(name, [128, tiles, T], F32R) as at_off:
                pass
            with nc.sbuf_tensor(name + "_first", [128, tiles, T], F32R) as at_start:
                pass
            return at_off if off else at_start
        used = [0]

        def part(off, *shape):
            n = 1
            for s in shape:
                n *= s
            used[0] = max(used[0], off + n)
            assert off + n <= ARENA, off + n
            v = arena[:, off:off + n]
            if len(shape) == 2:
                v = v.rearrange("p (a b) -> p a b", b=shape[1])
            if len(shape) == 3:
                v = v.rearrange("p (a b c) -> p a b c", b=shape[1], c=shape[2])
            return v

        ff_hi, ff_lo = over("ff_hi", 4960, KF), over("ff_lo", 4960 + KF * T, KF)
        y_hi, y_lo = over("y_hi", 7680, 16), over("y_lo", 7680 + 16 * T, 16)
        m_hi, m_lo = over("m_hi", 0, KD), over("m_lo", KD * T, KD)
        sb("arena_kept", [128, ARENA])

        pk = part(0, 3, 128)
        x_rows = part(384, 3, D)
        mh_rows = part(3456, 2048)
        sh_rows = part(5504, 3072)
        c_rows = part(8576, D)
        n_rows = part(9600, D)
        c_t = part(22880, KD, 32)
        mod_row = [part(23136 + 256 * r, 256) for r in range(2)]
        sq = part(20320, KD, T)
        u_t = part(20320, KD, T)
        ff_a = part(19040, 4, T)
        qk_t = part(0, 16, T)
        v_tok = part(5120, 3, 2048)
        hm = part(17920, 16, T)
        kw = part(16384, 3, 1024)
        pad = part(19456, 4, PADW)
        acc = part(20844, 4, PADW)
        dm = part(14304, MH, 448)
        v_tmp = part(14304, 4, T)
        cb = part(20000, MH, 2 * DV)
        soft_a, soft_e, soft_l, soft_r = (part(16100 + 108 * r, 108) for r in range(4))
        st_s = dm
        kwm = part(12952, MH, DK)
        num = part(0, 3, DV)
        num2 = part(1536, 3, DV)
        t1 = part(3072, DV)
        t2 = part(3584, DV)
        qm = part(11264, MH, 2, TS)
        xg = part(13976, T)
        ya = part(21536, KD, T)
        xbc_t = part(0, 24, T)
        pad2 = part(7680, 4, PADW)
        acc2 = part(9068, 4, PADW)
        xd = part(9984, 3, XCH)
        bt = part(16128, 3, 512)
        cbm = part(7680, SG, 448)
        w_int = part(17664, 2, 4 * 448)
        hb = part(9984, 2, 2048)
        h_t = part(17664, 2048)
        y_int = part(19712, 2, 512)
        btm = part(19712, 2, 512)
        cm = part(9472, 2, SG * TS)
        gate_tmp_m = part(4100, 4, T)
        gate_tmp = part(5120, 4, T)
        g_root = part(6400, SG, T)
        gsq = part(18124, 2, 4 * T)
        acc_q = part(19456, 8, TS)
        n_rows2 = part(11800, 1152)
        y_rows = part(0, 3, D)
        merged_g = part(18124, KD, T)
        tail_out = [part(17664, 2, 512), part(11800, 2, 512)]

        banks = [ctx.enter_context(nc.psum_tensor(f"bank{b}", [128, 512], FP32)) for b in range(4)]
        aux4 = ctx.enter_context(nc.psum_tensor("aux4", [128, 4, 512], FP32))
        aux = [aux4[:, b, :] for b in range(4)]

        slot_in = [sem(f"slot_in{s}") for s in range(SLOTS)]
        unit_done = sem("unit_done")
        bank_free = [sem(f"bank_free{b}") for b in range(4)]
        names = """params_in consts_made rows_clean packs_turned packs_read c_silu c_turned c_read x_turned x_read
            hist_turned hist_read mod_turned mod_read hi_done lo_done sq_ready sumsq_done root_ready u_ready u_hi_ready u_lo_ready res_done
            hist_put tails_saved rows_zero h_split y_split conv_done conv_silu v_turned v_copied gate_used
            gate_mm gate_lin gate_tr sp_abs sp_exp al_ready cum_mm g_ready gb_mm mt_ready wtok_ready qk_mm s_ready
            st_mm st_copied bmx_ready last_mm ws_arg ws_exp ws_ready kt_mm kt_read qn_prod n_mm n_new n_tr n_row n_out
            masks_ready state_mm c_updated pc_mm pc_copied num_mm num_copied t1_ready num_whole var_ready std_ready
            norm_coef hn_ready hn_turned hn_read tail_tr tail_cp xt_mm xt_read bt_mm bt_read cb_mm cb_read
            lastx_mm lastx_read decx_ready hd_mm hd_rhs hd_mm2 hd_read cb_bc t_ready w_exp w_ready y_mm y_read xw_ready
            ph_mm ph_copied hmask_ready ht_mm ht_read up_mm up_done yi_mm yi_read yi_tr yi_add gsq_ready gss_done
            grs_ready gnorm_done fin_ready fin_tr fin_cp pad_zero merged act_chain dve_chain pool_chain""".split()
        S = {n: sem(n) for n in names}
        state_in = [sem(f"state_in{h}") for h in range(MH)]
        ssm_in = [sem(f"ssm_in{r}") for r in range(2)]
        state_out = [sem(f"state_out{h}") for h in range(MH)]
        small_out = sem("small_out")
        tail_sent = [sem(f"tail_sent{h}") for h in range(2)]
        row_sent = sem("row_sent")

        def sequences(ap):
            return ap.rearrange("p (b t) -> p b t", t=ST)

        def convolved_samples(a):
            return a[:, TP + HIST:].rearrange("p (b w) -> p b w", w=HIST + ST)[:, :, 0:ST]

        def panel_source(name, p):
            if name == "ada":
                return io["ada_w"][0].rearrange("(k p) n -> p k n", p=128)[:, :, bass.ds(p * 256, 256)]
            if name in ("pa", "pb"):
                return io["w_" + name][0].rearrange("(k p) n -> p k n", p=128)[:, :, bass.ds(p * 128, 128)]
            if name == "out":
                return io["w_out"][0].rearrange("(k p) n -> p k n", p=128)[:, :, bass.ds(p * 256, 256)]
            off = IN_OFF["q" if name == "qk" else name]
            return io["w_in"][0].rearrange("(k p) n -> p k n", p=128)[:, :, bass.ds(p * 256 + off, 256)]

        def c_of(ap, b, h):
            return ap[0, bass.ds(b, 1), h].rearrange("o (d p) v -> p (o d) v", p=128)

        def cbuf(h):
            return cb[:, h, :].rearrange("p (d v) -> p d v", v=DV)

        def h_of(ap, b):
            return ap[0, bass.ds(b, 1)].rearrange("o (t e) q n -> (e q) (o t) n", e=2)

        def hbuf(r):
            return hb[:, r, :].rearrange("p (t n) -> p t n", n=SN)

        def panel_part(seg, q):
            j = q % seg.per_panel
            w = ring[seg.slot(q)][:, 0:seg.chunks * seg.width].rearrange("p (k n) -> p k n", n=seg.width)
            return w[:, :, j * 128:(j + 1) * 128] if seg.parts == 1 else w[:, j * seg.kc:(j + 1) * seg.kc, :]

        block = ctx.enter_context(nc.Block())

        @block.sync
        def _(sp_):
            rows = [
                (pk[0:72, 0, :], io["ada_b"][0].rearrange("(r p) -> r p", p=128)),
                (pk[72:80, 0, :], io["norm_ff1"][0].rearrange("(r p) -> r p", p=128)),
                (pk[80:88, 0, :], io["norm_mix"][0].rearrange("(r p) -> r p", p=128)),
                (pk[88:96, 0, :], io["norm_ff2"][0].rearrange("(r p) -> r p", p=128)),
                (pk[96:104, 0, :], io["final_norm"].rearrange("(r p) -> r p", p=128)),
                (pk[0:16, 1, :], io["m_conv_b"][0].rearrange("(r p) -> r p", p=128)),
                (pk[16:80, 1, :], io["m_conv_w"][0].rearrange("w (r p) -> (w r) p", p=128)),
                (pk[80:96, 1, :], io["m_head_g"][0].rearrange("(r p) -> r p", p=128)),
                (pk[96:112, 1, :], io["s_norm_g"][0].rearrange("(r p) -> r p", p=128)),
                (pk[0:24, 2, :], io["s_conv_b"][0].rearrange("(r p) -> r p", p=128)),
                (pk[24:120, 2, :], io["s_conv_w"][0].rearrange("w (r p) -> (w r) p", p=128)),
                (x_rows[:, 0:2, :], io["x_prompt"][0].rearrange("(c p) d -> p c d", p=128)),
                (x_rows[0:64, 2, :], io["x_sample"].rearrange("b t d -> (b t) d")),
                (mh_rows[0:24, :], io["state_mlstm_conv"][0].rearrange("b j c -> (b j) c")),
                (sh_rows[0:24, :], io["state_ssm_conv"][0].rearrange("b j c -> (b j) c")),
                (n_rows[0:8, :], io["state_mlstm_n"][0].rearrange("b h d -> b (h d)")),
                (m0_r[:, :], io["state_mlstm_m"][0]),
                (m0_b[:, :], io["state_mlstm_m"][0].rearrange("b h -> (b h)").partition_broadcast(128)),
                (a_neg[:, :], io["s_A_log"][0].partition_broadcast(128)),
                (gate_sb[0:8, 0:1], io["m_if_b"][0].rearrange("(h o) -> h o", o=1)),
                (gate_sb[8:40, 0:1], io["s_dt_bias"][0].rearrange("(h o) -> h o", o=1)),
                (d_col[:, :], io["s_D"][0].rearrange("(h o) -> h o", o=1)),
                (gate_w[:, :, 0:8], io["w_in"][0].rearrange("(k p) n -> p k n", p=128)[:, :, IN_OFF["if"]:IN_OFF["if"] + 8]),
                (gate_w[:, :, 8:40], io["w_in"][0].rearrange("(k p) n -> p k n", p=128)[:, :, IN_OFF["dt"]:IN_OFF["dt"] + 32]),
            ]
            sp_.wait_ge(S["rows_clean"], 1)
            rows += [(c_rows[0:1, :], io["c_prompt"]), (c_rows[1:9, :], io["c_sample"])]
            with nc.allow_non_contiguous_dma(reason="a few parameter columns"):
                for dst, src in rows:
                    sp_.dma_start(dst, src).then_inc(S["params_in"], 16)

            def load(seg, i, q):
                if q % seg.per_panel:
                    return
                k = q // seg.per_panel
                s = seg.slot(q)
                if not isinstance(i, int):
                    if seg.split:
                        sp_.wait_ge(S["lo_done"], i * seg.gu + (seg.s0 + (k - SLOTS + 1) * seg.per_panel))
                    else:
                        sp_.wait_ge(unit_done, i * seg.gu + (seg.u0 + (k - SLOTS + 1) * seg.per_panel))
                elif seg.g0 + seg.gp * i + k >= SLOTS:
                    split, n = panel_free[seg.g0 + seg.gp * i + k - SLOTS]
                    sp_.wait_ge(S["lo_done"] if split else unit_done, n)
                if seg.name in ("up1", "up2"):
                    which = ("ff1_" if seg.name == "up1" else "ff2_") + ("w1" if k % 2 == 0 else "w3")
                    src = io[which][0].rearrange("(k p) n -> p k n", p=128)[:, :, bass.ds(i * 512 + (k // 2) * 256, 256)]
                elif seg.name in ("down1", "down2"):
                    w2 = io["ff1_w2" if seg.name == "down1" else "ff2_w2"][0].rearrange("(e k p) n -> e p k n", p=128, e=2)
                    src = w2[k % 2][:, :, bass.ds(i * 512 + (k // 2) * 128, 128)]
                else:
                    src = panel_source(seg.name, i * seg.gp + k)
                dst = ring[s][:, 0:seg.chunks * seg.width].rearrange("p (k n) -> p k n", n=seg.width)
                sp_.dma_start(dst, src).then_inc(slot_in[s], 16)

            def memory_loads():
                sp_.wait_ge(S["conv_silu"], 16)
                sp_.wait_ge(S["tails_saved"], 16)
                for h in range(MH):
                    sp_.dma_start(cbuf(h), c_of(io["state_mlstm_C"], 0, h)).then_inc(state_in[h], 16)
                with sp_.Fori(1, SB) as b:
                    for h in range(MH):
                        sp_.wait_ge(state_out[h], b * 16)
                        sp_.dma_start(cbuf(h), c_of(io["state_mlstm_C"], b, h)).then_inc(state_in[h], 16)

            def load_segment(seg):
                def step(i, q):
                    if seg.name == "mo" and isinstance(i, int) and i == 1 and q == 0:
                        memory_loads()
                    load(seg, i, q)
                walk(sp_, seg, step)
            for seg in segs.values():
                load_segment(seg)

        @block.gpsimd
        def _(pool):
            ch = Chain(pool, S["pool_chain"])
            nc.gpsimd.memset(c_rows[0:32, :], 0.0).then_inc(S["rows_clean"], 1)
            for m, v in ((ident, 0.0), (ones, 1.0), (tri, 1.0), (tri_s, 1.0), (neg_p, 0.0), (neg_s, 0.0), (seg_m, 1.0),
                         (seg_b, 0.0), (seg_t, 0.0), (row_last, 0.0), (last_s, 0.0), (last_b, 0.0), (mod_sum, 0.0),
                         (tile_of_head, 1.0), (g3, 0.0), (cum, 0.0), (sm, 0.0), (mean_var, 0.0)):
                ch.inc(nc.gpsimd.memset(m[:], v))
            ch.settle()

            def keep(ap, pattern, op, fill, base=0, per_partition=0):
                ch.link(nc.gpsimd.affine_select(out=ap, in_=ap, compare_op=op, fill=fill, base=base, pattern=pattern,
                                                channel_multiplier=per_partition))

            keep(ident[:, :], [[-1, 128]], ALU.not_equal, 1.0, 0, 1)
            keep(tri[:, 0:128], [[1, 128]], ALU.is_ge, 0.0, 0, -1)
            keep(tri[:, 256:384], [[1, 128]], ALU.is_ge, 0.0, 0, -1)
            ts4 = tri_s[:, :].rearrange("p (r b t) -> p r b t", r=2, t=ST)
            keep(ts4, [[0, 2], [-8, 8], [0, 8]], ALU.is_ge, 0.0, 0, 1)
            keep(ts4, [[0, 2], [8, 8], [1, 8]], ALU.is_ge, 0.0, 0, -1)
            keep(neg_p[:, :], [[-1, 128]], ALU.is_ge, NEG, 0, 1)
            ns3 = neg_s[:, :].rearrange("p (b t) -> p b t", t=ST)
            keep(ns3, [[-8, 8], [-1, 8]], ALU.is_ge, NEG, 0, 1)
            keep(ns3, [[8, 8], [0, 8]], ALU.is_ge, NEG, 7, -1)
            keep(seg_m[:, :], [[-8, 8]], ALU.is_ge, 0.0, 0, 1)
            keep(seg_m[:, :], [[8, 8]], ALU.is_ge, 0.0, 7, -1)
            keep(seg_b[:, :, :].rearrange("p c (b t) -> p c b t", t=ST), [[1, 8], [-1, 8], [0, 8]], ALU.not_equal, 1.0)
            keep(seg_t[:, :].rearrange("p (b t) -> p b t", t=ST), [[-1, 8], [0, 8]], ALU.not_equal, 1.0, 0, 1)
            keep(row_last[:, :], [[0, 128]], ALU.not_equal, 1.0, -127, 1)
            keep(last_s[:, :].rearrange("p (b t) -> p b t", t=ST), [[-8, 8], [0, 8]], ALU.not_equal, 1.0, -7, 1)
            keep(last_b[:, :], [[-8, 8]], ALU.not_equal, 1.0, -7, 1)
            for j in range(4):
                keep(mod_sum[:, :], [[-1, NSEQ]], ALU.not_equal, 1.0, -32 * j, 1)
            keep(tile_of_head[:, :], [[-2, 16]], ALU.is_ge, 0.0, 0, 1)
            keep(tile_of_head[:, :], [[2, 16]], ALU.is_ge, 0.0, 1, -1)
            nc.gpsimd.memset(sp[:], 0.0).then_inc(S["consts_made"], 1)

            def conv_side(seg, first, padded):
                def step(i, q):
                    r = q % 4
                    c = seg.own(i, q) + first
                    r2 = padded[:, r, TP + HIST:].rearrange("p (b w) -> p b w", w=HIST + ST)
                    if not isinstance(i, int) or seg.gu * i + q >= 4:
                        pool.wait_ge(S["conv_done"], c - 3)
                    nc.gpsimd.tensor_copy(r2[:, :, 0:HIST], hist[:, bass.ds(c, 1), :].rearrange("p o (b w) -> p (o b) w", w=HIST))\
                        .then_inc(S["hist_put"], 1)
                    pool.wait_ge(bank_free[seg.bank(q)], seg.bank_use(i, q) + 1)
                    ch.inc(nc.gpsimd.tensor_copy(tails[:, bass.ds(c, 1), 0:HIST], padded[:, r:r + 1, TP:TP + HIST]))
                    nc.gpsimd.tensor_copy(tails[:, bass.ds(c, 1), HIST:].rearrange("p o (b w) -> p (o b) w", w=HIST),
                                          r2[:, :, ST:]).then_inc(S["tails_saved"], 1)
                    pool.wait_ge(S["tails_saved"], c + 1)
                walk(pool, seg, step, None, ch, 1)

            pool.wait_ge(S["hist_read"], 3)
            pool.wait_ge(S["gate_mm"], 1)
            pool.wait_ge(S["u_lo_ready"], 2)
            nc.gpsimd.memset(pad[:, :, 0:HIST], 0.0).then_inc(S["pad_zero"], 1)
            pool.wait_ge(S["pad_zero"], 1)
            ch.link(nc.gpsimd.memset(kwm[64:128, :, :], 0.0))
            nc.gpsimd.memset(v_tok[64:128, 2, :], 0.0).then_inc(S["rows_zero"], 1)
            pool.wait_ge(S["rows_zero"], 1)
            conv_side(segs["qk"], 0, pad)

            def send_tails(first, tiles, prompt, sample, count0):
                for r in range(tiles // 4):
                    n = count0 + r
                    pool.wait_ge(S["tail_cp"], n + 1)
                    cols = slice(r * 512, (r + 1) * 512)
                    pool.dma_start(prompt[0, 0][:, cols], tail_out[n < 4][0:HIST, n % 2, :]).then_inc(tail_sent[n % 2], 16)
                    pool.dma_start(sample[0].rearrange("b j c -> (b j) c")[:, cols], tail_out[n < 4][HIST:27, n % 2, :])\
                        .then_inc(tail_sent[n % 2], 16)
            send_tails(0, 16, out["p_mconv"], out["s_mconv"], 0)

            with pool.Fori(0, SB) as b:
                for h in range(MH):
                    pool.wait_ge(S["c_updated"], b * MH + (h + 1))
                    pool.dma_start(c_of(out["s_C"], b, h), cbuf(h)).then_inc(state_out[h], 16)
            for h in range(MH):
                pool.wait_ge(S["pc_copied"], 2 * (h + 1))
                pool.dma_start(c_of(out["p_C"], 0, h), cbuf(h)).then_inc(state_out[h], 16)
            pool.wait_ge(S["ws_ready"], 1)
            pool.dma_start(out["p_m"][0], sm[0:1, 6, 4:8]).then_inc(small_out, 16)
            pool.dma_start(out["s_m"].rearrange("o b h -> o (b h)"), sm[0:1, 11, 0:32]).then_inc(small_out, 16)
            pool.wait_ge(S["n_row"], 2)
            pool.dma_start(out["p_n"][0, 0].rearrange("h (d p) -> (h d) p", p=128), n_rows2[0:8, 1024:1152]).then_inc(small_out, 16)
            pool.dma_start(out["s_n"][0].rearrange("b h d -> b (h d)"), n_rows2[0:8, 0:1024]).then_inc(small_out, 16)

            pool.wait_ge(unit_done, segs["xbc"].u0)
            nc.gpsimd.memset(pad2[:, :, 0:HIST], 0.0).then_inc(S["pad_zero"], 1)
            conv_side(segs["xbc"], 16, pad2)
            pool.wait_ge(S["conv_silu"], 40)
            nc.gpsimd.memset(xd[64:128, 2, :], 0.0).then_inc(S["rows_zero"], 1)
            pool.wait_ge(S["rows_zero"], 2)
            send_tails(16, 24, out["p_sconv"], out["s_sconv"], 4)

            pool.wait_ge(S["y_mm"], 16)
            nc.gpsimd.memset(btm[64:128, :, :], 0.0).then_inc(S["rows_zero"], 1)
            pool.wait_ge(S["ph_copied"], 4)
            pool.dma_start(h_of(out["p_ssm"], 0), h_t.rearrange("p (t n) -> p t n", n=SN)).then_inc(row_sent, 16)
            for r in range(2):
                pool.dma_start(hbuf(r), h_of(io["state_ssm"], r)).then_inc(ssm_in[r], 16)
            with pool.Fori(0, SB // 2 - 1) as i:
                for r in range(2):
                    pool.wait_ge(S["up_done"], i * 8 + 4 * (r + 1))
                    pool.dma_start(h_of(out["s_ssm"], i * 2 + r), hbuf(r)).then_inc(state_out[r], 16)
                    pool.wait_ge(state_out[r], i * 16 + (16 * (SB + 1) + 16))
                    pool.dma_start(hbuf(r), h_of(io["state_ssm"], i * 2 + (r + 2))).then_inc(ssm_in[r], 16)
            for r in range(2):
                pool.wait_ge(S["up_done"], (SB // 2 - 1) * 8 + 4 * (r + 1))
                pool.dma_start(h_of(out["s_ssm"], SB - 2 + r), hbuf(r)).then_inc(state_out[r], 16)

            for c in range(3):
                pool.wait_ge(S["fin_cp"], 2 * (c + 1))
                if c < 2:
                    pool.dma_start(out["y_p"][0, c * 128:(c + 1) * 128, :], y_rows[:, c, :]).then_inc(small_out, 16)
                else:
                    pool.dma_start(out["y_s"].rearrange("b t d -> (b t) d"), y_rows[0:64, 2, :]).then_inc(small_out, 16)
            pool.wait_ge(small_out, 7 * 16)
            pool.wait_ge(row_sent, 16)
            for r in range(2):
                pool.wait_ge(tail_sent[r], 5 * 32)
            for h in range(MH):
                pool.wait_ge(state_out[h], 16 * (SB + 1) + (16 * (SB // 2) if h < 2 else 0))

        @block.tensor
        def _(pe):
            def turn(dst, src, rows):
                return nc.tensor.transpose(dst, src, ident[0:rows, 0:rows])

            def mm(dst, lhs, rhs, first=True, last=True):
                return nc.tensor.matmul(dst, lhs, rhs, start=first, stop=last)

            def dense(seg, high=u_hi, low=u_lo, after=None):
                def step(i, q):
                    bank = banks[seg.bank(q)][:, 0:T]
                    part_no, r = q % seg.parts, (seg.s0 + q) % 2
                    rows = range(part_no * seg.kc, (part_no + 1) * seg.kc)
                    if part_no == 0:
                        pe.wait_ge(bank_free[seg.bank(q)], seg.bank_use(i, q))
                    pe.wait_ge(S["hi_done"], seg.split_no(i, q) + 1)
                    for kc, row in enumerate(rows):
                        mm(bank, w_hi[r][:, kc, :], high[:, row, :], row == 0, False)
                    for kc, row in enumerate(rows):
                        mm(bank, w_hi[r][:, kc, :], low[:, row, :], False, False)
                    pe.wait_ge(S["lo_done"], seg.split_no(i, q) + 1)
                    for kc, row in enumerate(rows):
                        ins = mm(bank, w_lo[r][:, kc, :], high[:, row, :], False, row == seg.parts * seg.kc - 1)
                    ins.then_inc(unit_done, 1)
                    if after and (not isinstance(i, int) or i + q > 0):
                        after(i + (q - 1) // seg.gu, (q - 1) % seg.gu)
                walk(pe, seg, step)

            def settle_banks(seg):
                for b in range(4):
                    pe.wait_ge(bank_free[b], (seg.t0 + seg.tiles) // 4)

            pe.wait_ge(S["params_in"], 26 * 16)
            pe.wait_ge(S["consts_made"], 1)
            turn(aux[0][:, 0:104], pk[0:104, 0, :], 104)
            turn(aux[0][:, 104:216], pk[0:112, 1, :], 112)
            turn(aux[0][:, 216:336], pk[0:120, 2, :], 120)
            for kc in range(8):
                ins = turn(aux[0][:, 336 + 8 * kc:344 + 8 * kc], n_rows[0:8, kc * 128:(kc + 1) * 128], 8)
            ins.then_inc(S["packs_turned"], 1)
            pe.wait_ge(S["c_silu"], 1)
            for kc in range(KD):
                ins = turn(aux[1][:, 32 * kc:32 * kc + 32], c_rows[0:32, kc * 128:(kc + 1) * 128], 32)
            ins.then_inc(S["c_turned"], 1)
            for c in range(16):
                ins = turn(aux[2][:, 24 * c:24 * c + 24], mh_rows[0:24, c * 128:(c + 1) * 128], 24)
            for c in range(20):
                ins = turn(aux[3][:, 24 * c:24 * c + 24], sh_rows[0:24, c * 128:(c + 1) * 128], 24)
            for c in range(4):
                ins = turn(aux[2][:, 384 + 24 * c:408 + 24 * c], sh_rows[0:24, (20 + c) * 128:(21 + c) * 128], 24)
            ins.then_inc(S["hist_turned"], 1)
            for kc in range(KD):
                b = kc % 4
                if kc == 0:
                    pe.wait_ge(S["packs_read"], 1)
                elif kc == 1:
                    pe.wait_ge(S["c_read"], 1)
                elif kc == 2:
                    pe.wait_ge(S["hist_read"], 3)
                elif kc >= 4:
                    pe.wait_ge(S["x_read"], kc - 3)
                turn(aux[b][:, 0:128], x_rows[:, 0, kc * 128:(kc + 1) * 128], 128)
                turn(aux[b][:, 128:256], x_rows[:, 1, kc * 128:(kc + 1) * 128], 128)
                turn(aux[b][:, 256:320], x_rows[0:64, 2, kc * 128:(kc + 1) * 128], 64).then_inc(S["x_turned"], 1)
            pe.wait_ge(S["x_read"], KD)

            ada = segs["ada"]

            def mod_columns(i, k):
                p = ada.own(i, k)
                r = k % 2
                pe.wait_ge(bank_free[ada.bank(k)], ada.bank_use(i, k) + 1)
                if not isinstance(i, int) or 4 * i + k >= 2:
                    pe.wait_ge(S["mod_read"], p - 1)
                for j in range(2):
                    ins = mm(aux[r][:, NSEQ * j:NSEQ * (j + 1)], mod_row[r][:, j * 128:(j + 1) * 128], mod_sum[:, :])
                ins.then_inc(S["mod_turned"], 1)

            def ada_step(i, k):
                s, b = ada.slot(k), ada.bank(k)
                w = ring[s][:, 0:KD * 256].rearrange("p (k n) -> p k n", n=256)
                pe.wait_ge(slot_in[s], ada.arrivals(i, k))
                if not isinstance(i, int) or i > 0:
                    pe.wait_ge(bank_free[b], ada.bank_use(i, k))
                for kc in range(KD):
                    q = kc % 4
                    ins = mm(banks[b][32 * q:32 * q + 32, 0:256], c_t[:, kc, :], w[:, kc, :], kc < 4, kc >= 4)
                ins.then_inc(unit_done, 1)
            walk(pe, ada, mod_columns, ada_step, None, 0, 1)

            def sum_squares(n):
                pe.wait_ge(S["sq_ready"], n + 1)
                for kc in range(KD):
                    ins = mm(aux[0][:, 0:T], ones[:, :], sq[:, kc, :], kc == 0, kc == KD - 1)
                ins.then_inc(S["sumsq_done"], 1)

            pe.wait_ge(S["mod_read"], ada.tiles)
            sum_squares(0)
            pe.wait_ge(S["u_lo_ready"], 1)
            dense(segs["up1"])
            pe.wait_ge(S["h_split"], KF)
            dense(segs["down1"], ff_hi, ff_lo)
            sum_squares(1)

            pe.wait_ge(S["u_ready"], 2)
            for kc in range(KD):
                ins = mm(aux[1][0:40, 0:T], gate_w[:, kc, :], u_t[:, kc, :], kc == 0, kc == KD - 1)
            ins.then_inc(S["gate_mm"], 1)
            pe.wait_ge(S["u_lo_ready"], 2)
            dense(segs["qk"])
            pe.wait_ge(S["gate_lin"], 1)
            turn(aux[2][:, 0:40], xg[0:40, 0:128], 40)
            turn(aux[2][:, 40:80], xg[0:40, 128:256], 40)
            turn(aux[2][0:64, 80:120], xg[0:40, 256:320], 40).then_inc(S["gate_tr"], 1)

            vs = segs["v"]

            def turn_v(i, q):
                r = q % 4
                x = aux[r % 2]
                pe.wait_ge(bank_free[vs.bank(q)], vs.bank_use(i, q) + 1)
                if not isinstance(i, int) or vs.gu * i + q >= 2:
                    pe.wait_ge(S["v_copied"], vs.own(i, q) - 1)
                turn(x[:, 0:128], v_tmp[:, r, 0:128], 128)
                turn(x[:, 128:256], v_tmp[:, r, 128:256], 128)
                turn(x[0:64, 256:384], v_tmp[:, r, 256:320], 128).then_inc(S["v_turned"], 1)
            dense(vs, after=turn_v)
            turn_v(*vs.at(vs.units - 1))

            def turn_tails(first, tiles, count0):
                for r in range(tiles // 4):
                    n = count0 + r
                    x = aux[3 if count0 == 0 else n % 2]
                    if n > 0 and count0 == 0:
                        pe.wait_ge(S["tail_cp"], n)
                    if count0 and r >= 2:
                        pe.wait_ge(S["tail_cp"], n - 1)
                    for j in range(4):
                        ins = turn(x[0:27, j * 128:(j + 1) * 128], tails[:, first + 4 * r + j, :], 128)
                    ins.then_inc(S["tail_tr"], 1)
            pe.wait_ge(S["tails_saved"], 16)
            turn_tails(0, 16, 0)

            pe.wait_ge(S["al_ready"], 1)
            mm(aux[2][:, 0:36], tri[:, 0:128], al[:, 0, :])
            mm(aux[2][:, 36:72], ones[:, :], al[:, 0, :], True, False)
            mm(aux[2][:, 36:72], tri[:, 0:128], al[:, 1, :], False, True)
            mm(aux[2][:, 72:108], tri_s[:, :], al[0:64, 2, :])
            mm(aux[2][0:64, 108:112], seg_t[:, :], m0_r[:, :]).then_inc(S["cum_mm"], 1)
            pe.wait_ge(S["g_ready"], 1)
            pe.wait_ge(S["v_copied"], 16)
            pe.wait_ge(S["tail_cp"], 4)
            for h in range(MH):
                mm(aux[h][:, 0:128], sm[:, 0, h:h + 1].to_broadcast([128, 128]), ident[:, :])
                mm(aux[h][:, 128:256], sm[:, 1, h:h + 1].to_broadcast([128, 128]), ident[:, :])
                mm(aux[h][0:64, 256:320], sm[0:64, 2, h:h + 1].to_broadcast([64, 64]), ident[0:64, 0:64]).then_inc(S["gb_mm"], 1)
            pe.wait_ge(S["mt_ready"], 1)
            for h in range(MH):
                for d in range(2):
                    mm(aux[h][:, 0:128], qk_t[:, 2 * h + d, 0:128], qk_t[:, 8 + 2 * h + d, 0:128], d == 0, d == 1)
                for d in range(2):
                    mm(aux[h][:, 128:384], qk_t[:, 2 * h + d, 128:256], qk_t[:, 8 + 2 * h + d, 0:256], d == 0, d == 1)
                for d in range(2):
                    ins = mm(aux[h][0:64, 384:448], qk_t[:, 2 * h + d, 256:320], qk_t[:, 8 + 2 * h + d, 256:320], d == 0, d == 1)
                ins.then_inc(S["qk_mm"], 1)
            settle_banks(segs["v"])
            pe.wait_ge(S["bmx_ready"], 1)
            mm(banks[0][:, 0:8], row_last[:, :], sm[:, 4, 8:16])
            mm(banks[0][0:64, 8:16], last_s[:, :], sm[0:64, 4, 16:24])
            mm(banks[0][:, 16:80], ones[0:64, :], al2[0:64, :]).then_inc(S["last_mm"], 1)
            for h in range(MH):
                pe.wait_ge(S["s_ready"], h + 1)
                turn(aux[h][:, 0:128], dm[:, h, 0:128], 128)
                turn(aux[h][:, 128:256], dm[:, h, 128:256], 128)
                turn(aux[h][:, 256:384], dm[:, h, 256:384], 128)
                turn(aux[h][0:64, 384:448], dm[0:64, h, 384:448], 64).then_inc(S["st_mm"], 1)
            pe.wait_ge(S["ws_ready"], 1)
            for c in range(8):
                b = banks[c % 4]
                if c >= 4:
                    pe.wait_ge(S["kt_read"], c - 3)
                turn(b[:, 0:128], qk_t[:, 8 + c, 0:128], 128)
                turn(b[:, 128:256], qk_t[:, 8 + c, 128:256], 128)
                turn(b[0:64, 256:384], qk_t[:, 8 + c, 256:320], 128).then_inc(S["kt_mm"], 1)
            pe.wait_ge(S["kt_read"], 8)
            pe.wait_ge(S["qn_prod"], 1)
            for h in range(MH):
                for d in range(2):
                    mm(banks[0][0:64, h:h + 1], acc_q[:, 2 * h + d, :], ones[:, 0:1], d == 0, d == 1)
            for c in range(8):
                mm(banks[0][:, 8 + 8 * c:16 + 8 * c], kw[0:64, 2, c * 128:(c + 1) * 128], seg_m[:, :])
            for c in range(8):
                mm(banks[0][:, 80 + c:81 + c], kw[:, 0, c * 128:(c + 1) * 128], ones[:, 0:1], True, False)
                ins = mm(banks[0][:, 80 + c:81 + c], kw[:, 1, c * 128:(c + 1) * 128], ones[:, 0:1], False, True)
            ins.then_inc(S["n_mm"], 1)
            pe.wait_ge(S["n_new"], 1)
            for c in range(8):
                bk = banks[1 + c // 4]
                turn(bk[0:8, (c % 4) * 128:(c % 4 + 1) * 128], n_t[:, c, :], 128)
            turn(banks[3][0:8, 0:128], sm[:, 7, 0:8], 128).then_inc(S["n_tr"], 1)

            pe.wait_ge(S["st_copied"], MH)
            pe.wait_ge(S["n_row"], 2)
            pe.wait_ge(S["rows_zero"], 1)

            def memory(b, h, first, last=False):
                n = b * MH + h
                c_h = cb[:, h, :].rearrange("p (d v) -> p d v", v=DV)
                pe.wait_ge(state_in[h], b * 16 + 16)
                pe.wait_ge(S["masks_ready"], n + 1)
                for d in range(2):
                    mm(aux[h][64 * d:64 * d + 64, :], qm[:, h, d, :], c_h[:, d, :], first, last)
                if not first or h >= 2:
                    pe.wait_ge(S["c_updated"], n - 1)
                for d in range(2):
                    ins = mm(banks[2 * (h % 2) + d][:, :], kwm[:, h, d * 128:(d + 1) * 128], v_tok[:, 2, h * DV:(h + 1) * DV])
                ins.then_inc(S["state_mm"], 1)
            for h in range(MH):
                memory(0, h, True)
            with pe.Fori(1, SB - 1) as b:
                for h in range(MH):
                    memory(b, h, False)
            for h in range(MH):
                memory(SB - 1, h, False, True)
            for h in range(MH):
                for d in range(2):
                    n = 2 * h + d
                    bk = banks[n % 4]
                    pe.wait_ge(S["c_updated"], SB * MH)
                    if n >= 4:
                        pe.wait_ge(S["pc_copied"], n - 3)
                    c = h * 2 + d
                    mm(bk[:, :], kw[:, 0, c * 128:(c + 1) * 128], v_tok[:, 0, h * DV:(h + 1) * DV], True, False)
                    mm(bk[:, :], kw[:, 1, c * 128:(c + 1) * 128], v_tok[:, 1, h * DV:(h + 1) * DV], False, True).then_inc(S["pc_mm"], 1)
            pe.wait_ge(S["pc_copied"], 8)

            def turn_head(h):
                pe.wait_ge(S["hn_ready"], h + 1)
                nm = (num, num2)[h % 2]
                for j in range(4):
                    c = 4 * h + j
                    pe.wait_ge(S["num_whole"], h + 1)
                    x = aux[h]
                    if j > 0:
                        pe.wait_ge(S["hn_read"], c)
                    turn(x[:, 0:128], nm[:, 0, j * 128:(j + 1) * 128], 128)
                    turn(x[:, 128:256], nm[:, 1, j * 128:(j + 1) * 128], 128)
                    turn(x[:, 256:320], nm[0:64, 2, j * 128:(j + 1) * 128], 64).then_inc(S["hn_turned"], 1)
            for h in range(MH):
                if h > 0:
                    pe.wait_ge(S["num_whole"], h)
                v_h = slice(h * DV, (h + 1) * DV)
                mm(banks[0][:, :], st_s[:, h, 0:128], v_tok[:, 0, v_h])
                mm(banks[1][:, :], st_s[:, h, 128:256], v_tok[:, 0, v_h], True, False)
                mm(banks[1][:, :], st_s[:, h, 256:384], v_tok[:, 1, v_h], False, True)
                mm(banks[2][0:64, :], st_s[0:64, h, 384:448], v_tok[0:64, 2, v_h]).then_inc(S["num_mm"], 1)
                if h > 0:
                    turn_head(h - 1)
            turn_head(MH - 1)

            pe.wait_ge(S["num_whole"], MH)
            dense(segs["mo"])
            pe.wait_ge(S["y_split"], 16)
            dense(segs["pa"], y_hi, y_lo)
            dense(segs["xbc"])

            settle_banks(segs["xbc"])
            pe.wait_ge(S["tails_saved"], 40)
            turn_tails(16, 24, 4)
            pe.wait_ge(S["conv_silu"], 40)
            for n in range(12):
                gr, c = divmod(n, 3)
                b = banks[n % 4]
                if n >= 4:
                    pe.wait_ge(S["xt_read"], n - 3)
                for j in range(4):
                    src = xbc_t[:, 4 * gr + j, c * 128:min(T, (c + 1) * 128)]
                    dst = b[:, j * 128:(j + 1) * 128] if c < 2 else b[0:64, j * 128:(j + 1) * 128]
                    ins = turn(dst, src, 128)
                ins.then_inc(S["xt_mm"], 1)
            for c in range(3):
                if c == 0:
                    pe.wait_ge(S["tail_cp"], 10)
                x = aux[c]
                for j in range(4):
                    src = xbc_t[:, 16 + j, c * 128:min(T, (c + 1) * 128)]
                    dst = x[:, j * 128:(j + 1) * 128] if c < 2 else x[0:64, j * 128:(j + 1) * 128]
                    ins = turn(dst, src, 128)
                ins.then_inc(S["bt_mm"], 1)
            for gr in range(SG):
                b = banks[gr]
                pe.wait_ge(S["xt_read"], 12)
                mm(b[:, 0:256], xbc_t[:, 16 + gr, 0:128], xbc_t[:, 20 + gr, 0:256])
                mm(b[:, 256:384], xbc_t[:, 16 + gr, 128:256], xbc_t[:, 20 + gr, 128:256])
                mm(b[0:64, 384:448], xbc_t[:, 16 + gr, 256:320], xbc_t[:, 20 + gr, 256:320]).then_inc(S["cb_mm"], 1)
            mm(aux[3][:, 0:32], row_last[:, :], cum[:, 1, 4:36])
            mm(aux[3][0:64, 32:64], last_s[:, :], cum[0:64, 2, 4:36]).then_inc(S["lastx_mm"], 1)
            pe.wait_ge(S["decx_ready"], 1)
            mm(aux[3][0:32, 64:72], sm[0:64, 8, 0:32], last_b[:, :]).then_inc(S["hd_mm"], 1)
            pe.wait_ge(S["hd_rhs"], 1)
            mm(aux[3][:, 128:272], parity[:, :, :].rearrange("p a b -> p (a b)"), hd_in[0:32, :]).then_inc(S["hd_mm2"], 1)

            def decay_rows(q):
                for j in range(4):
                    h = 4 * q + j
                    if q == 0:
                        if j < 3:
                            pe.wait_ge(S["bt_read"], j + 1)
                        else:
                            pe.wait_ge(S["hd_read"], 1)
                    else:
                        pe.wait_ge(S["t_ready"], 4 * (q - 1) + j + 1)
                    mm(aux[j][:, 0:128], al[:, 0, 4 + h:5 + h].to_broadcast([128, 128]), tri[:, 0:128])
                    mm(aux[j][:, 128:256], al[:, 0, 4 + h:5 + h].to_broadcast([128, 128]), ones[:, :], True, False)
                    mm(aux[j][:, 128:256], al[:, 1, 4 + h:5 + h].to_broadcast([128, 128]), tri[:, 0:128], False, True)
                    mm(aux[j][0:64, 256:320], al[0:64, 2, 4 + h:5 + h].to_broadcast([64, 64]), tri_s[:, 0:64]).then_inc(S["cb_bc"], 1)

            def head_outputs(q):
                pe.wait_ge(S["w_ready"], q + 1)
                w = w_int[:, q % 2, :].rearrange("p (j s) -> p j s", s=448)
                for pr in range(2):
                    n = 2 * q + pr
                    b = banks[n % 4]
                    if n < 4:
                        pe.wait_ge(S["cb_read"], n + 1)
                    else:
                        pe.wait_ge(S["y_read"], n - 3)
                    for e in range(2):
                        h = 4 * q + 2 * pr + e
                        o = slice(64 * e, 64 * e + 64)
                        col = slice(h * 64, (h + 1) * 64)
                        mm(b[o, 0:128], xd[:, 0, col], w[:, 2 * pr + e, 0:128])
                        mm(b[o, 128:256], xd[:, 0, col], w[:, 2 * pr + e, 128:256], True, False)
                        mm(b[o, 128:256], xd[:, 1, col], w[:, 2 * pr + e, 256:384], False, True)
                        ins = mm(b[o, 256:320], xd[0:64, 2, col], w[0:64, 2 * pr + e, 384:448])
                    ins.then_inc(S["y_mm"], 1)
            decay_rows(0)
            for q in range(8):
                if q < 7:
                    decay_rows(q + 1)
                head_outputs(q)
            pe.wait_ge(S["xw_ready"], 1)
            for gr in range(SG):
                pe.wait_ge(S["y_read"], 16)
                for j in range(4):
                    c = slice((4 * gr + j) * 128, (4 * gr + j + 1) * 128)
                    mm(banks[gr][:, j * 128:(j + 1) * 128], xd[:, 0, c], bt[:, 0, gr * 128:(gr + 1) * 128], True, False)
                    ins = mm(banks[gr][:, j * 128:(j + 1) * 128], xd[:, 1, c], bt[:, 1, gr * 128:(gr + 1) * 128], False, True)
                ins.then_inc(S["ph_mm"], 1)

            def ssm_step(i, r, first, last=False):
                b = i * 2 + r
                h3 = hb[:, r, :].rearrange("p (t n) -> p t n", n=SN)
                up_banks = (aux[2], aux[3], banks[2], banks[3])
                pe.wait_ge(ssm_in[r], i * 16 + 16)
                pe.wait_ge(S["hmask_ready"], b + 1)
                for gr in range(SG):
                    if not first or gr >= 2:
                        pe.wait_ge(S["ht_read"], b * 4 + (gr - 1))
                    for j in range(4):
                        ins = turn(aux[gr % 2][:, j * 128:(j + 1) * 128], h3[:, 4 * gr + j, :], 128)
                    ins.then_inc(S["ht_mm"], 1)
                    if not first:
                        pe.wait_ge(S["up_done"], b * 4 + (gr - 3))
                    for j in range(4):
                        c = 4 * gr + j
                        ins = mm(up_banks[gr][:, j * 128:(j + 1) * 128], xd[:, 2, c * 128:(c + 1) * 128],
                                 btm[:, r, gr * 128:(gr + 1) * 128])
                    ins.then_inc(S["up_mm"], 1)
                for gr in range(SG):
                    pe.wait_ge(S["ht_read"], b * 4 + (gr + 1))
                    o = slice(64 * (gr % 2), 64 * (gr % 2) + 64)
                    ins = mm(banks[gr // 2][o, :], cm[:, r, gr * TS:(gr + 1) * TS], h_t[:, gr * 512:(gr + 1) * 512], first, last)
                ins.then_inc(S["yi_mm"], 1)
            pe.wait_ge(S["ph_copied"], 4)
            pe.wait_ge(row_sent, 16)
            pe.wait_ge(S["rows_zero"], 3)
            ssm_step(0, 0, True)
            ssm_step(0, 1, False)
            with pe.Fori(1, SB // 2 - 1) as i:
                ssm_step(i, 0, False)
                ssm_step(i, 1, False)
            ssm_step(SB // 2 - 1, 0, False)
            ssm_step(SB // 2 - 1, 1, False, True)
            pe.wait_ge(S["yi_read"], 2)
            pe.wait_ge(S["ht_read"], 4 * SB)
            for gr in range(SG):
                o = slice(64 * (gr % 2), 64 * (gr % 2) + 64)
                for j in range(4):
                    c = 4 * gr + j
                    ins = nc.tensor.transpose(aux[gr][:, j * 64:(j + 1) * 64], y_int[o, gr // 2, j * 128:(j + 1) * 128], ident[o, o])
                ins.then_inc(S["yi_tr"], 1)
            pe.wait_ge(S["up_done"], 4 * SB)
            pe.wait_ge(S["yi_add"], SG)
            dense(segs["z"])
            for gr in range(SG):
                pe.wait_ge(S["gsq_ready"], gr + 1)
                for j in range(4):
                    ins = mm(aux[gr][:, 0:T], ones[:, :], gsq[:, gr % 2, j * T:(j + 1) * T], j == 0, j == 3)
                ins.then_inc(S["gss_done"], 1)
            dense(segs["ga"])
            dense(segs["gb"])
            pe.wait_ge(S["gnorm_done"], 16)
            dense(segs["pb"], y_hi, y_lo)
            settle_banks(segs["pb"])
            pe.wait_ge(S["merged"], KD)
            dense(segs["out"], m_hi, m_lo)
            sum_squares(2)
            pe.wait_ge(S["u_lo_ready"], 3)
            dense(segs["up2"])
            pe.wait_ge(S["h_split"], 2 * KF)
            dense(segs["down2"], ff_hi, ff_lo)
            sum_squares(3)
            pe.wait_ge(S["fin_ready"], 1)
            for c in range(3):
                rows = 128 if c < 2 else 64
                for half in range(2):
                    n = 2 * c + half
                    x = aux[1 + n % 2]
                    if n >= 2:
                        pe.wait_ge(S["fin_cp"], n - 1)
                    for j in range(4):
                        ins = turn(x[0:rows, j * 128:(j + 1) * 128], u_t[:, 4 * half + j, c * 128:c * 128 + rows], 128)
                    ins.then_inc(S["fin_tr"], 1)

        @block.scalar
        def _(act):
            ch = Chain(act, S["act_chain"])

            def copy(dst, src, scale=1.0):
                return nc.scalar.activation(dst, src, ACT.Copy, scale=scale)

            act.wait_ge(S["params_in"], 26 * 16)
            nc.scalar.activation(c_rows[0:32, :], c_rows[0:32, :], ACT.Silu).then_inc(S["c_silu"], 1)
            act.wait_ge(S["packs_turned"], 1)
            ch.inc(copy(par[:, :], aux[0][:, 0:336]))
            copy(n_t[:, :, :], aux[0][:, 336:400].rearrange("p (a b) -> p a b", b=SB)).then_inc(S["packs_read"], 1)
            act.wait_ge(S["c_turned"], 1)
            copy(c_t[:, :, :], aux[1][:, 0:256].rearrange("p (a b) -> p a b", b=32)).then_inc(S["c_read"], 1)
            act.wait_ge(S["hist_turned"], 1)
            copy(hist[:, 0:16, :], aux[2][:, 0:384].rearrange("p (a b) -> p a b", b=24)).then_inc(S["hist_read"], 1)
            copy(hist[:, 16:36, :], aux[3][:, 0:480].rearrange("p (a b) -> p a b", b=24)).then_inc(S["hist_read"], 1)
            copy(hist[:, 36:40, :], aux[2][:, 384:480].rearrange("p (a b) -> p a b", b=24)).then_inc(S["hist_read"], 1)
            for kc in range(KD):
                act.wait_ge(S["x_turned"], kc + 1)
                copy(x_t[:, kc, :], aux[kc % 4][:, 0:T]).then_inc(S["x_read"], 1)
            nc.scalar.activation(a_neg[:, :], a_neg[:, :], ACT.Exp).then_inc(S["act_chain"], 1)
            ch.n += 1

            def square(n):
                nc.scalar.activation(sq[:, :, :], x_t[:, :, :], ACT.Square).then_inc(S["sq_ready"], 1)

            def root(n):
                act.wait_ge(S["sumsq_done"], n + 1)
                nc.scalar.activation(rs[:, :], aux[0][:, 0:T], ACT.Sqrt, bias=eps_col[:, 0:1], scale=1.0 / D).then_inc(S["root_ready"], 1)

            act.wait_ge(S["x_read"], KD)
            square(0)

            ada = segs["ada"]

            def ada_row(i, k):
                p, b = ada.own(i, k), ada.bank(k)
                act.wait_ge(unit_done, ada.unit(i, k) + 1)
                if not isinstance(i, int) or 4 * i + k >= 2:
                    act.wait_ge(S["mod_turned"], p - 1)
                copy(mod_row[k % 2][:, :], banks[b][:, 0:256]).then_inc(bank_free[b], 1)
            walk(act, ada, ada_row)
            root(0)

            def u_high(n):
                act.wait_ge(S["u_ready"], n + 1)
                nc.scalar.activation(u_hi[:, :, :], u_t[:, :, :], ACT.Copy).then_inc(S["u_hi_ready"], 1)

            def high(seg):
                def step(i, q):
                    r = (seg.s0 + q) % 2
                    act.wait_ge(slot_in[seg.slot(q)], seg.arrivals(i, q))
                    if not isinstance(i, int):
                        act.wait_ge(unit_done, seg.unit(i, q) - 1)
                    elif seg.split_no(i, q) >= 2:
                        act.wait_ge(unit_done, split_units[seg.split_no(i, q) - 2] + 1)
                    nc.scalar.activation(w_hi[r][:, 0:seg.kc, :], panel_part(seg, q), ACT.Copy).then_inc(S["hi_done"], 1)
                return step

            def up(seg, before):
                def step(i, q):
                    k, j = divmod(q, 2)
                    if k % 2:
                        return
                    b = seg.bank(q)
                    act.wait_ge(unit_done, seg.unit(i, q) + 1)
                    if not isinstance(i, int) or i > 0:
                        act.wait_ge(S["h_split"], i * 4 + (before + k + j - 3))
                    nc.scalar.activation(ff_a[:, k + j, :], banks[b][:, 0:T], ACT.Silu).then_inc(bank_free[b], 1)
                walk(act, seg, step, high(seg), None, 0, LAG)
            u_high(0)
            up(segs["up1"], 0)
            walk(act, segs["down1"], high(segs["down1"]))
            act.wait_ge(S["res_done"], KD)
            square(1)
            root(1)
            u_high(1)
            act.wait_ge(S["gate_mm"], 1)
            nc.scalar.activation(xg[0:40, :], aux[1][0:40, 0:T], ACT.Identity, bias=gate_sb[:, 2:3], scale=gate_sb[:, 1:2])\
                .then_inc(S["gate_lin"], 1)

            def conv(seg, first, padded, accs, dst):
                def silu(i, q):
                    c = seg.own(i, q)
                    a = accs[:, q % 4, :]
                    act.wait_ge(S["conv_done"], c + (first + 1))
                    nc.scalar.activation(dst[:, bass.ds(c, 1), 0:TP], accs[:, q % 4:q % 4 + 1, 0:TP], ACT.Silu)
                    nc.scalar.activation(dst[:, bass.ds(c, 1), TP:].rearrange("p o (b t) -> p (o b) t", t=ST),
                                         convolved_samples(a), ACT.Silu).then_inc(S["conv_silu"], 1)

                def step(i, q):
                    b, r, c = seg.bank(q), q % 4, seg.own(i, q)
                    act.wait_ge(unit_done, seg.unit(i, q) + 1)
                    if not isinstance(i, int) or seg.gu * i + q >= 4:
                        act.wait_ge(S["conv_done"], c + (first - 3))
                        act.wait_ge(S["tails_saved"], c + (first - 3))
                    elif q == 0:
                        act.wait_ge(S["pad_zero"], 1 if first == 0 else 2)
                    copy(padded[:, r, HIST:HIST + TP], banks[b][:, 0:TP])
                    copy(padded[:, r, HIST + TP:].rearrange("p (b w) -> p b w", w=HIST + ST)[:, :, HIST:],
                         sequences(banks[b][:, TP:T])).then_inc(bank_free[b], 1)
                    if not isinstance(i, int) or i + q > 0:
                        silu(i + (q - 1) // seg.gu, (q - 1) % seg.gu)
                walk(act, seg, step, high(seg), None, 0, LAG)
                silu(*seg.at(seg.units - 1))

            conv(segs["qk"], 0, pad, acc, qk_t)

            act.wait_ge(S["sp_abs"], 1)
            ch.link(nc.scalar.activation(soft_e[:, :], soft_a[:, :], ACT.Exp, scale=-1.0))
            nc.scalar.activation(soft_l[:, :], soft_e[:, :], ACT.Ln, bias=1.0).then_inc(S["sp_exp"], 1)

            vs = segs["v"]

            def v_row(i, q):
                b, r = vs.bank(q), q % 4
                act.wait_ge(unit_done, vs.unit(i, q) + 1)
                if not isinstance(i, int) or vs.gu * i + q >= 4:
                    act.wait_ge(S["v_turned"], vs.own(i, q) - 3)
                copy(v_tmp[:, r, :], banks[b][:, 0:T]).then_inc(bank_free[b], 1)
            act.wait_ge(S["conv_silu"], 16)
            walk(act, vs, v_row, high(vs), None, 0, LAG)

            def copy_tails(first_round, rounds):
                for n in range(first_round, first_round + rounds):
                    x = aux[3 if n < 4 else n % 2]
                    act.wait_ge(S["tail_tr"], n + 1)
                    if n >= 2:
                        act.wait_ge(tail_sent[n % 2], 32 * (n // 2))
                    copy(tail_out[n < 4][0:27, n % 2, :], x[0:27, :]).then_inc(S["tail_cp"], 1)
            copy_tails(0, 4)

            act.wait_ge(S["mt_ready"], 1)
            for h in range(MH):
                for c, (lo, hi, n) in enumerate(((0, 128, 128), (128, 384, 128), (384, 448, 64))):
                    ch.inc(nc.scalar.activation(dm[0:n, h, lo:hi], dm[0:n, h, lo:hi], ACT.Exp, bias=sm[0:n, 5, 12 + 4 * c + h:13 + 4 * c + h]))
            ch.inc(nc.scalar.activation(sm[:, 5, 24:36], sm[:, 5, 0:12], ACT.Exp))
            nc.scalar.activation(sm[:, 6, 16:28], sm[:, 5, 12:24], ACT.Exp).then_inc(S["wtok_ready"], 1)
            act.wait_ge(S["ws_arg"], 1)
            ch.inc(nc.scalar.activation(sm[:, 10, 0:12], sm[:, 10, 0:12], ACT.Exp))
            nc.scalar.activation(dec[:, :], dec[:, :], ACT.Exp).then_inc(S["ws_exp"], 1)
            for r in range(2):
                act.wait_ge(tail_sent[r], 64)
            for h in range(MH):
                act.wait_ge(S["st_mm"], h + 1)
                ch.inc(copy(st_s[:, h, 0:384], aux[h][:, 0:384]))
                copy(st_s[0:64, h, 384:448], aux[h][0:64, 384:448]).then_inc(S["st_copied"], 1)
            act.wait_ge(S["n_tr"], 1)
            ch.inc(copy(n_rows2[0:8, 0:512], banks[1][0:8, :]))
            ch.inc(copy(n_rows2[0:8, 512:1024], banks[2][0:8, :]))
            copy(n_rows2[0:8, 1024:1152], banks[3][0:8, 0:128]).then_inc(S["n_row"], 2)
            for h in range(MH):
                for d in range(2):
                    n = 2 * h + d
                    act.wait_ge(S["pc_mm"], n + 1)
                    act.wait_ge(state_out[h], 16 * SB)
                    copy(cb[:, h, d * DV:(d + 1) * DV], banks[n % 4][:, :]).then_inc(S["pc_copied"], 1)
            for h in range(MH):
                nm = (num, num2)[h % 2]
                act.wait_ge(S["num_mm"], h + 1)
                if h >= 2:
                    act.wait_ge(S["hn_turned"], 4 * (h - 1))
                if h >= 1:
                    act.wait_ge(S["num_whole"], h)
                ch.inc(copy(nm[:, 0, :], banks[0][:, :]))
                ch.inc(copy(nm[:, 1, :], banks[1][:, :]))
                copy(t1[0:64, :], aux[h][64:128, :], scale=sm[0:64, 5, 32 + h:33 + h]).then_inc(S["t1_ready"], 1)
                act.wait_ge(S["var_ready"], h + 1)
                nc.scalar.activation(coef[:, :, 0], coef[:, :, 0], ACT.Sqrt).then_inc(S["std_ready"], 1)
                act.wait_ge(S["norm_coef"], h + 1)
                for c, n in enumerate((128, 128, 64)):
                    ins = nc.scalar.activation(nm[0:n, c, :], nm[0:n, c, :], ACT.Identity, bias=coef[0:n, c, 1:2], scale=coef[0:n, c, 0:1])
                    if c < 2:
                        ch.inc(ins)
                ins.then_inc(S["hn_ready"], 1)

            def gate(seg, func, count0, tmp, dst=None):
                def step(i, q):
                    b, r = seg.bank(q), q % 4
                    act.wait_ge(unit_done, seg.unit(i, q) + 1)
                    if dst is None:
                        if not isinstance(i, int) or seg.gu * i + q >= 4 or count0:
                            act.wait_ge(S["gate_used"], seg.own(i, q) + (count0 - 3))
                        o = tmp[:, r:r + 1, :]
                    else:
                        o = dst[:, bass.ds(seg.own(i, q), 1), :]
                    nc.scalar.activation(o, banks[b][:, None, 0:T], func).then_inc(bank_free[b], 1)
                walk(act, seg, step, high(seg), None, 0, LAG)
            gate(segs["mo"], ACT.Sigmoid, 0, gate_tmp_m)

            def pa_row(i, q):
                if q % 2 == 0:
                    return
                b = segs["pa"].bank(q)
                act.wait_ge(unit_done, segs["pa"].unit(i, q) + 1)
                copy(ya[:, bass.ds(segs["pa"].own(i, q), 1), :], banks[b][:, None, 0:T]).then_inc(bank_free[b], 1)
            for h in range(MH):
                act.wait_ge(state_out[h], 16 * (SB + 1))
            walk(act, segs["pa"], pa_row, high(segs["pa"]), None, 0, LAG)
            conv(segs["xbc"], 16, pad2, acc2, xbc_t)
            copy_tails(4, 6)

            for c in range(3):
                n = 128 if c < 2 else 64
                act.wait_ge(S["bt_mm"], c + 1)
                copy(bt[0:n, c, :], aux[c][0:n, :]).then_inc(S["bt_read"], 1)
            act.wait_ge(S["lastx_read"], 1)
            ch.inc(nc.scalar.activation(sp2[:, :, :], sp2[:, :, :], ACT.Exp))
            nc.scalar.activation(sm[:, 8, 0:32], cum[:, 2, 4:36], ACT.Exp).then_inc(S["decx_ready"], 1)
            for q in range(8):
                act.wait_ge(S["t_ready"], 4 * (q + 1))
                w = w_int[:, q % 2, :].rearrange("p (j s) -> p j s", s=448)
                ch.inc(nc.scalar.activation(w[:, :, 0:384], w[:, :, 0:384], ACT.Exp))
                nc.scalar.activation(w[0:64, :, 384:448], w[0:64, :, 384:448], ACT.Exp).then_inc(S["w_exp"], 1)
            for gr in range(SG):
                act.wait_ge(S["ph_mm"], gr + 1)
                copy(h_t[:, gr * 512:(gr + 1) * 512], banks[gr][:, :]).then_inc(S["ph_copied"], 1)
            act.wait_ge(row_sent, 16)

            def turned_state(i, r, first):
                b = i * 2 + r
                for gr in range(SG):
                    act.wait_ge(S["ht_mm"], b * 4 + (gr + 1))
                    if gr == 0 and not first:
                        act.wait_ge(S["yi_mm"], b)
                    copy(h_t[:, gr * 512:(gr + 1) * 512], aux[gr % 2][:, :]).then_inc(S["ht_read"], 1)
            turned_state(0, 0, True)
            turned_state(0, 1, False)
            with act.Fori(1, SB // 2) as i:
                turned_state(i, 0, False)
                turned_state(i, 1, False)
            gate(segs["z"], ACT.Silu, 16, gate_tmp)
            for gr in range(SG):
                act.wait_ge(S["gate_used"], 32)
                if gr == 0:
                    for r in range(2):
                        act.wait_ge(state_out[r], 16 * (SB + 1) + 16 * (SB // 2))
                if gr >= 2:
                    act.wait_ge(S["gss_done"], gr - 1)
                nc.scalar.activation(gsq[:, gr % 2, :], xbc_t[:, 4 * gr:4 * gr + 4, :].rearrange("p a b -> p (a b)"), ACT.Square)\
                    .then_inc(S["gsq_ready"], 1)
            for gr in range(SG):
                act.wait_ge(S["gss_done"], gr + 1)
                nc.scalar.activation(g_root[:, gr, :], aux[gr][:, 0:T], ACT.Sqrt, bias=eps_col[:, 0:1], scale=1.0 / 512).then_inc(S["grs_ready"], 1)
            gate(segs["ga"], ACT.Sigmoid, 32, gate_tmp)
            gate(segs["gb"], ACT.Sigmoid, 40, None, merged_g)
            for name in ("pb", "out"):
                walk(act, segs[name], high(segs[name]))
            act.wait_ge(S["res_done"], 2 * KD)
            square(2)
            root(2)
            u_high(2)
            up(segs["up2"], KF)
            walk(act, segs["down2"], high(segs["down2"]))
            act.wait_ge(S["res_done"], 3 * KD)
            square(3)
            root(3)
            for n in range(6):
                c, half = divmod(n, 2)
                rows = 128 if c < 2 else 64
                act.wait_ge(S["fin_tr"], n + 1)
                copy(y_rows[0:rows, c, half * 512:(half + 1) * 512], aux[1 + n % 2][0:rows, :]).then_inc(S["fin_cp"], 1)

        @block.vector
        def _(dve):
            ch = Chain(dve, S["dve_chain"])
            V = nc.vector
            ch.inc(V.memset(eps_col[:, :], EPS))
            dve.wait_ge(S["params_in"], 26 * 16)
            ch.inc(V.memset(gate_sb[:, 1:2], 1.0))
            ch.settle()
            ch.link(V.memset(gate_sb[0:8, 1:2], -1.0))
            ch.link(V.tensor_tensor(gate_sb[:, 2:3], gate_sb[:, 0:1], gate_sb[:, 1:2], ALU.mult))
            dve.wait_ge(S["packs_read"], 1)

            ada = segs["ada"]

            def mod_read(i, k):
                p, r = ada.own(i, k), k % 2
                dve.wait_ge(S["mod_turned"], p + 1)
                V.tensor_tensor(mod[:, bass.ds(p * 2, 2), :], aux[r][:, 0:2 * NSEQ].rearrange("p (j s) -> p j s", s=NSEQ),
                                bias_of(p), ALU.add).then_inc(S["mod_read"], 1)

            def bias_of(p):
                return par[:, None, bass.ds(p * 2, 2)].rearrange("p o c -> p c o").to_broadcast([128, 2, NSEQ])
            walk(dve, ada, mod_read)
            dve.wait_ge(S["mod_read"], ada.tiles)

            def mod_of(q):
                return mod[:, q * KD:(q + 1) * KD, :]

            def per_token(ap):
                return ap[:, :, 1:NSEQ].unsqueeze(3).to_broadcast([128, KD, SB, ST])

            def samples(ap):
                return ap[:, :, TP:T].rearrange("p k (b t) -> p k b t", t=ST)

            def modulated(n, shift, scale, norm_col):
                g = par[:, norm_col:norm_col + KD].unsqueeze(2).to_broadcast([128, KD, NSEQ])
                ch.link(V.scalar_tensor_tensor(out=gain[:, :, :], in0=mod_of(scale), scalar=1.0, in1=g, op0=ALU.add, op1=ALU.mult))
                dve.wait_ge(S["root_ready"], n + 1)
                ch.link(V.reciprocal(rs[:, :], rs[:, :]))
                ch.link(V.tensor_tensor(u_t[:, :, :], x_t[:, :, :], rs[:, None, :].to_broadcast([128, KD, T]), ALU.mult))
                for kc in range(KD):
                    ch.inc(V.tensor_scalar(u_t[:, kc, 0:TP], u_t[:, kc, 0:TP], gain[:, kc, 0:1], mod_of(shift)[:, kc, 0:1], ALU.mult, ALU.add))
                ch.link(V.tensor_tensor(samples(u_t), samples(u_t), per_token(gain), ALU.mult))
                V.tensor_tensor(samples(u_t), samples(u_t), per_token(mod_of(shift)), ALU.add).then_inc(S["u_ready"], 1)
                dve.wait_ge(S["u_hi_ready"], n + 1)
                V.tensor_tensor(u_lo[:, :, :], u_t[:, :, :], u_hi[:, :, :].bitcast(FP32), ALU.subtract).then_inc(S["u_lo_ready"], 1)

            def low(seg):
                def step(i, q):
                    r = (seg.s0 + q) % 2
                    dve.wait_ge(S["hi_done"], seg.split_no(i, q) + 1)
                    V.tensor_tensor(w_lo[r][:, 0:seg.kc, :], panel_part(seg, q), w_hi[r][:, 0:seg.kc, :].bitcast(FP32), ALU.subtract)\
                        .then_inc(S["lo_done"], 1)
                return step

            def halves(high, low, c, src, signal):
                hi, lo = high[:, bass.ds(c, 1), :], low[:, bass.ds(c, 1), :]
                ch.link(V.tensor_copy(hi, src))
                V.tensor_tensor(lo, src, hi.bitcast(FP32), ALU.subtract).then_inc(S[signal], 1)

            def up(seg):
                base = ch.n

                def step(i, q):
                    k, j = divmod(q, 2)
                    if k % 2 == 0:
                        return
                    b = seg.bank(q)
                    dve.wait_ge(bank_free[seg.bank(q - 2)], seg.bank_use(i, q - 2) + 1)
                    dve.wait_ge(unit_done, seg.unit(i, q) + 1)
                    a = ff_a[:, k - 1 + j:k + j, :]
                    V.tensor_tensor(a, banks[b][:, None, 0:T], a, ALU.mult).then_inc(bank_free[b], 1)
                    dve.wait_ge(bank_free[b], seg.bank_use(i, q) + 1)
                    ch.n = base + i * 4 + (k - 1 + j)
                    halves(ff_hi, ff_lo, i * 4 + (k - 1 + j), a, "h_split")
                walk(dve, seg, step, low(seg), None, 0, LAG)
                ch.n = base + KF

            def residual(seg, gate_mod, factor, count0):
                ch.link(V.tensor_scalar(half_g[:, :, :], mod_of(gate_mod), factor, None, ALU.mult))
                base = ch.n

                def step(i, q):
                    if q % seg.parts != seg.parts - 1:
                        return
                    kc, b = seg.own(i, q), seg.bank(q)
                    r = q // seg.parts % 4
                    ch.n = base + kc
                    dve.wait_ge(unit_done, seg.unit(i, q) + 1)
                    x1 = x_t[:, bass.ds(kc, 1), 0:TP]
                    ch.inc(V.scalar_tensor_tensor(out=x1, in0=banks[b][:, None, 0:TP], scalar=half_g[:, bass.ds(kc, 1), 0:1].rearrange("p a b -> p (a b)"),
                                                  in1=x1, op0=ALU.mult, op1=ALU.add))
                    V.tensor_tensor(sequences(res_tmp[:, r, :]), sequences(banks[b][:, TP:T]),
                                    half_g[:, bass.ds(kc, 1), 1:NSEQ].rearrange("p o b -> p (o b)").unsqueeze(2).to_broadcast([128, SB, ST]),
                                    ALU.mult).then_inc(bank_free[b], 1)
                    dve.wait_ge(bank_free[b], seg.bank_use(i, q) + 1)
                    x2 = x_t[:, bass.ds(kc, 1), TP:T]
                    V.tensor_tensor(x2, x2, res_tmp[:, r:r + 1, :], ALU.add).then_inc(S["res_done"], 1)
                    dve.wait_ge(S["res_done"], kc + (count0 + 1))
                walk(dve, seg, step, low(seg), None, 0, LAG)
                ch.n = base + seg.tiles

            modulated(0, 0, 1, 72)
            up(segs["up1"])
            residual(segs["down1"], 2, 0.5, 0)
            modulated(1, 3, 4, 80)

            def conv(seg, first, padded, accs, b_col, w_col, tiles):
                def step(i, q):
                    r, c = q % 4, seg.own(i, q)
                    dve.wait_ge(bank_free[seg.bank(q)], seg.bank_use(i, q) + 1)
                    dve.wait_ge(S["hist_put"], c + (first + 1))
                    if not isinstance(i, int) or seg.gu * i + q >= 4:
                        dve.wait_ge(S["conv_silu"], c + (first - 3))
                    a, p = accs[:, r, 0:CONVW], padded[:, r, :]
                    ch.link(V.tensor_scalar(a, p[:, 0:CONVW], par[:, bass.ds(c + w_col, 1)], par[:, bass.ds(c + b_col, 1)], ALU.mult, ALU.add))
                    for tap in (1, 2):
                        ch.link(V.scalar_tensor_tensor(out=a, in0=p[:, tap:tap + CONVW], scalar=par[:, bass.ds(c + (w_col + tap * tiles), 1)],
                                                       in1=a, op0=ALU.mult, op1=ALU.add))
                    V.scalar_tensor_tensor(out=a, in0=p[:, 3:3 + CONVW], scalar=par[:, bass.ds(c + (w_col + 3 * tiles), 1)],
                                           in1=a, op0=ALU.mult, op1=ALU.add).then_inc(S["conv_done"], 1)
                walk(dve, seg, step, low(seg), ch, 3, LAG)
            conv(segs["qk"], 0, pad, acc, 104, 120, 16)

            dve.wait_ge(S["gate_tr"], 1)
            ch.inc(V.tensor_copy(g3[:, 0:2, :], aux[2][:, 0:80].rearrange("p (c g) -> p c g", g=40)))
            ch.link(V.tensor_copy(g3[0:64, 2, :], aux[2][0:64, 80:120]))
            gx = g3[:, :, 4:40]

            def f3(t):
                return t[:, :].rearrange("p (c g) -> p c g", g=36)
            ch.inc(V.tensor_scalar(sp[:, :, :], gx, 0.0, None, ALU.max))
            V.scalar_tensor_tensor(out=f3(soft_a), in0=gx, scalar=-1.0, in1=gx, op0=ALU.mult, op1=ALU.max).then_inc(S["sp_abs"], 1)

            vs = segs["v"]

            def v_read(i, q):
                x = aux[q % 2]
                c = vs.own(i, q)
                dve.wait_ge(S["v_turned"], c + 1)
                ch.inc(V.tensor_copy(v_tok[:, 0:2, bass.ds(c * 128, 128)], x[:, 0:256].rearrange("p (c n) -> p c n", n=128)))
                V.tensor_copy(v_tok[0:64, 2:3, bass.ds(c * 128, 128)], x[0:64, None, 256:384]).then_inc(S["v_copied"], 1)
            walk(dve, vs, v_read, low(vs), ch, 1, LAG + 1)

            dve.wait_ge(S["sp_exp"], 1)
            ch.link(V.tensor_scalar(soft_a[:, :], soft_e[:, :], 1.0, None, ALU.add))
            ch.inc(V.reciprocal(soft_r[:, :], soft_a[:, :]))
            ch.link(V.scalar_tensor_tensor(out=soft_e[:, :], in0=soft_a[:, :], scalar=-1.0, in1=soft_e[:, :], op0=ALU.add, op1=ALU.subtract))
            ch.link(V.scalar_tensor_tensor(out=soft_e[:, :], in0=soft_e[:, :], scalar=-1.0, in1=soft_r[:, :], op0=ALU.mult, op1=ALU.mult))
            ch.link(V.tensor_tensor(soft_l[:, :], soft_l[:, :], soft_e[:, :], ALU.add))
            ch.link(V.tensor_tensor(sp[:, :, :], sp[:, :, :], f3(soft_l), ALU.add))
            ch.inc(V.tensor_scalar(al[:, :, 0:4], sp[:, :, 0:4], -1.0, None, ALU.mult))
            V.scalar_tensor_tensor(out=al[:, :, 4:36], in0=sp[:, :, 4:36], scalar=-1.0, in1=a_neg[:, None, :].to_broadcast([128, 3, SH]),
                                   op0=ALU.mult, op1=ALU.mult).then_inc(S["al_ready"], 1)
            dve.wait_ge(S["cum_mm"], 1)
            inter = sm[:, 3, 0:12].rearrange("p (c h) -> p c h", h=MH)
            mx = sm[:, 3, 12:24].rearrange("p (c h) -> p c h", h=MH)
            mt = sm[:, 3, 24:36].rearrange("p (c h) -> p c h", h=MH)
            ch.inc(V.tensor_copy(cum[:, :, :], aux[2][:, 0:108].rearrange("p (c g) -> p c g", g=36)))
            ch.link(V.tensor_copy(sm[0:64, 9, 24:28], aux[2][0:64, 108:112]))
            ch.inc(V.tensor_copy(inter[:, 0:2, :], cum[:, 0:2, 0:4]))
            ch.inc(V.tensor_tensor(inter[:, 2, :], cum[:, 2, 0:4], sm[:, 9, 24:28], ALU.add))
            V.scalar_tensor_tensor(out=sm[:, 0:3, 0:4], in0=g3[:, :, 0:4], scalar=-1.0, in1=cum[:, :, 0:4], op0=ALU.mult, op1=ALU.subtract)\
                .then_inc(S["g_ready"], 1)
            for h in range(MH):
                dve.wait_ge(S["gb_mm"], h + 1)
                x = aux[h]
                ch.inc(V.scalar_tensor_tensor(out=dm[:, h, 0:128], in0=x[:, 0:128], scalar=cum[:, 0, h:h + 1], in1=neg_p[:, :], op0=ALU.add, op1=ALU.add))
                ch.inc(V.tensor_scalar(dm[:, h, 128:256], x[:, 0:128], cum[:, 1, h:h + 1], None, ALU.add))
                ch.inc(V.scalar_tensor_tensor(out=dm[:, h, 256:384], in0=x[:, 128:256], scalar=cum[:, 1, h:h + 1], in1=neg_p[:, :], op0=ALU.add, op1=ALU.add))
                ch.inc(V.scalar_tensor_tensor(out=dm[0:64, h, 384:448], in0=x[0:64, 256:320], scalar=cum[0:64, 2, h:h + 1], in1=neg_s[:, :], op0=ALU.add, op1=ALU.add))
            ch.settle()
            ch.inc(V.tensor_reduce(mx[:, 0, :], dm[:, :, 0:128], AX.X, ALU.max))
            ch.inc(V.tensor_reduce(mx[:, 1, :], dm[:, :, 128:384], AX.X, ALU.max))
            ch.link(V.tensor_reduce(mx[0:64, 2, :], dm[0:64, :, 384:448], AX.X, ALU.max))
            ch.link(V.tensor_tensor(mt, inter, mx, ALU.max))
            ch.inc(V.tensor_tensor(sm[:, 5, 0:12], sm[:, 3, 0:12], sm[:, 3, 24:36], ALU.subtract))
            V.tensor_scalar(sm[:, 5, 12:24], sm[:, 3, 24:36], -1.0, None, ALU.mult).then_inc(S["mt_ready"], 1)
            bm = sm[:, 4, 0:24].rearrange("p (c g) -> p c g", g=8)
            ch.inc(V.tensor_copy(bm[:, :, 0:4], cum[:, :, 0:4]))
            ch.link(V.tensor_copy(bm[:, :, 4:8], mt))
            V.tensor_tensor(al2[:, :].rearrange("p (b g) -> p b g", g=8), sm[0:64, 4, 16:24].unsqueeze(1).to_broadcast([64, SB, 8]),
                            last_b[:, :].unsqueeze(2).to_broadcast([64, SB, 8]), ALU.mult).then_inc(S["bmx_ready"], 1)
            dve.wait_ge(S["last_mm"], 1)
            ch.inc(V.tensor_copy(sm[:, 6, 0:8], banks[0][:, 0:8]))
            ch.inc(V.tensor_copy(sm[0:64, 6, 8:16], banks[0][0:64, 8:16]))
            ch.link(V.tensor_copy(lb[:, :, :], banks[0][:, 16:80].rearrange("p (b g) -> p b g", g=8)))
            ch.inc(V.tensor_tensor(sm[:, 9, 28:32], sm[:, 6, 0:4], sm[:, 6, 4:8], ALU.subtract))
            ch.inc(V.tensor_tensor(sm[:, 9, 32:36], sm[:, 6, 8:12], sm[:, 6, 12:16], ALU.subtract))
            ch.inc(V.tensor_copy(sm[:, 11, 0:32].rearrange("p (b h) -> p b h", h=MH), lb[:, :, 4:8]))
            ch.link(V.tensor_tensor(dec[:, :].rearrange("p (b h) -> p b h", h=MH), lb[:, :, 0:4], lb[:, :, 4:8], ALU.subtract))
            ch.inc(V.tensor_tensor(dec[:, :], dec[:, :], m0_b[:, :], ALU.add))
            w3 = sm[:, 10, 0:12].rearrange("p (c h) -> p c h", h=MH)
            ch.inc(V.tensor_tensor(w3[:, 0:2, :], sm[:, 0:2, 0:4], sm[:, 9, 28:32].unsqueeze(1).to_broadcast([128, 2, MH]), ALU.add))
            V.tensor_tensor(w3[:, 2, :], sm[:, 2, 0:4], sm[:, 9, 32:36], ALU.add).then_inc(S["ws_arg"], 1)
            dve.wait_ge(S["wtok_ready"], 1)
            for h in range(MH):
                dve.wait_ge(S["qk_mm"], h + 1)
                for c, (lo, hi, n) in enumerate(((0, 128, 128), (128, 384, 128), (384, 448, 64))):
                    ins = V.scalar_tensor_tensor(out=dm[0:n, h, lo:hi], in0=aux[h][0:n, lo:hi], scalar=DK ** -0.5, in1=dm[0:n, h, lo:hi],
                                                 op0=ALU.mult, op1=ALU.mult, accum_out=sm[0:n, 7, 8 + 4 * c + h:9 + 4 * c + h])
                    if c < 2:
                        ch.inc(ins)
                ins.then_inc(S["s_ready"], 1)
            dve.wait_ge(S["ws_exp"], 1)
            V.tensor_scalar(sm[:, 10, 0:12], sm[:, 10, 0:12], DK ** -0.5, None, ALU.mult).then_inc(S["ws_ready"], 1)
            dve.wait_ge(S["ws_ready"], 1)
            for c in range(8):
                h, b = c // 2, banks[c % 4]
                dve.wait_ge(S["kt_mm"], c + 1)
                for blk, n in ((0, 128), (1, 128), (2, 64)):
                    ins = V.tensor_scalar(kw[0:n, blk, c * 128:(c + 1) * 128], b[0:n, blk * 128:(blk + 1) * 128],
                                          sm[0:n, 10, 4 * blk + h:4 * blk + h + 1], None, ALU.mult)
                    if blk < 2:
                        ch.inc(ins)
                ins.then_inc(S["kt_read"], 1)
            dve.wait_ge(S["tails_saved"], 16)
            dve.wait_ge(S["st_mm"], MH)
            V.tensor_tensor(acc_q[:, :, :].rearrange("p k (b t) -> p k b t", t=ST),
                            qk_t[:, 0:8, TP:T].rearrange("p k (b t) -> p k b t", t=ST),
                            n_t[:, :, :].unsqueeze(3).to_broadcast([128, 8, SB, ST]), ALU.mult).then_inc(S["qn_prod"], 1)
            dve.wait_ge(S["n_mm"], 1)
            ch.inc(V.tensor_copy(sm[0:64, 7, 20:24], banks[0][0:64, 0:4]))
            ch.inc(V.tensor_copy(sm[:, 7, 0:8], banks[0][:, 80:88]))
            nt4 = n_t[:, :, :].rearrange("p (h d) b -> p h d b", d=2)
            dve.wait_ge(S["qn_prod"], 1)
            ch.link(V.tensor_tensor(nt4, nt4, dec[:, :].rearrange("p (b h) -> p h b", h=MH).unsqueeze(2).to_broadcast([128, MH, 2, SB]), ALU.mult))
            V.tensor_tensor(n_t[:, :, :], n_t[:, :, :], banks[0][:, 8:72].rearrange("p (c b) -> p c b", b=SB), ALU.add).then_inc(S["n_new"], 1)
            ch.link(V.tensor_tensor(sm[0:64, 7, 24:28], sm[0:64, 7, 20:24], sm[0:64, 5, 32:36], ALU.mult))
            ch.link(V.tensor_tensor(sm[0:64, 7, 16:20], sm[0:64, 7, 16:20], sm[0:64, 7, 24:28], ALU.add))
            ch.link(V.scalar_tensor_tensor(out=sm[:, 9, 0:12], in0=sm[:, 7, 8:20], scalar=-1.0, in1=sm[:, 7, 8:20], op0=ALU.mult, op1=ALU.max))
            ch.link(V.tensor_tensor(sm[:, 9, 0:12], sm[:, 9, 0:12], sm[:, 6, 16:28], ALU.max))
            ch.link(V.reciprocal(sm[:, 9, 0:12], sm[:, 9, 0:12]))
            ch.link(V.tensor_tensor(sm[:, 9, 12:24], sm[:, 9, 0:12], sm[:, 9, 0:12], ALU.mult))

            def masks(b, h, first):
                n = b * MH + h
                if not first:
                    dve.wait_ge(S["state_mm"], n - (MH - 1))
                ch.inc(V.tensor_scalar(kwm[0:64, h, :], kw[0:64, 2, h * DK:(h + 1) * DK], seg_m[:, bass.ds(b, 1)], None, ALU.mult))
                V.tensor_tensor(qm[:, h, :, :], qk_t[:, 2 * h:2 * h + 2, TP:T], seg_b[:, bass.ds(b, 1), :].to_broadcast([128, 2, TS]), ALU.mult)\
                    .then_inc(S["masks_ready"], 1)

            def update(b, h):
                n = b * MH + h
                dve.wait_ge(S["state_mm"], n + 1)
                for d in range(2):
                    c_h = cb[:, h, d * DV:(d + 1) * DV]
                    ins = V.scalar_tensor_tensor(out=c_h, in0=c_h, scalar=dec[:, bass.ds(n, 1)], in1=banks[2 * (h % 2) + d][:, :], op0=ALU.mult, op1=ALU.add)
                    if d == 0:
                        ch.inc(ins)
                ins.then_inc(S["c_updated"], 1)
            for h in range(MH):
                masks(0, h, True)
            base = ch.n
            with dve.Fori(0, SB - 1) as b:
                ch.n = base + b * (2 * MH)
                for h in range(MH):
                    update(b, h)
                    masks(b + 1, h, False)
            ch.n = base + (SB - 1) * 2 * MH
            for h in range(MH):
                update(SB - 1, h)

            for h in range(MH):
                nm = (num, num2)[h % 2]
                dve.wait_ge(S["t1_ready"], h + 1)
                ch.link(V.scalar_tensor_tensor(out=t2[0:64, :], in0=aux[h][0:64, :], scalar=sm[0:64, 5, 32 + h:33 + h], in1=t1[0:64, :], op0=ALU.mult, op1=ALU.add))
                V.tensor_tensor(nm[0:64, 2, :], banks[2][0:64, :], t2[0:64, :], ALU.add).then_inc(S["num_whole"], 1)
                dve.wait_ge(S["num_whole"], h + 1)
                for c, n in enumerate((128, 128, 64)):
                    ch.inc(V.bn_stats(stats[0:n, c, :], nm[0:n, c, :]))
                ch.settle()
                for c, n in enumerate((128, 128, 64)):
                    ch.inc(V.bn_aggr(mean_var[0:n, c, :], stats[0:n, c, :]))
                ch.settle()
                rd = sm[:, 9, 0:12].rearrange("p (c h) -> p c h", h=MH)[:, :, h]
                rd2 = sm[:, 9, 12:24].rearrange("p (c h) -> p c h", h=MH)[:, :, h]
                ch.link(V.tensor_tensor(coef[:, :, 0], mean_var[:, :, 1], rd2, ALU.mult))
                V.tensor_scalar(coef[:, :, 0], coef[:, :, 0], EPS, None, ALU.add).then_inc(S["var_ready"], 1)
                dve.wait_ge(S["std_ready"], h + 1)
                ch.link(V.reciprocal(coef[:, :, 0], coef[:, :, 0]))
                ch.link(V.tensor_tensor(coef[:, :, 0], coef[:, :, 0], rd, ALU.mult))
                V.scalar_tensor_tensor(out=coef[:, :, 1], in0=mean_var[:, :, 0], scalar=-1.0, in1=coef[:, :, 0], op0=ALU.mult, op1=ALU.mult)\
                    .then_inc(S["norm_coef"], 1)
                if h == 1:
                    for m in range(MH):
                        dve.wait_ge(state_out[m], 16 * (SB + 1))
                for j in range(4):
                    c = 4 * h + j
                    dve.wait_ge(S["hn_turned"], c + 1)
                    V.tensor_scalar(hm[:, c, :], aux[h][:, 0:T], par[:, 184 + c:185 + c], None, ALU.mult).then_inc(S["hn_read"], 1)

            def gated(seg, dst, tmp, split=False, now=None):
                def step(i, q):
                    dve.wait_ge(bank_free[seg.bank(q)], seg.bank_use(i, q) + 1)
                    own = seg.own(i, q)
                    c = dst[:, bass.ds(own, 1), :]
                    V.tensor_tensor(c, c, tmp[:, q % 4:q % 4 + 1, :], ALU.mult).then_inc(S["gate_used"], 1)
                    if split:
                        dve.wait_ge(S["gate_used"], own + 1)
                        halves(y_hi, y_lo, own, c, "y_split")
                walk(dve, seg, step, now or low(seg), *((ch, 1) if split else (None, 0)), LAG)
            dve.wait_ge(S["hn_read"], 16)
            dve.wait_ge(small_out, 64)
            gated(segs["mo"], hm, gate_tmp_m, split=True)
            walk(dve, segs["pa"], low(segs["pa"]))
            conv(segs["xbc"], 16, pad2, acc2, 216, 240, 24)

            for n in range(12):
                gr, c = divmod(n, 3)
                rows = 128 if c < 2 else 64
                dve.wait_ge(S["xt_mm"], n + 1)
                V.tensor_tensor(xd[0:rows, c, gr * 512:(gr + 1) * 512].rearrange("p (e q) -> p e q", q=64),
                                banks[n % 4][0:rows, :].rearrange("p (e q) -> p e q", q=64),
                                sp[0:rows, c, 4 + 8 * gr:12 + 8 * gr].unsqueeze(2).to_broadcast([rows, 8, 64]), ALU.mult).then_inc(S["xt_read"], 1)
            for gr in range(SG):
                dve.wait_ge(S["cb_mm"], gr + 1)
                ch.inc(V.tensor_tensor(cbm[:, gr, 0:384], banks[gr][:, 0:384], tri[:, :], ALU.mult))
                V.tensor_tensor(cbm[0:64, gr, 384:448], banks[gr][0:64, 384:448], tri_s[:, 0:64], ALU.mult).then_inc(S["cb_read"], 1)
            dve.wait_ge(S["lastx_mm"], 1)
            ch.inc(V.tensor_tensor(sp2[:, 0:2, :], aux[3][:, 0:32].unsqueeze(1).to_broadcast([128, 2, SH]), cum[:, 0:2, 4:36], ALU.subtract))
            ch.inc(V.memset(sp2[64:128, 2, :], 0.0))
            V.tensor_tensor(sp2[0:64, 2, :], aux[3][0:64, 32:64], cum[0:64, 2, 4:36], ALU.subtract).then_inc(S["lastx_read"], 1)
            dve.wait_ge(S["hd_mm"], 1)
            ch.inc(V.tensor_tensor(hd_in[:, 0:128].rearrange("p (t b) -> p t b", b=SB), aux[3][0:32, 64:72].unsqueeze(1).to_broadcast([SH, 16, SB]),
                                   tile_of_head[:, :].unsqueeze(2).to_broadcast([SH, 16, SB]), ALU.mult))
            ch.inc(V.tensor_reduce(parity2[:, :], ident[0:32, 0:32].rearrange("p (t e) -> p e t", e=2), AX.X, ALU.add))
            ch.link(V.tensor_scalar(hd_in[:, 128:144], tile_of_head[:, :], d_col[:, 0:1], None, ALU.mult))
            V.tensor_copy(parity[:, :, :], parity2[:, :].unsqueeze(2).to_broadcast([SH, 2, 64])).then_inc(S["hd_rhs"], 1)
            dve.wait_ge(S["hd_mm2"], 1)
            V.tensor_copy(h_dec[:, :], aux[3][:, 128:272]).then_inc(S["hd_read"], 1)
            dve.wait_ge(S["hd_read"], 1)
            for r in range(2):
                dve.wait_ge(tail_sent[r], 5 * 32)

            def exponents(q):
                w = w_int[:, q % 2, :].rearrange("p (j s) -> p j s", s=448)
                if q >= 2:
                    dve.wait_ge(S["y_mm"], 2 * (q - 1))
                for j in range(4):
                    h = 4 * q + j
                    dve.wait_ge(S["cb_bc"], h + 1)
                    ch.inc(V.tensor_scalar(w[:, j, 0:256], aux[j][:, 0:256], cum[:, 0, 4 + h:5 + h], 0.0, ALU.subtract, ALU.min))
                    ch.inc(V.tensor_scalar(w[:, j, 256:384], aux[j][:, 128:256], cum[:, 1, 4 + h:5 + h], 0.0, ALU.subtract, ALU.min))
                    V.tensor_scalar(w[0:64, j, 384:448], aux[j][0:64, 256:320], cum[0:64, 2, 4 + h:5 + h], 0.0, ALU.subtract, ALU.min).then_inc(S["t_ready"], 1)

            def weights(q):
                w = w_int[:, q % 2, :].rearrange("p (j s) -> p j s", s=448)
                dve.wait_ge(S["w_exp"], q + 1)
                gr = q // 2
                ch.inc(V.tensor_tensor(w[:, :, 0:384], w[:, :, 0:384], cbm[:, gr:gr + 1, 0:384].to_broadcast([128, 4, 384]), ALU.mult))
                V.tensor_tensor(w[0:64, :, 384:448], w[0:64, :, 384:448], cbm[0:64, gr:gr + 1, 384:448].to_broadcast([64, 4, 64]), ALU.mult).then_inc(S["w_ready"], 1)

            def outputs(q):
                for pr in range(2):
                    c = 2 * q + pr
                    dve.wait_ge(S["y_mm"], c + 1)
                    V.scalar_tensor_tensor(out=xbc_t[:, c, :], in0=xbc_t[:, c, :], scalar=h_dec[:, 128 + c:129 + c], in1=banks[c % 4][:, 0:T],
                                           op0=ALU.mult, op1=ALU.add).then_inc(S["y_read"], 1)
            exponents(0)
            for q in range(8):
                if q < 7:
                    exponents(q + 1)
                weights(q)
                outputs(q)
            dve.wait_ge(S["decx_ready"], 1)
            for blk, rows in ((0, 128), (1, 128), (2, 64)):
                v4 = xd[0:rows, blk, :].rearrange("p (e q) -> p e q", q=64)
                ins = V.tensor_tensor(v4, v4, sp2[0:rows, blk, :].unsqueeze(2).to_broadcast([rows, SH, 64]), ALU.mult)
                if blk < 2:
                    ch.inc(ins)
            ins.then_inc(S["xw_ready"], 1)
            dve.wait_ge(S["bt_read"], 3)

            def ssm_masks(i, r, first):
                b = i * 2 + r
                if not first:
                    dve.wait_ge(S["yi_mm"], b - 1)
                ch.inc(V.tensor_scalar(btm[0:64, r, :], bt[0:64, 2, :], seg_m[:, bass.ds(b, 1)], None, ALU.mult))
                V.tensor_tensor(cm[:, r, :].rearrange("p (g t) -> p g t", t=TS), xbc_t[:, 20:24, TP:T], seg_b[:, bass.ds(b, 1), :].to_broadcast([128, SG, TS]), ALU.mult)\
                    .then_inc(S["hmask_ready"], 1)

            def ssm_update(i, r):
                b = i * 2 + r
                up_banks = (aux[2], aux[3], banks[2], banks[3])
                hd3 = h_dec[:, 0:128].rearrange("p (t b) -> p t b", b=SB)
                for gr in range(SG):
                    dve.wait_ge(S["up_mm"], b * 4 + (gr + 1))
                    for j in range(4):
                        c = 4 * gr + j
                        hh = hb[:, r, c * SN:(c + 1) * SN]
                        ins = V.scalar_tensor_tensor(out=hh, in0=hh, scalar=hd3[:, c, bass.ds(b, 1)], in1=up_banks[gr][:, j * 128:(j + 1) * 128], op0=ALU.mult, op1=ALU.add)
                        if j < 3:
                            ch.inc(ins)
                    ins.then_inc(S["up_done"], 1)
            ssm_masks(0, 0, True)
            ssm_masks(0, 1, True)
            base = ch.n
            with dve.Fori(0, SB // 2 - 1) as i:
                ch.n = base + i * 26
                for r in range(2):
                    ssm_update(i, r)
                    ssm_masks(i + 1, r, False)
            ch.n = base + (SB // 2 - 1) * 26
            for r in range(2):
                ssm_update(SB // 2 - 1, r)
            dve.wait_ge(S["yi_mm"], SB)
            for q in range(2):
                for half in range(2):
                    gr = 2 * q + half
                    o = slice(64 * half, 64 * half + 64)
                    ins = V.tensor_tensor(y_int[o, q, :].rearrange("p (e q) -> p e q", q=64), banks[q][o, :].rearrange("p (e q) -> p e q", q=64),
                                          sm[o, 8, 8 * gr:8 * gr + 8].unsqueeze(2).to_broadcast([64, 8, 64]), ALU.mult)
                    if half == 0:
                        ch.inc(ins)
                ins.then_inc(S["yi_read"], 1)
            for gr in range(SG):
                dve.wait_ge(S["yi_tr"], gr + 1)
                y4 = xbc_t[:, 4 * gr:4 * gr + 4, TP:T]
                V.tensor_tensor(y4, y4, aux[gr][:, 0:4 * TS].rearrange("p (c t) -> p c t", t=TS), ALU.add).then_inc(S["yi_add"], 1)
            dve.wait_ge(S["yi_add"], SG)
            gated(segs["z"], xbc_t, gate_tmp)
            for r in range(2):
                dve.wait_ge(state_out[r], 16 * (SB + 1) + 16 * (SB // 2))

            def low_and_norm(seg, first):
                low_of = low(seg)

                def step(i, q):
                    low_of(i, q)
                    c = first + q
                    gr = c // 4
                    if c % 4 == 0:
                        dve.wait_ge(S["grs_ready"], gr + 1)
                        ch.link(V.reciprocal(g_root[:, gr, :], g_root[:, gr, :]))
                    ch.link(V.scalar_tensor_tensor(out=xbc_t[:, c, :], in0=xbc_t[:, c, :], scalar=par[:, 200 + c:201 + c], in1=g_root[:, gr, :], op0=ALU.mult, op1=ALU.mult))
                    halves(y_hi, y_lo, c, xbc_t[:, c:c + 1, :], "gnorm_done")
                return step
            gated(segs["ga"], ya, gate_tmp, now=low_and_norm(segs["ga"], 0))
            walk(dve, segs["gb"], low_and_norm(segs["gb"], 8))
            dve.wait_ge(S["gnorm_done"], 16)

            def merge(i, q):
                seg = segs["pb"]
                if q % 2 == 0:
                    return
                b, c = seg.bank(q), seg.own(i, q)
                dve.wait_ge(unit_done, seg.unit(i, q) + 1)
                g1 = merged_g[:, bass.ds(c, 1), :]
                V.tensor_tensor(g1, g1, banks[b][:, None, 0:T], ALU.mult).then_inc(bank_free[b], 1)
                dve.wait_ge(bank_free[b], seg.bank_use(i, q) + 1)
                y1 = ya[:, bass.ds(c, 1), :]
                ch.link(V.tensor_tensor(y1, y1, g1, ALU.add))
                halves(m_hi, m_lo, c, y1, "merged")
            gb = segs["gb"]
            for b in range(4):
                dve.wait_ge(bank_free[b], (gb.t0 + gb.tiles) // 4)
            dve.wait_ge(S["gate_used"], 40)
            walk(dve, segs["pb"], merge, low(segs["pb"]), None, 0, LAG)
            residual(segs["out"], 5, 1.0, KD)
            modulated(2, 6, 7, 88)
            up(segs["up2"])
            residual(segs["down2"], 8, 0.5, 2 * KD)
            dve.wait_ge(S["root_ready"], 4)
            ch.link(V.reciprocal(rs[:, :], rs[:, :]))
            for kc in range(KD):
                ins = V.scalar_tensor_tensor(out=u_t[:, kc, :], in0=x_t[:, kc, :], scalar=par[:, 96 + kc:97 + kc], in1=rs[:, :], op0=ALU.mult, op1=ALU.mult)
                if kc < KD - 1:
                    ch.inc(ins)
            ins.then_inc(S["fin_ready"], 1)


_OUTS = {
    "y_p": (1, TP, D), "y_s": (SB, ST, D),
    "p_C": (1, 1, MH, DK, DV), "p_n": (1, 1, MH, DK), "p_m": (1, 1, MH), "p_mconv": (1, 1, 3, XCH), "p_ssm": (1, 1, SH, 64, SN), "p_sconv": (1, 1, 3, SCH),
    "s_C": (1, SB, MH, DK, DV), "s_n": (1, SB, MH, DK), "s_m": (1, SB, MH), "s_mconv": (1, SB, 3, XCH), "s_ssm": (1, SB, SH, 64, SN), "s_sconv": (1, SB, 3, SCH),
}


def kernel(**inputs):
    import numpy as np
    import concourse.bacc as bacc
    from concourse.bass_utils import run_bass_kernel_spmd

    nc = bacc.Bacc("TRN2", target_bir_lowering=False, num_devices=1)
    arrays, io, out = {}, {}, {}
    for name, a in inputs.items():
        a = np.ascontiguousarray(a)
        arrays[f"in_{name}"] = a
        io[name] = nc.dram_tensor(f"in_{name}", a.shape, mybir.dt.from_np(a.dtype), kind="ExternalInput").ap()
    for name, shape in _OUTS.items():
        out[name] = nc.dram_tensor(f"out_{name}", shape, FP32, kind="ExternalOutput").ap()
    build(nc, io, out)
    r = run_bass_kernel_spmd(nc, [arrays], core_ids=[0])
    return tuple(r.results[0][f"out_{name}"] for name in _OUTS)
```
